# Optimizing a Trainium2 kernel written in Bass

```python
import math
import jax
import jax.numpy as jnp
from jax import lax
import numpy as np
import jax, jax.numpy as jnp

D_MODEL = 1024
BATCH = 1
SEQ = 256
DEPTH = 2

HEAD_DIM = 64
N_HEADS = D_MODEL // HEAD_DIM
ATTN_WIDTH = N_HEADS * HEAD_DIM
ATTN_SCALE = HEAD_DIM ** -0.5
N_MIXERS = 4
Q_BLOCK = 128
ROW_CHUNK = 128
REL_BUCKETS = 32
REL_MAX_DIST = 2048
DILATED_PAIRS = ((128, 1), (512, 4), (2048, 16))
SB_CLIP = 60.0
NSA_KV_HEADS = 4
NSA_GROUP = N_HEADS // NSA_KV_HEADS
NSA_KV_WIDTH = NSA_KV_HEADS * HEAD_DIM
NSA_CMP_LEN = 32
NSA_CMP_STRIDE = 16
NSA_CMP_HIDDEN = 256
NSA_SEL_BLOCK = 64
NSA_TOP_N = 16
NSA_WINDOW = 512
MOBA_BLOCK = 256
MOBA_TOP_K = 3
N_EXPERTS = 16
N_GROUPS = 4
EXPERTS_PER_GROUP = N_EXPERTS // N_GROUPS
MOE_TOP_K = 2
D_EXPERT = 256
MOE_BLOCK = 256
DEEPNORM_ALPHA = (2 * DEPTH) ** 0.25
DEEPNORM_BETA = (8 * DEPTH) ** -0.25
LN_EPS = 1e-5
NEG_INF = -1e30
FORCED_SCORE = 1e9


def layer_norm(x, g, b):
    xf = x.astype(jnp.float32)
    mu = xf.mean(-1, keepdims=True)
    var = jnp.square(xf - mu).mean(-1, keepdims=True)
    return ((xf - mu) * lax.rsqrt(var + LN_EPS) * g + b).astype(x.dtype)

def rel_bucket(dist):
    n = jnp.maximum(dist, 0)
    exact = REL_BUCKETS // 2
    logf = jnp.log(jnp.maximum(n, 1).astype(jnp.float32) / exact) / math.log(REL_MAX_DIST / exact)
    large = jnp.minimum(exact + (logf * (REL_BUCKETS - exact)).astype(jnp.int32), REL_BUCKETS - 1)
    return jnp.where(n < exact, n, large)

def rel_bias(table, dist):
    return jnp.moveaxis(table[rel_bucket(dist)], -1, 0).astype(jnp.float32)

def masked_softmax(logits, mask):
    logits = jnp.where(mask, logits.astype(jnp.float32), NEG_INF)
    m = logits.max(-1, keepdims=True)
    p = jnp.where(mask, jnp.exp(logits - m), 0.0)
    denom = jnp.maximum(p.sum(-1, keepdims=True), 1e-30)
    return p / denom, m + jnp.log(denom)

def merge_parts(o, lse):
    w = jax.nn.softmax(lse.astype(jnp.float32), axis=1)
    return jnp.einsum('npr,nprd->nrd', w, o.astype(jnp.float32))

def split_heads(t, h):
    b, s, _ = t.shape
    return t.reshape(b, s, h, HEAD_DIM).transpose(0, 2, 1, 3)

def merge_heads(t):
    b, h, s, d = t.shape
    return t.transpose(0, 2, 1, 3).reshape(b, s, h * d)

def dispatch_attention(q_src, pos_src, gid, k_groups, v_groups, kstart, bias_tbl, tbl_idx):
    n_src, n_slots = gid.shape
    n_groups, blk, _ = k_groups.shape
    R = q_src.shape[1]
    N = n_src * n_slots
    flat_g = gid.reshape(N)
    order = jnp.argsort(flat_g).astype(jnp.int32)
    sorted_g = flat_g[order]
    valid = sorted_g < n_groups
    sg = jnp.minimum(sorted_g, n_groups - 1)
    counts = jnp.zeros((n_groups + 1,), jnp.int32).at[flat_g].add(1)[:n_groups]
    padded = (counts + ROW_CHUNK - 1) // ROW_CHUNK * ROW_CHUNK
    pad_end = jnp.cumsum(padded)
    pad_start = pad_end - padded
    start = jnp.cumsum(counts) - counts
    n_chunks = -(-N // ROW_CHUNK) + n_groups
    P = n_chunks * ROW_CHUNK
    dest = jnp.where(valid, pad_start[sg] + jnp.arange(N) - start[sg], P)
    buf = jnp.full((P,), N, jnp.int32).at[dest].set(order, mode='drop')
    chunk_group = jnp.minimum(jnp.searchsorted(pad_end, jnp.arange(n_chunks) * ROW_CHUNK, side='right'),
                              n_groups - 1).astype(jnp.int32)
    q_pad = jnp.concatenate([q_src, jnp.zeros((1, R, HEAD_DIM), q_src.dtype)], axis=0)
    pos_pad = jnp.concatenate([pos_src, jnp.full((1,), -1, pos_src.dtype)], axis=0)
    off = jnp.arange(blk)

    def chunk(args):
        rows, g = args
        src = rows // n_slots
        qi = q_pad[src]
        dist = pos_pad[src][:, None] - (kstart[g] + off)[None, :]
        bias = bias_tbl[tbl_idx[g]][:, rel_bucket(dist)].astype(jnp.float32)
        logits = jnp.einsum('crd,kd->rck', qi, k_groups[g]).astype(jnp.float32) * ATTN_SCALE + bias
        p, lse = masked_softmax(logits, (dist >= 0)[None])
        o = jnp.einsum('rck,kd->crd', p, v_groups[g].astype(jnp.float32))
        return o, lse[..., 0].T

    o, lse = lax.map(chunk, (buf.reshape(n_chunks, ROW_CHUNK), chunk_group))
    o_all = jnp.zeros((N + 1, R, HEAD_DIM), jnp.float32).at[buf].set(o.reshape(P, R, HEAD_DIM))[:N]
    lse_all = jnp.full((N + 1, R), NEG_INF, jnp.float32).at[buf].set(lse.reshape(P, R))[:N]
    return o_all.reshape(n_src, n_slots, R, HEAD_DIM), lse_all.reshape(n_src, n_slots, R)

def dilated_group(q, k, v, table, window, dilation):
    Bsz, H, S_, _ = q.shape
    L = S_ // dilation
    nb = -(-L // Q_BLOCK)
    Lp = nb * Q_BLOCK
    span = window // dilation
    n_prev = -(-span // Q_BLOCK)

    def streams(t):
        t = t.reshape(Bsz, H, L, dilation, HEAD_DIM).transpose(0, 1, 3, 2, 4)
        t = jnp.pad(t, ((0, 0), (0, 0), (0, 0), (0, Lp - L), (0, 0)))
        return t.reshape(Bsz, H, dilation, nb, Q_BLOCK, HEAD_DIM)

    def band(t):
        tp = jnp.pad(t, ((0, 0), (0, 0), (0, 0), (n_prev, 0), (0, 0), (0, 0)))
        return jnp.concatenate([tp[:, :, :, o:o + nb] for o in range(n_prev + 1)], axis=4)

    qs = streams(q)
    kb, vb = band(streams(k)), band(streams(v))
    a = jnp.arange(Q_BLOCK)
    c = jnp.arange((n_prev + 1) * Q_BLOCK)
    steps = n_prev * Q_BLOCK + a[:, None] - c[None, :]
    key_idx = jnp.arange(nb)[:, None] * Q_BLOCK - n_prev * Q_BLOCK + c[None, :]
    mask = ((steps >= 0) & (steps <= span))[None] & (key_idx >= 0)[:, None, :]
    bias = rel_bias(table, steps * dilation)
    logits = jnp.einsum('bhrnqd,bhrnkd->bhrnqk', qs, kb).astype(jnp.float32) * ATTN_SCALE + bias[:, None, None]
    p, lse = masked_softmax(logits, mask)
    o = jnp.einsum('bhrnqk,bhrnkd->bhrnqd', p.astype(v.dtype), vb)
    o = o.reshape(Bsz, H, dilation, Lp, HEAD_DIM)[:, :, :, :L].transpose(0, 1, 3, 2, 4).reshape(Bsz, H, S_, HEAD_DIM)
    lse = lse[..., 0].reshape(Bsz, H, dilation, Lp)[..., :L].transpose(0, 1, 3, 2).reshape(Bsz, H, S_)
    return o, lse

def mixer_dilated(x, w_in, w_out, table):
    proj = x @ w_in
    gw = 3 * ATTN_WIDTH
    outs, lses = [], []
    for g, (window, dilation) in enumerate(DILATED_PAIRS):
        q, k, v = [split_heads(t, N_HEADS) for t in jnp.split(proj[..., g * gw:(g + 1) * gw], 3, axis=-1)]
        o, lse = dilated_group(q, k, v, table, window, dilation)
        outs.append(o)
        lses.append(lse)
    wts = jax.nn.softmax(jnp.stack(lses), axis=0)
    o = jnp.einsum('gbhs,gbhsd->bhsd', wts, jnp.stack(outs).astype(jnp.float32))
    return merge_heads(o.astype(x.dtype)) @ w_out

def mixer_stick_breaking(x, w_in, w_out):
    q, k, v = [split_heads(t, N_HEADS) for t in jnp.split(x @ w_in, 3, axis=-1)]
    Bsz, H, S_, _ = q.shape
    nb = S_ // Q_BLOCK
    nbp = nb + nb % 2
    pad = ((0, 0), (0, 0), (0, (nbp - nb) * Q_BLOCK), (0, 0))

    def blocks(t):
        return jnp.pad(t, pad).reshape(Bsz, H, nbp, Q_BLOCK, HEAD_DIM)

    qb, kb, vb = blocks(q * ATTN_SCALE), blocks(k), blocks(v)
    a = jnp.arange(Q_BLOCK)
    strict = a[None, :] < a[:, None]
    suffix = (a[:, None] >= a[None, :]).astype(jnp.float32)

    z = jnp.clip(jnp.einsum('bhnqd,bhnkd->bhnqk', qb, kb).astype(jnp.float32), -SB_CLIP, SB_CLIP)
    sp = jnp.where(strict, jnp.log1p(jnp.exp(z)), 0.0)
    r_in = jnp.einsum('bhnqj,js->bhnqs', sp, suffix)
    att = jnp.where(strict, jnp.exp(z - r_in), 0.0)
    acc_d = jnp.einsum('bhnqs,bhnsd->bhnqd', att, vb.astype(jnp.float32))
    r_d = r_in[..., 0]

    def pair(p):
        qb2 = nbp - 1 - p
        init_r2 = lax.dynamic_index_in_dim(r_d, qb2, axis=2, keepdims=False)
        init_a2 = lax.dynamic_index_in_dim(acc_d, qb2, axis=2, keepdims=False)

        def step(carry, kstep):
            r_sum, acc, acc_first = carry
            start2 = kstep == p
            acc_first = jnp.where(start2, acc, acc_first)
            r_sum = jnp.where(start2, init_r2, r_sum)
            acc = jnp.where(start2, init_a2, acc)
            first = kstep < p
            qi = jnp.where(first, p, qb2)
            kj = jnp.where(first, p - 1 - kstep, nbp - 2 - kstep)
            qblk = lax.dynamic_index_in_dim(qb, qi, axis=2, keepdims=False)
            kblk = lax.dynamic_index_in_dim(kb, kj, axis=2, keepdims=False)
            vblk = lax.dynamic_index_in_dim(vb, kj, axis=2, keepdims=False)
            zz = jnp.clip(jnp.einsum('bhqd,bhkd->bhqk', qblk, kblk).astype(jnp.float32), -SB_CLIP, SB_CLIP)
            rr = jnp.einsum('bhqj,js->bhqs', jnp.log1p(jnp.exp(zz)), suffix)
            pv = jnp.einsum('bhqs,bhsd->bhqd', jnp.exp(zz - rr), vblk.astype(jnp.float32))
            acc = acc + jnp.exp(-r_sum)[..., None] * pv
            r_sum = r_sum + rr[..., 0]
            return (r_sum, acc, acc_first), None

        init = (lax.dynamic_index_in_dim(r_d, p, axis=2, keepdims=False),
                lax.dynamic_index_in_dim(acc_d, p, axis=2, keepdims=False),
                jnp.zeros((Bsz, H, Q_BLOCK, HEAD_DIM), jnp.float32))
        (_, acc_b, acc_a), _ = lax.scan(step, init, jnp.arange(nbp - 1))
        return acc_a, acc_b

    out_a, out_b = lax.map(pair, jnp.arange(nbp // 2))
    o = jnp.concatenate([out_a, out_b[::-1]], axis=0)
    o = o.transpose(1, 2, 0, 3, 4).reshape(Bsz, H, nbp * Q_BLOCK, HEAD_DIM)[:, :, :S_]
    return merge_heads(o.astype(x.dtype)) @ w_out

def compress_blocks(t, pos, w1, w2):
    Bsz, G, S_, _ = t.shape
    halves = t.reshape(Bsz, G, S_ // NSA_CMP_STRIDE, NSA_CMP_STRIDE, HEAD_DIM)
    blocks = jnp.concatenate([halves[:, :, :-1], halves[:, :, 1:]], axis=3) + pos
    n_cmp = blocks.shape[2]
    flat = blocks.reshape(Bsz, G, n_cmp, NSA_CMP_LEN * HEAD_DIM)
    return jax.nn.gelu(flat @ w1) @ w2

def mixer_nsa(x, w_in, w_out, table, pos_k, w1_k, w2_k, pos_v, w1_v, w2_v):
    Bsz, S_, _ = x.shape
    G, R = NSA_KV_HEADS, NSA_GROUP
    proj = x @ w_in
    q = proj[..., :ATTN_WIDTH].reshape(Bsz, S_, G, R, HEAD_DIM).transpose(0, 2, 3, 1, 4)
    kv = jnp.split(proj[..., ATTN_WIDTH:ATTN_WIDTH + 6 * NSA_KV_WIDTH], 6, axis=-1)
    k_cmp, v_cmp, k_sel, v_sel, k_win, v_win = [split_heads(t, G) for t in kv]
    gates = jax.nn.sigmoid(proj[..., ATTN_WIDTH + 6 * NSA_KV_WIDTH:].astype(jnp.float32))
    gates = gates.reshape(Bsz, S_, 3, G, R).transpose(2, 0, 3, 4, 1)

    kc = compress_blocks(k_cmp, pos_k, w1_k, w2_k)
    vc = compress_blocks(v_cmp, pos_v, w1_v, w2_v)
    n_cmp = kc.shape[2]
    cmp_end = jnp.arange(n_cmp) * NSA_CMP_STRIDE + NSA_CMP_LEN - 1
    n_sel_blocks = S_ // NSA_SEL_BLOCK
    n_top = min(NSA_TOP_N, n_sel_blocks)
    offs = np.arange(1 - NSA_CMP_LEN // NSA_CMP_STRIDE, NSA_SEL_BLOCK // NSA_CMP_STRIDE)
    ov = np.arange(n_sel_blocks)[:, None] * (NSA_SEL_BLOCK // NSA_CMP_STRIDE) + offs[None]
    ov_valid = jnp.asarray((ov >= 0) & (ov < n_cmp))
    ov_idx = jnp.asarray(np.clip(ov, 0, n_cmp - 1))
    kwin = jnp.pad(k_win, ((0, 0), (0, 0), (NSA_WINDOW, 0), (0, 0)))
    vwin = jnp.pad(v_win, ((0, 0), (0, 0), (NSA_WINDOW, 0), (0, 0)))
    table_gr = table.T.reshape(G, R, REL_BUCKETS)
    nb = S_ // Q_BLOCK
    win_len = NSA_WINDOW + Q_BLOCK
    a = jnp.arange(Q_BLOCK)
    win_steps = NSA_WINDOW + a[:, None] - jnp.arange(win_len)[None, :]
    win_bias = rel_bias(table, win_steps).reshape(G, R, Q_BLOCK, win_len)
    sel_j = jnp.arange(n_sel_blocks)
    qb = q.reshape(Bsz, G, R, nb, Q_BLOCK, HEAD_DIM).transpose(3, 0, 1, 2, 4, 5)

    def block(args):
        qi, i = args
        qpos = i * Q_BLOCK + a
        cdist = qpos[:, None] - cmp_end[None, :]
        lc = jnp.einsum('bgrqd,bgcd->bgrqc', qi, kc).astype(jnp.float32) * ATTN_SCALE
        lc = lc + rel_bias(table, cdist).reshape(G, R, Q_BLOCK, n_cmp)
        pc, _ = masked_softmax(lc, cdist >= 0)
        o_cmp = jnp.einsum('bgrqc,bgcd->bgrqd', pc, vc.astype(jnp.float32))
        imp = (pc.sum(2)[..., ov_idx] * ov_valid).sum(-1)
        cur = qpos // NSA_SEL_BLOCK
        forced = (sel_j[None] == 0) | (sel_j[None] == cur[:, None]) | (sel_j[None] == cur[:, None] - 1)
        causal = sel_j[None] * NSA_SEL_BLOCK <= qpos[:, None]
        score = jnp.where(forced, FORCED_SCORE, jnp.where(causal, imp, NEG_INF))
        sel = lax.top_k(score, n_top)[1]
        kw = lax.dynamic_slice_in_dim(kwin, i * Q_BLOCK, win_len, axis=2)
        vw = lax.dynamic_slice_in_dim(vwin, i * Q_BLOCK, win_len, axis=2)
        wmask = (win_steps < NSA_WINDOW) & (win_steps >= 0) & (qpos[:, None] - win_steps >= 0)
        lw = jnp.einsum('bgrqd,bgkd->bgrqk', qi, kw).astype(jnp.float32) * ATTN_SCALE + win_bias
        pw, _ = masked_softmax(lw, wmask)
        o_win = jnp.einsum('bgrqk,bgkd->bgrqd', pw, vw.astype(jnp.float32))
        return o_cmp, o_win, sel

    o_cmp, o_win, sel = lax.map(block, (qb, jnp.arange(nb)))

    def unblock(t):
        return t.transpose(1, 2, 3, 0, 4, 5).reshape(Bsz, G, R, S_, HEAD_DIM)

    o_cmp, o_win = unblock(o_cmp), unblock(o_win)
    sel = sel.transpose(1, 2, 0, 3, 4).reshape(Bsz, G, S_, n_top)
    qpos_all = jnp.arange(S_)
    valid = sel * NSA_SEL_BLOCK <= qpos_all[:, None]
    n_groups = Bsz * G * n_sel_blocks
    bg = jnp.arange(Bsz * G).reshape(Bsz, G, 1, 1)
    gid = jnp.where(valid, bg * n_sel_blocks + sel, n_groups).reshape(Bsz * G * S_, n_top)
    q_src = q.transpose(0, 1, 3, 2, 4).reshape(Bsz * G * S_, R, HEAD_DIM)
    o_s, lse_s = dispatch_attention(
        q_src, jnp.tile(qpos_all, Bsz * G), gid,
        k_sel.reshape(n_groups, NSA_SEL_BLOCK, HEAD_DIM), v_sel.reshape(n_groups, NSA_SEL_BLOCK, HEAD_DIM),
        jnp.tile(jnp.arange(n_sel_blocks) * NSA_SEL_BLOCK, Bsz * G), table_gr,
        (jnp.arange(n_groups) // n_sel_blocks) % G)
    o_sel = merge_parts(o_s, lse_s).reshape(Bsz, G, S_, R, HEAD_DIM).transpose(0, 1, 3, 2, 4)
    out = gates[0][..., None] * o_cmp + gates[1][..., None] * o_sel + gates[2][..., None] * o_win
    return out.transpose(0, 3, 1, 2, 4).reshape(Bsz, S_, ATTN_WIDTH).astype(x.dtype) @ w_out

def mixer_moba(x, w_in, w_out, table):
    Bsz, S_, _ = x.shape
    H = N_HEADS
    q, k, v = [split_heads(t, H) for t in jnp.split(x @ w_in, 3, axis=-1)]
    nblk = -(-S_ // MOBA_BLOCK)
    Sp = nblk * MOBA_BLOCK
    pad = ((0, 0), (0, 0), (0, Sp - S_), (0, 0))
    qblk = jnp.pad(q, pad).reshape(Bsz, H, nblk, MOBA_BLOCK, HEAD_DIM)
    kblk = jnp.pad(k, pad).reshape(Bsz, H, nblk, MOBA_BLOCK, HEAD_DIM)
    vblk = jnp.pad(v, pad).reshape(Bsz, H, nblk, MOBA_BLOCK, HEAD_DIM)
    c = jnp.arange(MOBA_BLOCK)
    own_dist = c[:, None] - c[None, :]
    lo = jnp.einsum('bhnqd,bhnkd->bhnqk', qblk, kblk).astype(jnp.float32) * ATTN_SCALE + rel_bias(table, own_dist)[:, None]
    p_own, lse_own = masked_softmax(lo, own_dist >= 0)
    o_own = jnp.einsum('bhnqk,bhnkd->bhnqd', p_own, vblk.astype(jnp.float32)).reshape(Bsz, H, Sp, HEAD_DIM)[:, :, :S_]
    lse_own = lse_own[..., 0].reshape(Bsz, H, Sp)[:, :, :S_]
    kmean = kblk.mean(axis=3)
    n_top = max(1, min(MOBA_TOP_K, nblk - 1))
    cur = jnp.arange(S_) // MOBA_BLOCK
    gate = jnp.einsum('bhsd,bhnd->bhsn', q, kmean).astype(jnp.float32)
    gate = jnp.where(jnp.arange(nblk)[None, :] < cur[:, None], gate, NEG_INF)
    sel = lax.top_k(gate, n_top)[1]
    valid = sel < cur[:, None]
    n_groups = Bsz * H * nblk
    bh = jnp.arange(Bsz * H).reshape(Bsz, H, 1, 1)
    gid = jnp.where(valid, bh * nblk + sel, n_groups).reshape(Bsz * H * S_, n_top)
    o_sel, lse_sel = dispatch_attention(
        q.reshape(Bsz * H * S_, 1, HEAD_DIM), jnp.tile(jnp.arange(S_), Bsz * H), gid,
        kblk.reshape(n_groups, MOBA_BLOCK, HEAD_DIM), vblk.reshape(n_groups, MOBA_BLOCK, HEAD_DIM),
        jnp.tile(jnp.arange(nblk) * MOBA_BLOCK, Bsz * H), table.T[:, None, :],
        (jnp.arange(n_groups) // nblk) % H)
    o_all = jnp.concatenate([o_own.reshape(Bsz * H * S_, 1, 1, HEAD_DIM), o_sel], axis=1)
    lse_all = jnp.concatenate([lse_own.reshape(Bsz * H * S_, 1, 1), lse_sel], axis=1)
    o = merge_parts(o_all, lse_all).reshape(Bsz, H, S_, HEAD_DIM)
    return merge_heads(o.astype(x.dtype)) @ w_out

def moe_ffn(x, router_w, router_b, w_gate, w_up, w_down):
    Bsz, S_, D_ = x.shape
    T = Bsz * S_
    xt = x.reshape(T, D_)
    scores = jax.nn.sigmoid((xt @ router_w).astype(jnp.float32))
    biased = (scores + router_b.astype(jnp.float32)).reshape(T, N_GROUPS, EXPERTS_PER_GROUP)
    group_score = lax.top_k(biased, MOE_TOP_K)[0].sum(-1)
    best_group = jnp.argmax(group_score, axis=-1).astype(jnp.int32)
    in_group = jnp.take_along_axis(biased, best_group[:, None, None], axis=1)[:, 0]
    local = lax.top_k(in_group, MOE_TOP_K)[1]
    expert_idx = best_group[:, None] * EXPERTS_PER_GROUP + local
    gate = jnp.take_along_axis(scores, expert_idx, axis=1)
    gate = gate / gate.sum(-1, keepdims=True)
    n_assign = T * MOE_TOP_K
    flat_e = expert_idx.reshape(n_assign)
    order = jnp.argsort(flat_e)
    sorted_e = flat_e[order]
    sorted_tok = (order // MOE_TOP_K).astype(jnp.int32)
    sorted_w = gate.reshape(n_assign)[order]
    counts = jnp.zeros((N_EXPERTS,), jnp.int32).at[flat_e].add(1)
    padded = (counts + MOE_BLOCK - 1) // MOE_BLOCK * MOE_BLOCK
    pad_end = jnp.cumsum(padded)
    pad_start = pad_end - padded
    start = jnp.cumsum(counts) - counts
    dest = pad_start[sorted_e] + jnp.arange(n_assign) - start[sorted_e]
    n_blocks = -(-n_assign // MOE_BLOCK) + N_EXPERTS
    P = n_blocks * MOE_BLOCK
    buf_tok = jnp.full((P,), T, jnp.int32).at[dest].set(sorted_tok)
    buf_w = jnp.zeros((P,), x.dtype).at[dest].set(sorted_w.astype(x.dtype))
    block_expert = jnp.minimum(jnp.searchsorted(pad_end, jnp.arange(n_blocks) * MOE_BLOCK, side='right'), N_EXPERTS - 1)
    x_pad = jnp.concatenate([xt, jnp.zeros((1, D_), xt.dtype)], axis=0)
    xb = x_pad[buf_tok].reshape(n_blocks, MOE_BLOCK, D_)

    def expert_block(args):
        xi, e = args
        return (jax.nn.silu(xi @ w_gate[e]) * (xi @ w_up[e])) @ w_down[e]

    yb = lax.map(expert_block, (xb, block_expert)).reshape(P, D_) * buf_w[:, None]
    y = jnp.zeros((T + 1, D_), yb.dtype).at[buf_tok].add(yb)[:T]
    return y.reshape(Bsz, S_, D_)

def first_inputs(seed: int = 0) -> dict:
    key = jax.random.key(seed)
    ks = jax.random.split(key, 26)
    n_occ = [len(range(m, DEPTH, N_MIXERS)) for m in range(N_MIXERS)]
    beta = DEEPNORM_BETA

    def normal(k, shape, scale):
        return jax.random.normal(k, shape, jnp.float32) * scale

    def col_scale(pieces):
        return jnp.asarray(np.concatenate([np.full((w,), s, np.float32) for w, s in pieces]))

    qkv_pieces = [(ATTN_WIDTH, 1.0), (ATTN_WIDTH, 1.0), (ATTN_WIDTH, beta)]
    dil_scale = col_scale(qkv_pieces * len(DILATED_PAIRS))
    qkv_scale = col_scale(qkv_pieces)
    nsa_scale = col_scale([(ATTN_WIDTH, 1.0)] + [(NSA_KV_WIDTH, 1.0), (NSA_KV_WIDTH, beta)] * 3 + [(3 * N_HEADS, 1.0)])
    din = D_MODEL ** -0.5
    out_scale = ATTN_WIDTH ** -0.5 * beta
    cmp_in = NSA_CMP_LEN * HEAD_DIM
    return {
        'x': normal(ks[0], (BATCH, SEQ, D_MODEL), 1.0),
        'rel_table': normal(ks[1], (REL_BUCKETS, N_HEADS), 0.1),
        'router_w': normal(ks[2], (D_MODEL, N_EXPERTS), din),
        'router_b': normal(ks[3], (N_EXPERTS,), 0.01),
        'ln1_g': 1.0 + normal(ks[4], (DEPTH, D_MODEL), 0.01),
        'ln1_b': normal(ks[5], (DEPTH, D_MODEL), 0.01),
        'ln2_g': 1.0 + normal(ks[6], (DEPTH, D_MODEL), 0.01),
        'ln2_b': normal(ks[7], (DEPTH, D_MODEL), 0.01),
        'exp_w_gate': normal(ks[8], (DEPTH, N_EXPERTS, D_MODEL, D_EXPERT), din),
        'exp_w_up': normal(ks[9], (DEPTH, N_EXPERTS, D_MODEL, D_EXPERT), din),
        'exp_w_down': normal(ks[10], (DEPTH, N_EXPERTS, D_EXPERT, D_MODEL), D_EXPERT ** -0.5 * beta),
        'dil_w_in': normal(ks[11], (n_occ[0], D_MODEL, 3 * len(DILATED_PAIRS) * ATTN_WIDTH), din) * dil_scale,
        'dil_w_out': normal(ks[12], (n_occ[0], ATTN_WIDTH, D_MODEL), out_scale),
        'sb_w_in': normal(ks[13], (n_occ[1], D_MODEL, 3 * ATTN_WIDTH), din) * qkv_scale,
        'sb_w_out': normal(ks[14], (n_occ[1], ATTN_WIDTH, D_MODEL), out_scale),
        'nsa_w_in': normal(ks[15], (n_occ[2], D_MODEL, ATTN_WIDTH + 6 * NSA_KV_WIDTH + 3 * N_HEADS), din) * nsa_scale,
        'nsa_w_out': normal(ks[16], (n_occ[2], ATTN_WIDTH, D_MODEL), out_scale),
        'nsa_cmp_pos_k': normal(ks[17], (n_occ[2], NSA_CMP_LEN, HEAD_DIM), 0.1),
        'nsa_cmp_w1_k': normal(ks[18], (n_occ[2], cmp_in, NSA_CMP_HIDDEN), cmp_in ** -0.5),
        'nsa_cmp_w2_k': normal(ks[19], (n_occ[2], NSA_CMP_HIDDEN, HEAD_DIM), NSA_CMP_HIDDEN ** -0.5),
        'nsa_cmp_pos_v': normal(ks[20], (n_occ[2], NSA_CMP_LEN, HEAD_DIM), 0.1),
        'nsa_cmp_w1_v': normal(ks[21], (n_occ[2], cmp_in, NSA_CMP_HIDDEN), cmp_in ** -0.5),
        'nsa_cmp_w2_v': normal(ks[22], (n_occ[2], NSA_CMP_HIDDEN, HEAD_DIM), NSA_CMP_HIDDEN ** -0.5),
        'moba_w_in': normal(ks[23], (n_occ[3], D_MODEL, 3 * ATTN_WIDTH), din) * qkv_scale,
        'moba_w_out': normal(ks[24], (n_occ[3], ATTN_WIDTH, D_MODEL), out_scale),
    }

def first_block(x, rel_table, router_w, router_b, ln1_g, ln1_b, ln2_g, ln2_b,
              exp_w_gate, exp_w_up, exp_w_down, dil_w_in, dil_w_out, sb_w_in, sb_w_out,
              nsa_w_in, nsa_w_out, nsa_cmp_pos_k, nsa_cmp_w1_k, nsa_cmp_w2_k,
              nsa_cmp_pos_v, nsa_cmp_w1_v, nsa_cmp_w2_v, moba_w_in, moba_w_out):
    for layer in range(DEPTH):
        kind, occ = layer % N_MIXERS, layer // N_MIXERS
        if kind == 0:
            mixed = mixer_dilated(x, dil_w_in[occ], dil_w_out[occ], rel_table)
        elif kind == 1:
            mixed = mixer_stick_breaking(x, sb_w_in[occ], sb_w_out[occ])
        elif kind == 2:
            mixed = mixer_nsa(x, nsa_w_in[occ], nsa_w_out[occ], rel_table,
                              nsa_cmp_pos_k[occ], nsa_cmp_w1_k[occ], nsa_cmp_w2_k[occ],
                              nsa_cmp_pos_v[occ], nsa_cmp_w1_v[occ], nsa_cmp_w2_v[occ])
        else:
            mixed = mixer_moba(x, moba_w_in[occ], moba_w_out[occ], rel_table)
        x = layer_norm(DEEPNORM_ALPHA * x + mixed, ln1_g[layer], ln1_b[layer])
        ffn = moe_ffn(x, router_w, router_b, exp_w_gate[layer], exp_w_up[layer], exp_w_down[layer])
        x = layer_norm(DEEPNORM_ALPHA * x + ffn, ln2_g[layer], ln2_b[layer])
    return x


GROUP_HEADS = 4
GROUP_WIDTH = D_MODEL // N_GROUPS
HEAD_DIM_2 = GROUP_WIDTH // GROUP_HEADS
MIX_WIDTH = N_GROUPS * GROUP_WIDTH
CONV_WIDTH = 3
RWKV_DECAY_RANK = 64
RWKV_ICLR_RANK = 64
RWKV_GATE_RANK = 128
RWKV_GN_EPS = 64e-5
RET_CHUNK = 128
MLA_Q_RANK = 384
MLA_KV_RANK = 128
MLA_NOPE = 64
MLA_ROPE = 32
MLA_V = 64
ATTN_BLOCK = 128
D_FF = 2816
ROPE_BASE = 10000.0
NORM_EPS = 1e-6
MAX_POS_OFFSET = 4096
IN_SPLITS = (
    GROUP_WIDTH, GROUP_WIDTH, GROUP_WIDTH,
    GROUP_WIDTH, GROUP_WIDTH, GROUP_WIDTH,
    RWKV_DECAY_RANK, RWKV_DECAY_RANK,
    RWKV_ICLR_RANK, RWKV_ICLR_RANK,
    RWKV_GATE_RANK,
    GROUP_WIDTH, GROUP_WIDTH, GROUP_WIDTH, GROUP_WIDTH,
    MLA_Q_RANK, MLA_KV_RANK + MLA_ROPE,
)
IN_WIDTH = sum(IN_SPLITS)


def rmsnorm(x, g):
    xf = x.astype(jnp.float32)
    y = xf * lax.rsqrt(jnp.mean(xf * xf, axis=-1, keepdims=True) + NORM_EPS)
    return (y * g.astype(jnp.float32)).astype(x.dtype)

def swiglu(x, w_gate, w_up, w_down):
    return (jax.nn.silu(x @ w_gate) * (x @ w_up)) @ w_down

def rope(x, pos):
    half = x.shape[-1] // 2
    inv = ROPE_BASE ** (-jnp.arange(half, dtype=jnp.float32) / half)
    ang = pos.astype(jnp.float32)[:, :, None, None] * inv
    cos, sin = jnp.cos(ang), jnp.sin(ang)
    xf = x.astype(jnp.float32)
    x1, x2 = xf[..., :half], xf[..., half:]
    return jnp.concatenate([x1 * cos - x2 * sin, x1 * sin + x2 * cos], axis=-1).astype(x.dtype)

def heads(t):
    b, s, _ = t.shape
    return t.reshape(b, s, GROUP_HEADS, HEAD_DIM_2).astype(jnp.float32)

def short_conv_mixer(x_in, b_gate, c_gate, conv_w):
    u = c_gate * x_in
    y = lax.conv_general_dilated(
        u, conv_w[:, None, :].astype(u.dtype), window_strides=(1,), padding=[(1, 1)],
        dimension_numbers=('NWC', 'WIO', 'NWC'), feature_group_count=GROUP_WIDTH)
    return b_gate * y

def rwkv7_scan(r, k, v, kk, a, decay, reverse):
    xs = tuple(jnp.moveaxis(t, 1, 0) for t in (r, k, v, kk, a, decay))
    b, _, h, n = r.shape

    def step(S, inp):
        r_t, k_t, v_t, kk_t, a_t, w_t = inp
        sa = jnp.einsum('bhvk,bhk->bhv', S, -kk_t)
        S = (S * w_t[:, :, None, :] + sa[..., None] * (kk_t * a_t)[:, :, None, :]
             + v_t[..., None] * k_t[:, :, None, :])
        return S, jnp.einsum('bhvk,bhk->bhv', S, r_t)

    S0 = jnp.zeros((b, h, n, n), jnp.float32)
    _, y = lax.scan(step, S0, xs, reverse=reverse)
    return jnp.moveaxis(y, 0, 1)

def rwkv7_mixer(r, k, v, wd_f, wd_b, ad_f, ad_b, gd, w0_f, w0_b, w2_f, w2_b,
                a0_f, a0_b, a2_f, a2_b, g2, k_k, k_a, r_k, lnx_g, lnx_b):
    b, s, _ = r.shape
    g = jax.nn.sigmoid(gd) @ g2
    kk = heads(k * k_k)
    kk = kk / jnp.maximum(jnp.sqrt(jnp.sum(kk * kk, axis=-1, keepdims=True)), 1e-12)
    rh, vh = heads(r), heads(v)
    y = jnp.zeros_like(rh)
    k_sum = jnp.zeros_like(rh)
    for wd, ad, w0, w2, a0, a2, rev in ((wd_f, ad_f, w0_f, w2_f, a0_f, a2_f, False),
                                        (wd_b, ad_b, w0_b, w2_b, a0_b, a2_b, True)):
        w_log = -jax.nn.softplus(-(w0 + jnp.tanh(wd) @ w2)) - 0.5
        decay = jnp.exp(-jnp.exp(w_log.astype(jnp.float32)))
        a = jax.nn.sigmoid(a0 + ad @ a2)
        k_dir = heads(k * (1.0 + (a - 1.0) * k_a))
        y = y + rwkv7_scan(rh, k_dir, vh, kk, heads(a), heads(decay), rev)
        k_sum = k_sum + k_dir
    mu = jnp.mean(y, axis=-1, keepdims=True)
    var = jnp.mean(jnp.square(y - mu), axis=-1, keepdims=True)
    yn = ((y - mu) * lax.rsqrt(var + RWKV_GN_EPS)).reshape(b, s, GROUP_WIDTH)
    yn = yn * lnx_g.astype(jnp.float32) + lnx_b.astype(jnp.float32)
    bonus = (jnp.sum(rh * k_sum * r_k.astype(jnp.float32), axis=-1, keepdims=True) * vh).reshape(b, s, GROUP_WIDTH)
    return (yn + bonus).astype(r.dtype) * g

def retention_mixer(q, k, v, g, pos, gn_g):
    b, s, _ = q.shape
    nc, C = s // RET_CHUNK, RET_CHUNK
    qh = rope(q.reshape(b, s, GROUP_HEADS, HEAD_DIM_2), pos)
    kh = rope(k.reshape(b, s, GROUP_HEADS, HEAD_DIM_2), pos) * (HEAD_DIM_2 ** -0.5)
    vh = v.reshape(b, s, GROUP_HEADS, HEAD_DIM_2)
    chunk = lambda t: t.reshape(b, nc, C, GROUP_HEADS, HEAD_DIM_2).transpose(0, 3, 1, 2, 4).astype(jnp.float32)
    qc, kc, vc = chunk(qh), chunk(kh), chunk(vh)
    log_gamma = jnp.log(1.0 - 2.0 ** (-5.0 - jnp.arange(GROUP_HEADS, dtype=jnp.float32)))
    idx = jnp.arange(C, dtype=jnp.float32)
    intra_decay = jnp.exp(log_gamma[:, None, None] * jnp.abs(idx[:, None] - idx[None, :]))
    dec_start = jnp.exp(log_gamma[:, None] * idx)[None, :, None, :, None]
    dec_end = jnp.exp(log_gamma[:, None] * (C - idx))[None, :, None, :, None]
    chunk_decay = jnp.exp(log_gamma * C)[None, :, None, None]
    scores = jnp.einsum('bhnid,bhnjd->bhnij', qc, kc) * intra_decay[None, :, None]
    o = jnp.einsum('bhnij,bhnjd->bhnid', scores, vc)
    kv_f = jnp.einsum('bhnjd,bhnje->nbhde', kc * dec_end, vc)
    kv_b = jnp.einsum('bhnjd,bhnje->nbhde', kc * dec_start, vc)

    def step(R, summ):
        return R * chunk_decay + summ, R

    R0 = jnp.zeros((b, GROUP_HEADS, HEAD_DIM_2, HEAD_DIM_2), jnp.float32)
    _, R_f = lax.scan(step, R0, kv_f)
    _, R_b = lax.scan(step, R0, kv_b, reverse=True)
    o = (o + dec_start * jnp.einsum('bhnid,nbhde->bhnie', qc, R_f)
         + dec_end * jnp.einsum('bhnid,nbhde->bhnie', qc, R_b))
    o = o.transpose(0, 2, 3, 1, 4).reshape(b, s, GROUP_HEADS, HEAD_DIM_2)
    o = o * lax.rsqrt(jnp.mean(o * o, axis=-1, keepdims=True) + NORM_EPS)
    o = o.reshape(b, s, GROUP_WIDTH) * gn_g.astype(jnp.float32)
    return jax.nn.silu(g) * o.astype(q.dtype)

def mla_mixer(q_a, kv_a, pos, q_a_norm, q_b, kv_a_norm, kv_b):
    b, s, _ = q_a.shape
    q = (rmsnorm(q_a, q_a_norm) @ q_b).reshape(b, s, GROUP_HEADS, MLA_NOPE + MLA_ROPE)
    q_nope, q_rope = q[..., :MLA_NOPE], rope(q[..., MLA_NOPE:], pos)
    c_kv, k_rope = kv_a[..., :MLA_KV_RANK], kv_a[..., MLA_KV_RANK:]
    kv = (rmsnorm(c_kv, kv_a_norm) @ kv_b).reshape(b, s, GROUP_HEADS, MLA_NOPE + MLA_V)
    k_nope, v = kv[..., :MLA_NOPE], kv[..., MLA_NOPE:]
    k_rope = rope(k_rope[:, :, None, :], pos)[:, :, 0]
    scale = (MLA_NOPE + MLA_ROPE) ** -0.5
    nb = s // ATTN_BLOCK
    blocks = lambda t: t.reshape(b, nb, ATTN_BLOCK, GROUP_HEADS, t.shape[-1]).transpose(1, 0, 2, 3, 4)

    def attend(blk):
        qn, qr = blk
        sc = jnp.einsum('bqhd,bkhd->bhqk', qn, k_nope) + jnp.einsum('bqhr,bkr->bhqk', qr, k_rope)
        p = jax.nn.softmax(sc.astype(jnp.float32) * scale, axis=-1)
        return jnp.einsum('bhqk,bkhd->bqhd', p.astype(v.dtype), v)

    o = lax.map(attend, (blocks(q_nope), blocks(q_rope)))
    return o.transpose(1, 0, 2, 3, 4).reshape(b, s, GROUP_WIDTH)

def second_inputs(seed: int = 0) -> dict:
    key = jax.random.key(seed)
    ks = iter(jax.random.split(key, 48))
    L, W, H, N = DEPTH, GROUP_WIDTH, GROUP_HEADS, HEAD_DIM_2
    f32 = jnp.float32

    def nrm(shape):
        return jax.random.normal(next(ks), shape, f32)

    def dense(shape, fan_in, scale=1.0):
        return nrm(shape) * (scale * fan_in ** -0.5)

    def gain(shape):
        return 1.0 + 0.02 * nrm(shape)

    decay_base = jnp.tile(jnp.linspace(-6.0, -1.0, N, dtype=f32), H)
    x = nrm((BATCH, SEQ, D_MODEL))
    offsets = jax.random.randint(next(ks), (BATCH, 1), 0, MAX_POS_OFFSET, dtype=jnp.int32)
    positions = offsets + jnp.arange(SEQ, dtype=jnp.int32)[None, :]
    return {
        'x': x,
        'positions': positions,
        'ffn1_norm': gain((L, D_MODEL)),
        'ffn1_w_gate': dense((L, D_MODEL, D_FF), D_MODEL),
        'ffn1_w_up': dense((L, D_MODEL, D_FF), D_MODEL),
        'ffn1_w_down': dense((L, D_FF, D_MODEL), D_FF),
        'mix_norm': gain((L, D_MODEL)),
        'w_in': dense((L, D_MODEL, IN_WIDTH), D_MODEL),
        'w_out': dense((L, MIX_WIDTH, D_MODEL), MIX_WIDTH),
        'conv_w': dense((L, CONV_WIDTH, W), CONV_WIDTH),
        'rwkv_w0_f': decay_base + 0.1 * nrm((L, W)),
        'rwkv_w0_b': decay_base + 0.1 * nrm((L, W)),
        'rwkv_w2_f': dense((L, RWKV_DECAY_RANK, W), RWKV_DECAY_RANK, 0.1),
        'rwkv_w2_b': dense((L, RWKV_DECAY_RANK, W), RWKV_DECAY_RANK, 0.1),
        'rwkv_a0_f': 0.1 * nrm((L, W)),
        'rwkv_a0_b': 0.1 * nrm((L, W)),
        'rwkv_a2_f': dense((L, RWKV_ICLR_RANK, W), RWKV_ICLR_RANK, 0.1),
        'rwkv_a2_b': dense((L, RWKV_ICLR_RANK, W), RWKV_ICLR_RANK, 0.1),
        'rwkv_g2': dense((L, RWKV_GATE_RANK, W), RWKV_GATE_RANK),
        'rwkv_k_k': 0.85 + 0.02 * nrm((L, W)),
        'rwkv_k_a': 1.0 + 0.02 * nrm((L, W)),
        'rwkv_r_k': 0.1 * nrm((L, H, N)),
        'rwkv_lnx_g': gain((L, W)),
        'rwkv_lnx_b': 0.01 * nrm((L, W)),
        'ret_gn_g': gain((L, W)),
        'mla_q_a_norm': gain((L, MLA_Q_RANK)),
        'mla_q_b': dense((L, MLA_Q_RANK, H * (MLA_NOPE + MLA_ROPE)), MLA_Q_RANK),
        'mla_kv_a_norm': gain((L, MLA_KV_RANK)),
        'mla_kv_b': dense((L, MLA_KV_RANK, H * (MLA_NOPE + MLA_V)), MLA_KV_RANK),
        'ffn2_norm': gain((L, D_MODEL)),
        'ffn2_w_gate': dense((L, D_MODEL, D_FF), D_MODEL),
        'ffn2_w_up': dense((L, D_MODEL, D_FF), D_MODEL),
        'ffn2_w_down': dense((L, D_FF, D_MODEL), D_FF),
        'final_norm': gain((D_MODEL,)),
    }

def second_block(x, positions, ffn1_norm, ffn1_w_gate, ffn1_w_up, ffn1_w_down, mix_norm, w_in, w_out,
              conv_w, rwkv_w0_f, rwkv_w0_b, rwkv_w2_f, rwkv_w2_b, rwkv_a0_f, rwkv_a0_b, rwkv_a2_f,
              rwkv_a2_b, rwkv_g2, rwkv_k_k, rwkv_k_a, rwkv_r_k, rwkv_lnx_g, rwkv_lnx_b, ret_gn_g,
              mla_q_a_norm, mla_q_b, mla_kv_a_norm, mla_kv_b, ffn2_norm, ffn2_w_gate, ffn2_w_up,
              ffn2_w_down, final_norm):
    split_points = tuple(int(p) for p in np.cumsum(IN_SPLITS)[:-1])
    for l in range(DEPTH):
        x = x + 0.5 * swiglu(rmsnorm(x, ffn1_norm[l]), ffn1_w_gate[l], ffn1_w_up[l], ffn1_w_down[l])
        h = rmsnorm(x, mix_norm[l])
        u = h @ w_in[l]
        (c_x, c_b, c_c, rw_r, rw_k, rw_v, rw_wd_f, rw_wd_b, rw_ad_f, rw_ad_b, rw_gd,
         rt_q, rt_k, rt_v, rt_g, ml_qa, ml_kva) = jnp.split(u, split_points, axis=-1)
        y_conv = short_conv_mixer(c_x, c_b, c_c, conv_w[l])
        y_rwkv = rwkv7_mixer(rw_r, rw_k, rw_v, rw_wd_f, rw_wd_b, rw_ad_f, rw_ad_b, rw_gd,
                             rwkv_w0_f[l], rwkv_w0_b[l], rwkv_w2_f[l], rwkv_w2_b[l],
                             rwkv_a0_f[l], rwkv_a0_b[l], rwkv_a2_f[l], rwkv_a2_b[l], rwkv_g2[l],
                             rwkv_k_k[l], rwkv_k_a[l], rwkv_r_k[l], rwkv_lnx_g[l], rwkv_lnx_b[l])
        y_ret = retention_mixer(rt_q, rt_k, rt_v, rt_g, positions, ret_gn_g[l])
        y_mla = mla_mixer(ml_qa, ml_kva, positions, mla_q_a_norm[l], mla_q_b[l], mla_kv_a_norm[l], mla_kv_b[l])
        x = x + jnp.concatenate([y_conv, y_rwkv, y_ret, y_mla], axis=-1) @ w_out[l]
        x = x + 0.5 * swiglu(rmsnorm(x, ffn2_norm[l]), ffn2_w_gate[l], ffn2_w_up[l], ffn2_w_down[l])
    return rmsnorm(x, final_norm)


def setup_inputs(seed=0):
    out = dict(first_inputs(seed))
    for name, value in second_inputs(seed + 1).items():
        if name != "x":
            out[name + "_2"] = value
    return out


def reference(
    x, rel_table, router_w, router_b, ln1_g, ln1_b, ln2_g, ln2_b, exp_w_gate, exp_w_up,
    exp_w_down, dil_w_in, dil_w_out, sb_w_in, sb_w_out, nsa_w_in, nsa_w_out, nsa_cmp_pos_k,
    nsa_cmp_w1_k, nsa_cmp_w2_k, nsa_cmp_pos_v, nsa_cmp_w1_v, nsa_cmp_w2_v, moba_w_in,
    moba_w_out, positions_2, ffn1_norm_2, ffn1_w_gate_2, ffn1_w_up_2, ffn1_w_down_2, mix_norm_2,
    w_in_2, w_out_2, conv_w_2, rwkv_w0_f_2, rwkv_w0_b_2, rwkv_w2_f_2, rwkv_w2_b_2, rwkv_a0_f_2,
    rwkv_a0_b_2, rwkv_a2_f_2, rwkv_a2_b_2, rwkv_g2_2, rwkv_k_k_2, rwkv_k_a_2, rwkv_r_k_2,
    rwkv_lnx_g_2, rwkv_lnx_b_2, ret_gn_g_2, mla_q_a_norm_2, mla_q_b_2, mla_kv_a_norm_2,
    mla_kv_b_2, ffn2_norm_2, ffn2_w_gate_2, ffn2_w_up_2, ffn2_w_down_2, final_norm_2,
):
    x = first_block(
        x, rel_table, router_w, router_b, ln1_g, ln1_b, ln2_g, ln2_b, exp_w_gate, exp_w_up,
        exp_w_down, dil_w_in, dil_w_out, sb_w_in, sb_w_out, nsa_w_in, nsa_w_out, nsa_cmp_pos_k,
        nsa_cmp_w1_k, nsa_cmp_w2_k, nsa_cmp_pos_v, nsa_cmp_w1_v, nsa_cmp_w2_v, moba_w_in,
        moba_w_out,
    )
    return second_block(
        x, positions_2, ffn1_norm_2, ffn1_w_gate_2, ffn1_w_up_2, ffn1_w_down_2, mix_norm_2,
        w_in_2, w_out_2, conv_w_2, rwkv_w0_f_2, rwkv_w0_b_2, rwkv_w2_f_2, rwkv_w2_b_2,
        rwkv_a0_f_2, rwkv_a0_b_2, rwkv_a2_f_2, rwkv_a2_b_2, rwkv_g2_2, rwkv_k_k_2, rwkv_k_a_2,
        rwkv_r_k_2, rwkv_lnx_g_2, rwkv_lnx_b_2, ret_gn_g_2, mla_q_a_norm_2, mla_q_b_2,
        mla_kv_a_norm_2, mla_kv_b_2, ffn2_norm_2, ffn2_w_gate_2, ffn2_w_up_2, ffn2_w_down_2,
        final_norm_2,
    )


_drawn_inputs = setup_inputs


def setup_inputs(seed=0):
    import zlib

    import numpy as np

    out = dict(_drawn_inputs(seed))
    spreads = {}
    factors = {'ffn1_norm_2': 3.624,
     'rwkv_w2_f_2': 8.0,
     'rwkv_w2_b_2': 8.0,
     'rwkv_a0_f_2': 4.785,
     'rwkv_a0_b_2': 4.973,
     'rwkv_a2_f_2': 4.368,
     'rwkv_a2_b_2': 4.38,
     'rwkv_k_k_2': 21.942,
     'rwkv_k_a_2': 5.891,
     'rwkv_lnx_g_2': 8.0,
     'rwkv_lnx_b_2': 30.454,
     'ret_gn_g_2': 7.527,
     'mla_q_a_norm_2': 8.0,
     'mla_kv_a_norm_2': 8.0,
     'ffn2_norm_2': 5.382,
     'final_norm_2': 8.29}
    for name, (base, spread) in spreads.items():
        noise = np.random.default_rng([zlib.crc32(name.encode()), seed]).standard_normal(out[name].shape)
        drawn = base * np.exp(spread * noise) if base else spread * noise
        out[name] = jnp.asarray(drawn.astype(out[name].dtype))
    for name, factor in factors.items():
        out[name] = (out[name] * factor).astype(out[name].dtype)
    return out
```

```python
from contextlib import ExitStack

import concourse.bass as bass
import numpy as np
from concourse import mybir

F32 = mybir.dt.float32
F32R = mybir.dt.float32r
I32 = mybir.dt.int32
U32 = mybir.dt.uint32
ALU = mybir.AluOpType
ACT = mybir.ActivationFunctionType
AX_X = mybir.AxisListType.X

P = 128
SEQ = 256
TILES = SEQ // P
D = 1024
KC = D // P
HD = 64
HEADS = 16
PAIRS = HEADS // 2
GROUPS = 3
DILATION = (1, 4, 16)
SPAN = (128, 512, 2048)
BUCKETS, BUCKET_DIST = 32, 2048
EXPERTS, EXPERT_FF = 16, 256
MOE_CHUNKS = EXPERTS * EXPERT_FF // P
FF_CHUNKS = 2816 // P
DEPTH = 2
ALPHA = (2 * DEPTH) ** 0.25
UNIT = 3 * KC * P
SLOTS = 4
NEG = -1e30
SB_CLIP = 60.0
CH = 64
MIX_HEADS = 4
U_CHUNKS = 30
(U_CX, U_CB, U_CC, U_RQ, U_RK, U_RV, U_RG, U_QA, U_CKV, U_KR, U_R, U_K, U_V, U_WD, U_AD, U_GD) = (
    0, 2, 4, 6, 8, 10, 12, 14, 17, 18, 19, 21, 23, 25, 26, 27)
(V_F1, V_MIX, V_F2, V_CONV, V_W0, V_A0, V_KK, V_KA, V_RK, V_LG, V_LB, V_GN, V_QN, V_KVN) = (
    0, 8, 16, 24, 30, 34, 38, 40, 42, 44, 46, 48, 50, 53)
N_VEC = 54
W_W2, W_A2, W_G2, W_QB, W_KB, W_VB = 0, 256, 512, 768, 768 + 3 * 512, 768 + 3 * 512 + 256
N_SMALL = W_VB + 256


def bucket(dist):
    n = np.maximum(dist, 0)
    exact = BUCKETS // 2
    logf = np.log(np.maximum(n, 1).astype(np.float32) / np.float32(exact)) / np.float32(
        np.log(BUCKET_DIST / exact))
    large = np.minimum(exact + (logf * np.float32(BUCKETS - exact)).astype(np.int32), BUCKETS - 1)
    return np.where(n < exact, n, large)


def constants():
    r, c = np.arange(P)[:, None], np.arange(P)[None, :]
    out = {"ident": (r == c) * 1.0, "flip": (r + c == P - 1) * 1.0}
    def turn(half, lo, hi):
        m = np.zeros((P, P))
        for t in range(lo, hi):
            j = (t - lo) % (2 * half)
            if j < half:
                m[t + half, t] = -1.0
            else:
                m[t - half, t] = 1.0
        return m
    out["turn_ret"] = turn(32, 0, 128)
    out["turn_mla"] = turn(16, 64, 96)
    same = (r // HD) == (c // HD)
    out["ones_head"] = same * 1.0
    out["ones"] = np.ones((P, SEQ))
    out["sb_mask"] = (c > P - 1 - r) * 1.0
    gamma = 1.0 - 2.0 ** (-5.0 - np.arange(MIX_HEADS))
    dist = np.abs(np.arange(3 * P)[None, :] - P - r)
    out["decay"] = np.concatenate([g ** dist / 8.0 for g in gamma], 1)
    out["tri"] = np.concatenate([same * (r < c), same * (r <= c), same * (r > c), same * (r >= c)], 1)
    levels = []
    for lower in (True, False):
        for lv in range(6):
            b = 1 << lv
            a, z = (r, c) if lower else (c, r)
            levels.append(((a // (2 * b)) == (z // (2 * b))) & (a // b % 2 == 1) & (z // b % 2 == 0))
    out["levels"] = np.concatenate(levels, 1) * 1.0
    t = np.arange(SEQ)
    out["keep"] = np.tile(np.concatenate([t % CH != 0, t % CH != CH - 1])[None] * 1.0, (P, 1))
    inv_r = 10000.0 ** (-(np.arange(32, dtype=np.float32)) / np.float32(32))
    inv_m = 10000.0 ** (-(np.arange(16, dtype=np.float32)) / np.float32(16))
    out["inv"] = np.stack([np.tile(inv_r.astype(np.float32), 4), np.tile(inv_m.astype(np.float32), 8)], 1)
    out["eps"] = np.tile(np.array([[1e-5, 1e-6, 64e-5, 1.0, 0.0]]), (P, 1))
    dist = 255 - np.arange(3 * P)
    hot = np.zeros((P, GROUPS, 3 * P))
    for g in range(GROUPS):
        seen = (dist >= 0) & (dist % DILATION[g] == 0) & (dist <= SPAN[g])
        hot[bucket(dist), g, np.arange(3 * P)] = 8.0
        hot[:, g, ~seen] = 0.0
        hot[BUCKETS, g, ~seen] = 1.0
    out["hot"] = hot.reshape(P, -1)
    pick = np.zeros((P, EXPERTS, P))
    pick[np.arange(EXPERTS), np.arange(EXPERTS), :] = 1.0
    out["pick"] = pick.reshape(P, -1)
    lower4 = np.tril(np.ones((4, 4)), -1)
    out["before"] = np.tile(lower4.reshape(1, 16), (P, 1))
    return {k: np.ascontiguousarray(v, np.float32) for k, v in out.items()}


CONST_ORDER = ["ident", "flip", "turn_ret", "turn_mla", "ones_head", "ones", "sb_mask", "decay", "tri",
               "levels", "keep", "inv", "eps", "before"]
EARLY_ORDER = ["hot", "pick"]


def layout(inputs):
    f = {k: np.asarray(v) for k, v in inputs.items()}

    def rows(w):
        return w.reshape(-1, P, w.shape[-1]).transpose(1, 0, 2)

    def glu(gate, up, down):
        n = gate.shape[1] // P
        g = gate.reshape(KC, P, n, P).transpose(2, 1, 0, 3).reshape(n, P, -1)
        u = up.reshape(KC, P, n, P).transpose(2, 1, 0, 3).reshape(n, P, -1)
        return np.concatenate([g, u, down.reshape(n, P, D)], 2)

    out = {"x": f["x"][0], "rel_table": f["rel_table"], "router_b": f["router_b"],
           "router_w": rows(f["router_w"]), "positions": f["positions_2"].astype(np.int32)}
    w = f["dil_w_in"][0].reshape(KC, P, GROUPS, 3, PAIRS, P)
    out["dil_w"] = w.transpose(4, 2, 1, 0, 3, 5).reshape(PAIRS, GROUPS, P, UNIT)
    w = f["sb_w_in"][0].reshape(KC, P, 3, PAIRS, P)
    out["sb_w"] = w.transpose(3, 1, 0, 2, 4).reshape(PAIRS, P, UNIT)
    out["proj_w"] = np.stack([rows(w).reshape(P, 4, 2 * D).transpose(1, 0, 2)
                              for w in (f["dil_w_out"][0], f["sb_w_out"][0], f["w_out_2"][0], f["w_out_2"][1])])
    moe = []
    for l in range(DEPTH):
        g = f["exp_w_gate"][l].transpose(1, 0, 2).reshape(D, -1)
        u = f["exp_w_up"][l].transpose(1, 0, 2).reshape(D, -1)
        moe.append(glu(g, u, f["exp_w_down"][l].reshape(-1, D)))
    out["moe_w"] = np.stack(moe)
    out["ff_w"] = np.stack([glu(f[f"ffn{n}_w_gate_2"][l], f[f"ffn{n}_w_up_2"][l], f[f"ffn{n}_w_down_2"][l])
                            for l in range(DEPTH) for n in (1, 2)])
    mix, small, vec = [], [], []
    for l in range(DEPTH):
        w = f["w_in_2"][l]
        cut = np.cumsum([256] * 6 + [64, 64, 64, 64, 128] + [256] * 4 + [384, 160])[:-1]
        (cx, cb, cc, r, k, v, wdf, wdb, adf, adb, gd, rq, rk, rv, rg, qa, kva) = np.split(w, cut, axis=1)
        z64 = np.zeros((D, 64), np.float32)
        kr = np.concatenate([z64, kva[:, 128:], np.zeros((D, 32), np.float32)], 1)
        u = np.concatenate([cx, cb, cc, rq, rk, rv, rg, qa, kva[:, :128], kr, r, k, v, wdf, wdb, adf, adb, gd,
                            np.zeros((D, 256), np.float32)], 1)
        mix.append(u.reshape(KC, P, U_CHUNKS // 3, 3 * P).transpose(2, 1, 0, 3).reshape(U_CHUNKS // 3, P, UNIT))
        qb = f["mla_q_b_2"][l].reshape(384, 4, 96)
        qb = np.concatenate([qb, np.zeros((384, 4, 32), np.float32)], 2).reshape(384, 512)
        kvb = f["mla_kv_b_2"][l].reshape(P, 4, 128)
        small.append(np.concatenate([
            np.concatenate([f["rwkv_w2_f_2"][l], f["rwkv_w2_b_2"][l]], 0),
            np.concatenate([f["rwkv_a2_f_2"][l], f["rwkv_a2_b_2"][l]], 0),
            f["rwkv_g2_2"][l], rows(qb).reshape(P, -1),
            kvb[:, :, :64].reshape(P, 256), kvb[:, :, 64:].reshape(P, 256)], 1))
        col = lambda a: a.reshape(-1, P).T
        vec.append(np.concatenate([
            col(f["ffn1_norm_2"][l]), col(f["mix_norm_2"][l]), col(f["ffn2_norm_2"][l]),
            col(f["conv_w_2"][l]), col(f["rwkv_w0_f_2"][l]), col(f["rwkv_w0_b_2"][l]),
            col(f["rwkv_a0_f_2"][l]), col(f["rwkv_a0_b_2"][l]), col(f["rwkv_k_k_2"][l]), col(f["rwkv_k_a_2"][l]),
            col(f["rwkv_r_k_2"][l].reshape(-1)), col(f["rwkv_lnx_g_2"][l]), col(f["rwkv_lnx_b_2"][l]),
            col(f["ret_gn_g_2"][l]), col(f["mla_q_a_norm_2"][l]), col(f["mla_kv_a_norm_2"][l])], 1))
    out["mix_w"] = np.stack(mix)
    out["small_w"] = np.stack(small)
    out["vectors"] = np.stack(vec)
    out["row_vectors"] = np.stack([f["ln1_g"][0], f["ln1_b"][0], f["ln2_g"][0], f["ln2_b"][0],
                                   f["ln1_g"][1], f["ln1_b"][1], f["ln2_g"][1], f["ln2_b"][1],
                                   f["final_norm_2"]])
    c = constants()
    out["tables"] = np.concatenate([c[k] for k in CONST_ORDER], 1)
    out["early_tables"] = np.concatenate([c[k] for k in EARLY_ORDER], 1)
    return {k: np.ascontiguousarray(v) for k, v in out.items()}


class Ring:

    def __init__(self):
        self.count = [0] * SLOTS
        self.silent = [0] * SLOTS
        self.next = 0

    def take(self, n):
        out = []
        for _ in range(n):
            out.append((self.next, self.count[self.next]))
            self.count[self.next] += 1
            self.next = (self.next + 1) % SLOTS
        return out

    def skip(self, slots, turns):
        for s in slots:
            self.count[s] += turns


def build_kernel(nc, d, out):
    ctx = ExitStack()
    consts = constants()

    with ctx:
        def sb(name, shape, dt=F32):
            return ctx.enter_context(nc.sbuf_tensor(name, shape, dt))

        def sem(name):
            return ctx.enter_context(nc.semaphore(name))

        base = nc.sbuf_base + -nc.sbuf_base % 32

        def place(name, at, shape, dt=F32):
            return nc.alloc_sbuf_tensor_at(name, shape, dt, offset=base + 4 * at)

        n_tab = sum(consts[k].shape[1] for k in CONST_ORDER)
        plan, at = {}, 0
        for name, size in (("x", TILES * D), ("xT", KC * SEQ), ("oT", KC * SEQ), ("ring", SLOTS * UNIT),
                           ("small", N_SMALL), ("rowv", 2 * D), ("zero", 256), ("stat", 32), ("lead", 8),
                           ("PC", 16), ("om", 8), ("scratch", 21760), ("vec", DEPTH * N_VEC + 4), ("tab", n_tab)):
            plan[name] = at
            at += size
        x = place("x_rows", plan["x"], [P, TILES, D])
        xT = place("xT", plan["xT"], [P, KC, SEQ])
        oT = place("oT", plan["oT"], [P, KC, SEQ])
        xT_hi = place("xT_hi", plan["xT"], [P, KC, SEQ], F32R)
        xT_lo = place("xT_lo", plan["oT"], [P, KC, SEQ], F32R)
        ring = place("ring", plan["ring"], [P, SLOTS, UNIT])
        ring_lo = place("ring_lo", plan["ring"], [P, SLOTS, UNIT], F32R)
        ring_hi = place("ring_hi", plan["scratch"] + 8192, [P, SLOTS, UNIT], F32R)
        tab = place("tab_sb", plan["tab"], [P, n_tab])
        small = place("small", plan["small"], [P, N_SMALL])
        early = place("early", plan["small"], [P, N_SMALL])
        vec = place("vec", plan["vec"], [P, DEPTH, N_VEC])
        rowv = place("rowv", plan["rowv"], [P, 2, D])
        stat = place("stat", plan["stat"], [P, TILES, 16])
        lead = place("lead", plan["lead"], [P, TILES, 4])
        zero = place("zero", plan["zero"], [P, 512], mybir.dt.bfloat16)
        scratch = place("scratch", plan["scratch"], [P, 21760])
        psum = ctx.enter_context(nc.psum_tensor("psum", [P, 8, 512], F32))
        rel_dram = nc.dram_tensor("rel_dram", [HEADS, GROUPS * 3 * P], F32, kind="Internal").ap()

        at, T = 0, {}
        for k in CONST_ORDER:
            T[k] = tab[:, at:at + consts[k].shape[1]]
            at += consts[k].shape[1]
        eps = {k: T["eps"][:, i:i + 1] for i, k in enumerate(("ln", "rms", "gn", "one", "zero"))}

        def carve(at, *shape):
            size = int(np.prod(shape))
            v = scratch[:, at:at + size]
            names = "abcd"[:len(shape)]
            if len(shape) == 1:
                return v
            return v.rearrange(f"p ({' '.join(names)}) -> p {' '.join(names)}",
                               **{n: s for n, s in zip(names[1:], shape[1:])})

        glu_s = carve(0, SLOTS, SEQ)
        glu_t = carve(1024, SLOTS, SEQ)
        glu_hi = place("glu_hi", plan["scratch"] + 2048, [P, SLOTS, SEQ], F32R)
        glu_lo = place("glu_lo", plan["scratch"] + 3072, [P, SLOTS, SEQ], F32R)
        hn = carve(4096, TILES, D)
        route_w = carve(4096, EXPERTS, SEQ)
        pick = early[:, 0:2048].rearrange("p (e n) -> p e n", e=EXPERTS)
        router_w = early[:, 2048:2176].rearrange("p (k e) -> p k e", k=KC)
        router_b = early[:, 2176:2192]
        rt = carve(0, 1024)
        hot = carve(13968, GROUPS * 3 * P)
        rel_tab = carve(15120, HEADS)
        rel_rows = carve(15816, GROUPS * 3 * P)
        xTr = carve(13968, KC, SEQ)
        qk_sb = carve(0, 2, GROUPS, 2 * SEQ)
        v_sb = carve(3072, 2, GROUPS, TILES * P)
        bias_sb = carve(4608, 2, 2, GROUPS * SEQ)
        probs = carve(15816, 2, GROUPS * 3 * P)
        probsT = carve(18120, 2, GROUPS * 3 * P)
        soft = carve(20424, 4, 4)
        sb_qk = carve(0, 2, 2 * SEQ)
        sb_v = carve(1024, 2, SEQ)
        sb_z = carve(1536, 2, 3 * P)
        sb_a = carve(2304, 2, 3 * P)
        sb_p = carve(3072, 2, 3 * P)
        sb_r = carve(3840, 2, 3 * P)
        sb_aT = carve(4608, 2, 3 * P)

        ring_full = [sem(f"ring_full{i}") for i in range(SLOTS)]
        ring_free = [sem(f"ring_free{i}") for i in range(SLOTS)]
        x_loaded, tables_loaded = sem("x_loaded"), sem("tables_loaded")
        early_loaded, router_loaded = sem("early_loaded"), sem("router_loaded")
        rel_ready, rel_copied, rel_stored = sem("rel_ready"), sem("rel_copied"), sem("rel_stored")
        bias_full = [sem("bias_full0"), sem("bias_full1")]
        rowv_full, rowv_used = sem("rowv_full"), sem("rowv_used")
        acc_ready = sem("acc_ready")
        acc_used = sem("acc_used")
        var_ready, dev_ready = sem("var_ready"), sem("dev_ready")
        rows_ready = sem("rows_ready")
        turned, turned_used = sem("turned"), sem("turned_used")
        high_ready, low_ready = sem("high_ready"), sem("low_ready")
        turned_high = sem("turned_high")
        gate_up, silu_ready, hidden_ready = sem("gate_up"), sem("silu_ready"), sem("hidden_ready")
        logits_ready, router_sig = sem("logits_ready"), sem("router_sig")
        gates_ready, gatesT_ready, gatesT_copied = sem("gates_ready"), sem("gatesT_ready"), sem("gatesT_copied")
        spread_ready, spread_copied = sem("spread_ready"), sem("spread_copied")
        qk_ready, qk_copied = sem("qk_ready"), sem("qk_copied")
        v_ready, v_copied = sem("v_ready"), sem("v_copied")
        scores_ready, max_ready, exp_ready = sem("scores_ready"), sem("max_ready"), sem("exp_ready")
        probs_ready, probsT_ready, probsT_copied = sem("probs_ready"), sem("probsT_ready"), sem("probsT_copied")
        o_ready, o_copied = sem("o_ready"), sem("o_copied")
        sb_qk_ready, sb_qk_copied = sem("sb_qk_ready"), sem("sb_qk_copied")
        sb_v_ready, sb_v_copied = sem("sb_v_ready"), sem("sb_v_copied")
        sb_scores, sb_clipped, sb_exp1, sb_soft = sem("sb_scores"), sem("sb_clipped"), sem("sb_exp1"), sem("sb_soft")
        sb_minus, sb_exp2, sb_att = sem("sb_minus"), sem("sb_exp2"), sem("sb_att")
        sb_aT_ready, sb_aT_copied = sem("sb_aT_ready"), sem("sb_aT_copied")
        sb_o_ready, sb_o_copied = sem("sb_o_ready"), sem("sb_o_copied")
        vec_loaded = sem("vec_loaded")
        dumped, zero_ready = sem("dumped"), sem("zero_ready")
        stored = sem("stored")

        acc = psum[:, 4:8, :].rearrange("p (t n) c -> p t (n c)", t=TILES)

        def load_units(sp, units, n, floats):
            r = sync_ring
            turns = n // SLOTS
            first = r.next
            lanes = [(first + k) % SLOTS for k in range(SLOTS)]

            def load(k, s, value, src):
                if not isinstance(value, int) or value > 0:
                    sp.wait_ge(ring_free[s], value)
                sp.dma_start(ring[:, s, 0:floats], src).then_inc(ring_full[s], 16)

            freed = lambda s: r.count[s] - r.silent[s]
            start = 1 if min(freed(s) for s in lanes) < 1 else 0
            for k in range(start * SLOTS):
                load(k, lanes[k], freed(lanes[k]), units[k])
                r.count[lanes[k]] += 1
            if turns - start > 1:
                with sp.Fori(0, turns - start) as i:
                    for k, s in enumerate(lanes):
                        src = units[bass.ds(i * SLOTS + (start * SLOTS + k), 1)].rearrange("o p n -> (o p) n")
                        load(k, s, i + freed(s), src)
                r.skip(lanes, turns - start)
                start = turns
            for k in range(start * SLOTS, n):
                s = lanes[k % SLOTS]
                load(k, s, freed(s), units[k])
                r.count[s] += 1
            r.next = (first + n) % SLOTS

        def load_dilated(sp):
            for g in range(GROUPS):
                sp.dma_start(ring[:, g, :], d["dil_w"][0, g]).then_inc(ring_full[g], 16)
            with sp.Fori(1, PAIRS) as p:
                for g in range(GROUPS):
                    sp.wait_ge(v_copied, p * GROUPS + (g + 1 - GROUPS))
                    src = d["dil_w"].rearrange("a g p n -> (a g) p n")[bass.ds(p * GROUPS + g, 1)]
                    sp.dma_start(ring[:, g, :], src.rearrange("o p n -> (o p) n")).then_inc(ring_full[g], 16)
            sync_ring.skip(range(GROUPS), PAIRS)
            for g in range(GROUPS):
                sync_ring.silent[g] = PAIRS
            sp.wait_ge(v_copied, PAIRS * GROUPS)

        sync_ring, pe_ring, act_ring, dve_ring = Ring(), Ring(), Ring(), Ring()

        def products(dst, w_hi, w_lo, m_hi, m_lo, start, stop, **kw):
            nc.tensor.matmul(dst, w_hi, m_hi, start=start, stop=False, **kw)
            nc.tensor.matmul(dst, w_hi, m_lo, start=False, stop=False, **kw)
            return nc.tensor.matmul(dst, w_lo, m_hi, start=False, stop=stop, **kw)

        n_norm = [0, 0, 0, 0]

        class Uses:
            def __init__(self):
                self.acc = self.var = self.dev = self.rows = self.turned = self.high = self.rowv = 0
        pe_u, dve_u, act_u = Uses(), Uses(), Uses()

        def dve_norm(update, ln=False, rms=False, gain=None, turn=True, flip=False, parts=False):
            u, v = dve_u, nc.vector
            if update is not None:
                v.wait_ge(acc_ready, u.acc + 1)
                u.acc += 1
                for t in range(TILES):
                    if update == "norm":
                        v.scalar_tensor_tensor(out=x[:, t, :], in0=x[:, t, :], scalar=ALPHA, in1=acc[:, t, :],
                                               op0=ALU.mult, op1=ALU.add).then_inc(acc_used, 1)
                    else:
                        v.scalar_tensor_tensor(out=x[:, t, :], in0=acc[:, t, :], scalar=update, in1=x[:, t, :],
                                               op0=ALU.mult, op1=ALU.add).then_inc(acc_used, 1)
                v.drain()
            if ln:
                for t in range(TILES):
                    for h in range(2):
                        v.bn_stats(stat[:, t, 6 * h:6 * h + 6], x[:, t, 512 * h:512 * h + 512])
                v.drain()
                for t in range(TILES):
                    last = v.bn_aggr(lead[:, t, 0:2], stat[:, t, 0:12])
                last.then_inc(var_ready, 1)
                v.wait_ge(dev_ready, u.dev + 1)
                u.dev += 1
                v.reciprocal(lead[:, :, 3:4], lead[:, :, 2:3])
                v.drain()
                for t in range(TILES):
                    v.tensor_scalar(x[:, t, :], x[:, t, :], lead[:, t, 0:1], lead[:, t, 3:4],
                                    ALU.subtract, ALU.mult)
                v.drain()
                v.wait_ge(rowv_full, 16 * (u.rowv + 1))
                u.rowv += 1
                for t in range(TILES):
                    v.tensor_tensor(x[:, t, :], x[:, t, :], rowv[:, 0, :], ALU.mult)
                v.drain()
                for t in range(TILES):
                    last = v.tensor_tensor(x[:, t, :], x[:, t, :], rowv[:, 1, :], ALU.add)
                    if not rms:
                        last.then_inc(rows_ready, 1)
                v.drain()
                v.sem_inc(rowv_used, 1)
            rows = x
            if rms:
                v.sem_inc(var_ready, 1)
                v.wait_ge(dev_ready, u.dev + 1)
                u.dev += 1
                v.reciprocal(lead[:, :, 3:4], lead[:, :, 2:3])
                v.drain()
                rows = hn
                for t in range(TILES):
                    v.tensor_scalar(hn[:, t, :], x[:, t, :], lead[:, t, 3:4], None, ALU.mult)\
                     .then_inc(rows_ready, 1)
            if not turn:
                v.drain()
                return
            for side in range(2 if flip else 1):
                for b in range(4):
                    u.turned += 1
                    dst = (xT, xTr)[side]
                    if parts:
                        u.high += 1
                        v.wait_ge(turned_high, u.high)
                        for c in range(2):
                            lo, hi = xT_lo[:, 2 * b + c, :], xT_hi[:, 2 * b + c, :].bitcast(F32)
                            src = psum[:, b, c * SEQ:(c + 1) * SEQ]
                            if gain is None:
                                last = v.tensor_tensor(lo, src, hi, ALU.subtract)
                            else:
                                last = v.scalar_tensor_tensor(out=lo, in0=src, scalar=gain[:, 2 * b + c:2 * b + c + 1],
                                                              in1=hi, op0=ALU.mult, op1=ALU.subtract)
                        last.then_inc(turned_used, 1)
                        continue
                    v.wait_ge(turned, u.turned)
                    if gain is None:
                        v.tensor_copy(dst[:, 2 * b:2 * b + 2, :], psum[:, b, :]).then_inc(turned_used, 1)
                    else:
                        for c in range(2):
                            last = v.tensor_scalar(dst[:, 2 * b + c, :], psum[:, b, c * SEQ:(c + 1) * SEQ],
                                                   gain[:, 2 * b + c:2 * b + c + 1], None, ALU.mult)
                        last.then_inc(turned_used, 1)

        def act_norm(ln=False, rms=False, gain=None, turns=4, parts=False):
            u = act_u
            if ln:
                nc.scalar.wait_ge(var_ready, u.var + 1)
                u.var += 1
                nc.scalar.activation(lead[:, :, 2:3], lead[:, :, 1:2], ACT.Sqrt, bias=eps["ln"]).then_inc(dev_ready, 1)
            if rms:
                nc.scalar.wait_ge(var_ready, u.var + 1)
                u.var += 1
                for t in range(TILES):
                    nc.scalar.activation(hn[:, t, :], x[:, t, :], ACT.Square, accum_out=lead[:, t, 0:1])
                nc.scalar.drain()
                nc.scalar.activation(lead[:, :, 2:3], lead[:, :, 0:1], ACT.Sqrt, bias=eps["rms"],
                                     scale=1.0 / D).then_inc(dev_ready, 1)
            if parts:
                for b in range(4):
                    nc.scalar.wait_ge(turned, u.turned + b + 1)
                    if gain is None:
                        nc.scalar.copy(xT_hi[:, 2 * b:2 * b + 2, :].rearrange("p c n -> p (c n)"), psum[:, b, :])\
                          .then_inc(turned_high, 1)
                    else:
                        for c in range(2):
                            last = nc.scalar.activation(xT_hi[:, 2 * b + c, :], psum[:, b, c * SEQ:(c + 1) * SEQ],
                                                        ACT.Copy, scale=gain[:, 2 * b + c:2 * b + c + 1])
                        last.then_inc(turned_high, 1)
            u.turned += turns

        def pe_turn(rows, flip=False, counted=True):
            u = pe_u
            for side in range(2 if flip else 1):
                for b in range(4):
                    if side:
                        nc.tensor.wait_ge(turned_used, u.turned - 3)
                    for c in range(2):
                        for t in range(TILES):
                            if counted and side == 0 and b == 0 and c == 0 and t == 0:
                                u.rows += TILES
                                nc.tensor.wait_ge(rows_ready, u.rows)
                            src = rows[:, t, (2 * b + c) * P:(2 * b + c + 1) * P]
                            dst = psum[:, b, c * SEQ + t * P:c * SEQ + (t + 1) * P]
                            if side:
                                dst = psum[:, b, c * SEQ + (1 - t) * P:c * SEQ + (2 - t) * P]
                                last = nc.tensor.matmul(dst, src, T["flip"], start=True, stop=True)
                            else:
                                last = nc.tensor.transpose(dst, src, T["ident"])
                    last.then_inc(turned, 1)
                    u.turned += 1

        def pe_project(src, ready, value):
            nc.tensor.wait_ge(ready, value)
            for u, (s, turn) in enumerate(pe_ring.take(4)):
                nc.tensor.wait_ge(ring_full[s], 16 * (turn + 1))
                if u == 0 and pe_u.acc:
                    nc.tensor.wait_ge(acc_used, 2 * pe_u.acc)
                for c in range(2):
                    k = 2 * u + c
                    for t in range(TILES):
                        for n in range(2):
                            last = nc.tensor.matmul(
                                psum[:, 4 + 2 * t + n, :], src[:, k, t * P:(t + 1) * P],
                                ring[:, s, c * D + n * 512:c * D + (n + 1) * 512],
                                start=(k == 0), stop=(k == KC - 1))
                last.then_inc(ring_free[s], 1)
            nc.tensor.matmul(psum[0:1, 0, 0:1], src[:, 0, 0:1], src[:, 0, 0:1], start=True, stop=True)\
              .then_inc(acc_ready, 1)
            pe_u.acc += 1

        glu_done = {"pe": 0, "act": 0, "dve": 0}

        def steps(engine, n, body):
            turns, rest = divmod(n, SLOTS)
            with engine.Fori(0, turns) as i:
                for j in range(SLOTS):
                    body(i, j)
            for j in range(rest):
                body(0, turns * SLOTS + j)

        def pe_glu(chunks):
            base, s0 = glu_done["pe"], pe_ring.next

            def gates(i, j):
                s = (s0 + j) % SLOTS
                nc.tensor.wait_ge(low_ready, i * SLOTS + (base + j + 1))
                for part in range(2):
                    for k in range(KC):
                        cols = slice(part * D + k * P, part * D + (k + 1) * P)
                        last = products(psum[:, j % SLOTS, part * SEQ:(part + 1) * SEQ],
                                        ring_hi[:, s, cols], ring_lo[:, s, cols], xT_hi[:, k, :], xT_lo[:, k, :],
                                        start=(k == 0), stop=(k == KC - 1))
                last.then_inc(gate_up, 1)

            def down(i, j):
                s = (s0 + j) % SLOTS
                nc.tensor.wait_ge(hidden_ready, i * SLOTS + (base + j + 1))
                for t in range(TILES):
                    tok = slice(t * P, (t + 1) * P)
                    for h in range(2):
                        cols = slice(2 * D + h * 512, 2 * D + (h + 1) * 512)
                        last = products(psum[:, 4 + 2 * t + h, :], glu_hi[:, j % SLOTS, tok], glu_lo[:, j % SLOTS, tok],
                                        ring_hi[:, s, cols], ring_lo[:, s, cols],
                                        start=False, stop=False, skip_group_check=True)
                last.then_inc(ring_free[s], 1)

            def step(i, j):
                gates(i, j + 1)
                down(i, j)

            if pe_u.acc:
                nc.tensor.wait_ge(acc_used, 2 * pe_u.acc)
            for b in range(4):
                nc.tensor.matmul(psum[:, 4 + b, :], zero[:, 0:P], zero[:, 0:512], start=True, stop=False)
            gates(0, 0)
            steps(nc.tensor, chunks - 1, step)
            down(0, chunks - 1)
            for b in range(4):
                last = nc.tensor.matmul(psum[:, 4 + b, :], zero[:, 0:P], zero[:, 0:512], start=False, stop=True)
            last.then_inc(acc_ready, 1)
            pe_ring.take(chunks)
            pe_u.acc += 1
            glu_done["pe"] += chunks

        def act_split(r, base, i, j):
            s = (r.next + j) % SLOTS
            nc.scalar.wait_ge(ring_full[s], i * 16 + 16 * (r.count[s] + j // SLOTS + 1))
            nc.scalar.copy(ring_hi[:, s, :], ring[:, s, :]).then_inc(high_ready, 1)

        def dve_split(r, base, i, j):
            s = (r.next + j) % SLOTS
            nc.vector.wait_ge(high_ready, i * SLOTS + (base + j + 1))
            nc.vector.tensor_tensor(ring_lo[:, s, :], ring[:, s, :], ring_hi[:, s, :].bitcast(F32), ALU.subtract)\
              .then_inc(low_ready, 1)

        def act_glu(chunks):
            base = glu_done["act"]

            def silu(i, j):
                b = j % SLOTS
                nc.scalar.wait_ge(gate_up, i * SLOTS + (base + j + 1))
                nc.scalar.activation(glu_s[:, b, :], psum[:, b, 0:SEQ], ACT.Silu).then_inc(silu_ready, 1)

            def step(i, j):
                silu(i, j)
                act_split(act_ring, base, i, j + 2)

            act_split(act_ring, base, 0, 0)
            act_split(act_ring, base, 0, 1)
            steps(nc.scalar, chunks - 2, step)
            silu(0, chunks - 2)
            silu(0, chunks - 1)
            act_ring.take(chunks)
            glu_done["act"] += chunks

        def dve_glu(chunks, weighted):
            base, v = glu_done["dve"], nc.vector

            def hidden(i, j):
                b = j % SLOTS
                v.wait_ge(silu_ready, i * SLOTS + (base + j + 1))
                v.tensor_tensor(glu_t[:, b, :], psum[:, b, SEQ:2 * SEQ], glu_s[:, b, :], ALU.mult)
                v.drain()
                if weighted:
                    w = route_w[:, bass.ds(i * (SLOTS // 2) + j // 2, 1), :].rearrange("p o n -> p (o n)")
                    v.tensor_tensor(glu_t[:, b, :], glu_t[:, b, :], w, ALU.mult)
                    v.drain()
                v.tensor_copy(glu_hi[:, b, :], glu_t[:, b, :])
                v.drain()
                v.tensor_tensor(glu_lo[:, b, :], glu_t[:, b, :], glu_hi[:, b, :].bitcast(F32), ALU.subtract)\
                 .then_inc(hidden_ready, 1)

            def step(i, j):
                hidden(i, j)
                dve_split(dve_ring, base, i, j + 2)

            dve_split(dve_ring, base, 0, 0)
            dve_split(dve_ring, base, 0, 1)
            steps(v, chunks - 2, step)
            hidden(0, chunks - 2)
            hidden(0, chunks - 1)
            dve_ring.take(chunks)
            glu_done["dve"] += chunks

        R = lambda at, *shape: rt[:, at:at + int(np.prod(shape))].rearrange(
            "p (" + " ".join("abcd"[:len(shape)]) + ") -> p " + " ".join("abcd"[:len(shape)]),
            **{n: s for n, s in zip("bcd"[:len(shape) - 1], shape[1:])}) if len(shape) > 1 else rt[:, at:at + shape[0]]
        G4 = TILES * 4
        score = R(0, TILES, EXPERTS)
        biased = R(32, TILES, EXPERTS)
        b_grp = R(32, G4, 4)
        later_ge, later_gt = R(64, G4, 4, 4), R(192, G4, 4, 4)
        rank = R(320, G4, 4)
        pair_sum = R(352, G4, 6)
        best2 = R(400, G4)
        g_ge, g_gt = R(408, TILES, 4, 4), R(440, TILES, 4, 4)
        g_rank = R(472, TILES, 4)
        chosen = R(480, G4, 4)
        gate_w = R(512, TILES, EXPERTS)
        gate_sum = R(544, TILES)
        gateT = rt[:, 560:560 + SEQ]

        def pe_router(l):
            if l == 0:
                nc.tensor.wait_ge(router_loaded, 32)
                nc.tensor.wait_ge(early_loaded, 48)
            for t in range(TILES):
                for k in range(KC):
                    if t == 0 and k == 0:
                        nc.tensor.wait_ge(turned_used, pe_u.turned)
                    for part, half in enumerate((xT_hi, xT_lo)):
                        last = nc.tensor.matmul(psum[:, 0, t * EXPERTS:(t + 1) * EXPERTS],
                                                half[:, k, t * P:(t + 1) * P].bitcast(F32), router_w[:, k, :],
                                                start=(k == 0 and part == 0), stop=(k == KC - 1 and part == 1))
            last.then_inc(logits_ready, 1)
            nc.tensor.wait_ge(gates_ready, l + 1)
            for t in range(TILES):
                last = nc.tensor.transpose(psum[0:EXPERTS, 1, t * P:(t + 1) * P], gate_w[:, t, :], T["ident"])
            last.then_inc(gatesT_ready, 1)
            nc.tensor.wait_ge(gatesT_copied, l + 1)
            for e in range(EXPERTS):
                if e >= 8 and e % 4 == 0:
                    nc.tensor.wait_ge(spread_copied, 8 * l + e // 2 - 2)
                last = nc.tensor.matmul(psum[:, e // 2 % 4, e % 2 * SEQ:(e % 2 + 1) * SEQ],
                                        pick[0:EXPERTS, e, :], gateT[0:EXPERTS, :], start=True, stop=True)
                if e % 2:
                    last.then_inc(spread_ready, 1)
            nc.tensor.wait_ge(spread_copied, 8 * l + EXPERTS // 2)

        def act_router(l):
            nc.scalar.wait_ge(logits_ready, l + 1)
            nc.scalar.activation(score, psum[:, 0, 0:TILES * EXPERTS].rearrange("p (t e) -> p t e", t=TILES),
                                 ACT.Sigmoid).then_inc(router_sig, 1)

        def dve_router(l):
            v = nc.vector
            v.wait_ge(router_sig, l + 1)
            if l == 0:
                v.wait_ge(router_loaded, 32)
            v.tensor_tensor(biased, score, router_b.unsqueeze(1).broadcast_to([P, TILES, EXPERTS]), ALU.add)
            v.drain()
            other = b_grp.unsqueeze(2).broadcast_to([P, G4, 4, 4])
            own = b_grp.unsqueeze(3).broadcast_to([P, G4, 4, 4])
            before = T["before"].rearrange("p (i j) -> p i j", i=4).unsqueeze(1)
            v.tensor_tensor(later_ge, other, own, ALU.is_ge)
            v.tensor_tensor(later_gt, other, own, ALU.is_gt)
            n = 0
            for i in range(4):
                for j in range(i + 1, 4):
                    v.tensor_tensor(pair_sum[:, :, n:n + 1], b_grp[:, :, i:i + 1], b_grp[:, :, j:j + 1], ALU.add)
                    n += 1
            v.drain()
            v.tensor_tensor(later_ge, later_ge, later_gt, ALU.subtract)
            v.tensor_reduce(best2, pair_sum, AX_X, ALU.max)
            v.drain()
            v.tensor_tensor(later_ge, later_ge, before.broadcast_to([P, G4, 4, 4]), ALU.mult)
            g_own = best2.rearrange("p (t g) -> p t g", t=TILES)
            v.tensor_tensor(g_ge, g_own.unsqueeze(2).broadcast_to([P, TILES, 4, 4]),
                            g_own.unsqueeze(3).broadcast_to([P, TILES, 4, 4]), ALU.is_ge)
            v.tensor_tensor(g_gt, g_own.unsqueeze(2).broadcast_to([P, TILES, 4, 4]),
                            g_own.unsqueeze(3).broadcast_to([P, TILES, 4, 4]), ALU.is_gt)
            v.drain()
            v.tensor_tensor(later_ge, later_ge, later_gt, ALU.add)
            v.tensor_tensor(g_ge, g_ge, g_gt, ALU.subtract)
            v.drain()
            v.tensor_reduce(rank, later_ge, AX_X, ALU.add)
            v.tensor_tensor(g_ge, g_ge, before.broadcast_to([P, TILES, 4, 4]), ALU.mult)
            v.drain()
            v.tensor_tensor(g_ge, g_ge, g_gt, ALU.add)
            v.drain()
            v.tensor_reduce(g_rank, g_ge, AX_X, ALU.add)
            v.drain()
            v.tensor_scalar(g_rank, g_rank, 0.5, None, ALU.is_lt)
            v.drain()
            v.scalar_tensor_tensor(out=chosen, in0=rank, scalar=1.5,
                                   in1=g_rank.rearrange("p t g -> p (t g)").unsqueeze(2).broadcast_to([P, G4, 4]),
                                   op0=ALU.is_lt, op1=ALU.mult)
            v.drain()
            v.tensor_tensor(gate_w, score, chosen.rearrange("p (t g) e -> p t (g e)", t=TILES), ALU.mult)
            v.drain()
            v.tensor_reduce(gate_sum, gate_w, AX_X, ALU.add)
            v.drain()
            v.reciprocal(gate_sum, gate_sum)
            v.drain()
            v.tensor_tensor(gate_w, gate_w, gate_sum.unsqueeze(2).broadcast_to([P, TILES, EXPERTS]), ALU.mult)\
             .then_inc(gates_ready, 1)
            v.wait_ge(gatesT_ready, l + 1)
            v.tensor_copy(gateT[0:EXPERTS, :], psum[0:EXPERTS, 1, 0:SEQ]).then_inc(gatesT_copied, 1)
            for b in range(EXPERTS // 2):
                v.wait_ge(spread_ready, 8 * l + b + 1)
                v.tensor_copy(route_w[:, 2 * b:2 * b + 2, :], psum[:, b % 4, :].rearrange("p (e n) -> p e n", e=2))\
                 .then_inc(spread_copied, 1)

        def width(t):
            return P * (t + 1)

        def pe_dilated():
            pe = nc.tensor

            def project_qk(p, g, par, turn):
                pe.wait_ge(ring_full[g], 16 * p + 16 * (turn + 1))
                if not (isinstance(p, int) and p == 0 and g == 0):
                    pe.wait_ge(qk_copied, 3 * p + g)
                for part in range(2):
                    for k in range(KC):
                        last = pe.matmul(psum[:, 0, part * SEQ:(part + 1) * SEQ],
                                         ring[:, g, k * 384 + part * P:k * 384 + (part + 1) * P], xT[:, k, :],
                                         start=(k == 0), stop=(k == KC - 1))
                last.then_inc(qk_ready, 1)

            def project_v(p, g, par):
                if not (isinstance(p, int) and p == 0 and g == 0):
                    pe.wait_ge(v_copied, 3 * p + g)
                for t in range(TILES):
                    for k in range(KC):
                        last = pe.matmul(psum[:, 1, t * P:(t + 1) * P], xT[:, k, t * P:(t + 1) * P],
                                         ring[:, g, k * 384 + 2 * P:k * 384 + 3 * P],
                                         start=(k == 0), stop=(k == KC - 1))
                last.then_inc(v_ready, 1)

            def scores(p, u, par):
                a, t = divmod(u, 2)
                if u == 0:
                    pe.wait_ge(qk_copied, 3 * p + 3)
                if u >= 2 or not isinstance(p, int) or p:
                    pe.wait_ge(max_ready, 4 * p + u - 1)
                for g in range(GROUPS):
                    dst = psum[:, 4, g * P:(g + 1) * P] if t == 0 else psum[:, 2 + g // 2, g % 2 * SEQ:(g % 2 + 1) * SEQ]
                    last = pe.matmul(dst, qk_sb[a * HD:(a + 1) * HD, par, g, t * P:(t + 1) * P],
                                     qk_sb[a * HD:(a + 1) * HD, par, g, SEQ:SEQ + width(t)], start=True, stop=True)
                last.then_inc(scores_ready, 1)

            def turn_probs(p, u, par):
                a, t = divmod(u, 2)
                pe.wait_ge(probs_ready, 4 * p + u + 1)
                for b in range(GROUPS * (t + 1)):
                    last = pe.transpose(psum[:, 5 + b // 4, b % 4 * P:(b % 4 + 1) * P],
                                        probs[:, a, (3 * t + b) * P:(3 * t + b + 1) * P], T["ident"])
                last.then_inc(probsT_ready, 1)

            def weigh(p, u, par):
                a, t = divmod(u, 2)
                if u == 0:
                    pe.wait_ge(v_copied, 3 * p + 3)
                    if not isinstance(p, int) or p:
                        pe.wait_ge(o_copied, p)
                pe.wait_ge(probsT_copied, 4 * p + u + 1)
                n = GROUPS * (t + 1)
                for b in range(n):
                    g, kt = divmod(b, t + 1)
                    last = pe.matmul(psum[a * HD:(a + 1) * HD, 7, t * P:(t + 1) * P],
                                     v_sb[:, par, g, kt * P + a * HD:kt * P + (a + 1) * HD],
                                     probsT[:, a, (3 * t + b) * P:(3 * t + b + 1) * P],
                                     start=(b == 0), stop=(b == n - 1))
                if u == 3:
                    last.then_inc(o_ready, 1)

            def body(p, par, more):
                qk = lambda g: more and project_qk(p + 1, g, 1 - par, 0)
                vv = lambda g: more and project_v(p + 1, g, 1 - par)
                scores(p, 0, par); scores(p, 1, par); qk(0)
                turn_probs(p, 0, par); scores(p, 2, par); vv(0)
                weigh(p, 0, par); turn_probs(p, 1, par); qk(1)
                scores(p, 3, par); weigh(p, 1, par); vv(1)
                turn_probs(p, 2, par); weigh(p, 2, par); qk(2)
                turn_probs(p, 3, par); weigh(p, 3, par); vv(2)

            pe.wait_ge(turned_used, pe_u.turned)
            for g in range(GROUPS):
                project_qk(0, g, 0, 0)
                project_v(0, g, 0)
            body(0, 0, True)
            body(1, 1, True)
            with pe.Fori(1, PAIRS // 2 - 1) as i:
                body(i * 2, 0, True)
                body(i * 2 + 1, 1, True)
            body(PAIRS - 2, 0, True)
            body(PAIRS - 1, 1, False)
            pe_ring.skip(range(GROUPS), PAIRS)

        def loop_pairs(engine, body):
            body(0, 0, True)
            body(1, 1, True)
            with engine.Fori(1, PAIRS // 2 - 1) as i:
                body(i * 2, 0, True)
                body(i * 2 + 1, 1, True)
            body(PAIRS - 2, 0, True)
            body(PAIRS - 1, 1, False)

        def unit_cols(t):
            return slice(3 * P * t, 3 * P * t + GROUPS * width(t))

        def dve_dilated():
            v = nc.vector

            def take_v(p, g, par):
                v.wait_ge(v_ready, 3 * p + g + 1)
                v.tensor_copy(v_sb[:, par, g, :], psum[:, 1, 0:SEQ]).then_inc(v_copied, 1)

            def biased_max(p, u, par):
                a, t = divmod(u, 2)
                if u == 0:
                    v.wait_ge(bias_full[par], bias_count(p, par))
                v.wait_ge(scores_ready, 4 * p + u + 1)
                v.memset(soft[:, u, 3:4], 0.0)
                if t == 0:
                    src = psum[:, 4, 0:3 * P].rearrange("p (g c) -> p g c", g=GROUPS)
                    bias = bias_sb[:, par, a, :].rearrange("p (g c) -> p g c", g=GROUPS)[:, :, P:SEQ]
                else:
                    src = psum[:, 2:4, :].rearrange("p b c -> p (b c)")[:, 0:3 * SEQ]
                    bias = bias_sb[:, par, a, :]
                dst = probs[:, a, unit_cols(t)]
                if t == 0:
                    dst = dst.rearrange("p (g c) -> p g c", g=GROUPS)
                v.tensor_tensor_reduce(dst, src, bias, 0.125, NEG * 4, ALU.add, ALU.max, soft[:, u, 0:1])
                v.drain()
                v.tensor_scalar(soft[:, u, 1:2], soft[:, u, 0:1], -1.0, None, ALU.mult).then_inc(max_ready, 1)

            def normalise(p, u, par):
                a, t = divmod(u, 2)
                v.wait_ge(exp_ready, 4 * p + u + 1)
                v.reciprocal(soft[:, u, 3:4], soft[:, u, 2:3])
                v.drain()
                v.tensor_scalar(probs[:, a, unit_cols(t)], probs[:, a, unit_cols(t)], soft[:, u, 3:4], None,
                                ALU.mult).then_inc(probs_ready, 1)

            def body(p, par, more):
                vv = lambda g: more and take_v(p + 1, g, 1 - par)
                biased_max(p, 0, par); biased_max(p, 1, par)
                normalise(p, 0, par); normalise(p, 1, par)
                biased_max(p, 2, par); vv(0)
                biased_max(p, 3, par); normalise(p, 2, par); vv(1)
                normalise(p, 3, par)
                v.wait_ge(o_ready, p + 1)
                dst = oT[:, bass.ds(p, 1), :].rearrange("p o (t n) -> p (o t) n", t=TILES)
                v.tensor_copy(dst, psum[:, 7, 0:SEQ].rearrange("p (t n) -> p t n", t=TILES)[:, :, ::-1])\
                 .then_inc(o_copied, 1)
                vv(2)

            for g in range(GROUPS):
                take_v(0, g, 0)
            loop_pairs(v, body)

        def bias_count(p, par):
            if isinstance(p, int):
                return 32 * (p // 2 + 1)
            return p * 16 + (32 if par == 0 else 16)

        def act_dilated():
            act = nc.scalar

            def take_qk(p, g, par):
                act.wait_ge(qk_ready, 3 * p + g + 1)
                act.copy(qk_sb[:, par, g, 0:SEQ].rearrange("p (t n) -> p t n", t=TILES),
                         psum[:, 0, 0:SEQ].rearrange("p (t n) -> p t n", t=TILES)[:, :, ::-1])
                act.copy(qk_sb[:, par, g, SEQ:2 * SEQ], psum[:, 0, SEQ:2 * SEQ]).then_inc(qk_copied, 1)

            def exps(p, u, par):
                a, t = divmod(u, 2)
                act.wait_ge(max_ready, 4 * p + u + 1)
                act.activation(probs[:, a, unit_cols(t)], probs[:, a, unit_cols(t)], ACT.Exp,
                               bias=soft[:, u, 1:2], accum_out=soft[:, u, 2:3]).then_inc(exp_ready, 1)

            def take_probs(p, u, par):
                a, t = divmod(u, 2)
                act.wait_ge(probsT_ready, 4 * p + u + 1)
                src = psum[:, 5:7, :].rearrange("p b c -> p (b c)")[:, 0:GROUPS * width(t)]
                act.copy(probsT[:, a, unit_cols(t)], src).then_inc(probsT_copied, 1)

            def body(p, par, more):
                qk = lambda g: more and take_qk(p + 1, g, 1 - par)
                exps(p, 0, par); exps(p, 1, par); qk(0)
                take_probs(p, 0, par); exps(p, 2, par); take_probs(p, 1, par); qk(1)
                exps(p, 3, par); take_probs(p, 2, par); qk(2); take_probs(p, 3, par)

            for g in range(GROUPS):
                take_qk(0, g, 0)
            loop_pairs(act, body)

        def pool_rows(n, rows=2):
            if n:
                nc.gpsimd.wait_ge(rowv_used, n)
            nc.gpsimd.dma_start(rowv[:, 0:rows, :], d["row_vectors"][2 * n:2 * n + rows].partition_broadcast(P))\
                .then_inc(rowv_full, 16)

        def pool_bias():
            pool = nc.gpsimd
            pool.wait_ge(rel_stored, 16)

            def load(p, par):
                for a in range(2):
                    src = bass.AP(tensor=rel_dram.tensor, offset=p * (2 * GROUPS * 3 * P) + a * GROUPS * 3 * P,
                                  ap=[[1, P], [3 * P, GROUPS], [1, SEQ]])
                    pool.dma_start(bias_sb[:, par, a, :].rearrange("p (g c) -> p g c", g=GROUPS), src)\
                        .then_inc(bias_full[par], 16)

            load(0, 0)
            load(1, 1)
            with pool.Fori(1, PAIRS // 2) as i:
                for par in range(2):
                    pool.wait_ge(max_ready, i * 8 + 4 * (par - 1))
                    load(i * 2 + par, par)

        def pe_sticks():
            pe = nc.tensor
            slots = pe_ring.take(SLOTS)
            pe_ring.skip([s for s, _ in slots], PAIRS // SLOTS - 1)

            def project_qk(p, m, lap, par):
                s, turn = slots[m]
                pe.wait_ge(ring_full[s], lap * 16 + 16 * (turn + 1))
                if not (isinstance(p, int) and p == 0):
                    pe.wait_ge(sb_qk_copied, p)
                for part, src in enumerate((xT, xTr)):
                    for k in range(KC):
                        last = pe.matmul(psum[:, 0, part * SEQ:(part + 1) * SEQ],
                                         ring[:, s, k * 384 + part * P:k * 384 + (part + 1) * P], src[:, k, :],
                                         start=(k == 0), stop=(k == KC - 1))
                last.then_inc(sb_qk_ready, 1)

            def project_v(p, m, par):
                s, _ = slots[m]
                if not (isinstance(p, int) and p == 0):
                    pe.wait_ge(sb_v_copied, p)
                for t in range(TILES):
                    for k in range(KC):
                        last = pe.matmul(psum[:, 1, t * P:(t + 1) * P], xTr[:, k, t * P:(t + 1) * P],
                                         ring[:, s, k * 384 + 2 * P:k * 384 + 3 * P],
                                         start=(k == 0), stop=(k == KC - 1))
                last.then_inc(sb_v_ready, 1)

            def scores(p, a, par):
                if a == 0:
                    pe.wait_ge(sb_qk_copied, p + 1)
                q, k = sb_qk[a * HD:(a + 1) * HD, par, 0:SEQ], sb_qk[a * HD:(a + 1) * HD, par, SEQ:2 * SEQ]
                pe.matmul(psum[:, 2 + a, 0:P], q[:, 0:P], k[:, P:SEQ], start=True, stop=True)
                pe.matmul(psum[:, 2 + a, P:3 * P], q[:, P:SEQ], k, start=True, stop=True).then_inc(sb_scores, 1)

            def turn_att(p, a):
                pe.wait_ge(sb_att, p * 2 + (a + 1))
                for b in range(3):
                    last = pe.transpose(psum[:, 4 + a, b * P:(b + 1) * P], sb_a[:, a, b * P:(b + 1) * P], T["ident"])
                last.then_inc(sb_aT_ready, 1)

            def weigh(p, a, par, m):
                if a == 0:
                    pe.wait_ge(sb_v_copied, p + 1)
                    if not isinstance(p, int) or p:
                        pe.wait_ge(sb_o_copied, p)
                pe.wait_ge(sb_aT_copied, p * 2 + (a + 1))
                for t, blocks in enumerate((((0, 1),), ((1, 0), (2, 1)))):
                    for n, (b, kt) in enumerate(blocks):
                        last = pe.matmul(psum[a * HD:(a + 1) * HD, 7, t * P:(t + 1) * P],
                                         sb_v[:, par, kt * P + a * HD:kt * P + (a + 1) * HD],
                                         sb_aT[:, a, b * P:(b + 1) * P], start=(n == 0), stop=(n == len(blocks) - 1))
                        if a == 0 and t == 0:
                            last.then_inc(ring_free[slots[m][0]], 1)
                if a == 1:
                    last.then_inc(sb_o_ready, 1)

            def body(p, m, lap, more=True):
                par = m % 2
                scores(p, 0, par); scores(p, 1, par)
                if more:
                    project_qk(p + 1, (m + 1) % SLOTS, lap + (m + 1) // SLOTS, 1 - par)
                turn_att(p, 0); weigh(p, 0, par, m); turn_att(p, 1)
                if more:
                    project_v(p + 1, (m + 1) % SLOTS, 1 - par)
                weigh(p, 1, par, m)

            pe.wait_ge(turned_used, pe_u.turned)
            project_qk(0, 0, 0, 0)
            project_v(0, 0, 0)
            for p in range(PAIRS):
                body(p, p % SLOTS, p // SLOTS, p < PAIRS - 1)

        def dve_sticks():
            v = nc.vector

            def take_v(p, par):
                v.wait_ge(sb_v_ready, p + 1)
                v.tensor_copy(sb_v[:, par, :], psum[:, 1, 0:SEQ]).then_inc(sb_v_copied, 1)

            def clip(p, a):
                v.wait_ge(sb_scores, p * 2 + (a + 1))
                z = sb_z[:, a, :]
                v.tensor_scalar(z, psum[:, 2 + a, 0:3 * P], 0.125, SB_CLIP, ALU.mult, ALU.min)
                v.drain()
                v.tensor_scalar(z, z, -SB_CLIP, None, ALU.max)
                v.drain()
                v.scalar_tensor_tensor(out=sb_a[:, a, :], in0=z, scalar=-1.0, in1=z, op0=ALU.mult, op1=ALU.min)\
                 .then_inc(sb_clipped, 1)

            mask = T["sb_mask"].unsqueeze(1).broadcast_to([P, 2, P])

            def own(buf, a):
                return buf[:, a, 0:2 * P].rearrange("p (b c) -> p b c", b=2)

            def suffix(p, a):
                v.wait_ge(sb_exp1, p * 2 + (a + 1))
                v.scalar_tensor_tensor(out=sb_p[:, a, :], in0=sb_z[:, a, :], scalar=0.0, in1=sb_a[:, a, :],
                                       op0=ALU.max, op1=ALU.add)
                v.drain()
                v.tensor_tensor(own(sb_p, a), own(sb_p, a), mask, ALU.mult)
                v.drain()
                v.tensor_tensor_scan(sb_r[:, a, 0:P], T["ones"][:, 0:P], sb_p[:, a, 0:P], 0.0, ALU.mult, ALU.add)
                v.tensor_tensor_scan(sb_r[:, a, P:3 * P], T["ones"], sb_p[:, a, P:3 * P], 0.0, ALU.mult, ALU.add)
                v.drain()
                v.tensor_tensor(sb_p[:, a, :], sb_z[:, a, :], sb_r[:, a, :], ALU.subtract).then_inc(sb_minus, 1)

            def strict(p, a):
                v.wait_ge(sb_exp2, p * 2 + (a + 1))
                v.tensor_tensor(own(sb_a, a), own(sb_a, a), mask, ALU.mult).then_inc(sb_att, 1)

            take_v(0, 0)
            for p in range(PAIRS):
                par = p % 2
                clip(p, 0); clip(p, 1); suffix(p, 0); suffix(p, 1); strict(p, 0); strict(p, 1)
                if p < PAIRS - 1:
                    take_v(p + 1, 1 - par)
                v.wait_ge(sb_o_ready, p + 1)
                v.tensor_copy(oT[:, p, :], psum[:, 7, 0:SEQ]).then_inc(sb_o_copied, 1)

        def act_sticks():
            act = nc.scalar

            def take_qk(p, par):
                act.wait_ge(sb_qk_ready, p + 1)
                act.copy(sb_qk[:, par, :], psum[:, 0, :]).then_inc(sb_qk_copied, 1)

            take_qk(0, 0)
            for p in range(PAIRS):
                for a in range(2):
                    act.wait_ge(sb_clipped, p * 2 + (a + 1))
                    act.activation(sb_a[:, a, :], sb_a[:, a, :], ACT.Exp)
                    act.drain()
                    act.activation(sb_a[:, a, :], sb_a[:, a, :], ACT.Ln, bias=eps["one"]).then_inc(sb_exp1, 1)
                for a in range(2):
                    act.wait_ge(sb_minus, p * 2 + (a + 1))
                    act.activation(sb_a[:, a, :], sb_p[:, a, :], ACT.Exp).then_inc(sb_exp2, 1)
                if p < PAIRS - 1:
                    take_qk(p + 1, 1 - p % 2)
                for a in range(2):
                    act.wait_ge(sb_aT_ready, p * 2 + (a + 1))
                    act.copy(sb_aT[:, a, :], psum[:, 4 + a, 0:3 * P]).then_inc(sb_aT_copied, 1)

        uT = carve(0, 28, SEQ)
        rope = carve(20736, 4, SEQ)
        B0 = 28 * SEQ
        pos_i = scratch[:, B0:B0 + SEQ].bitcast(I32)
        pos_f, ang, turns_n = carve(B0 + 256, SEQ), carve(B0 + 512, 4, SEQ), carve(B0 + 1536, 4, SEQ)
        cv_u, cv_y, cv_t = carve(B0, 2, SEQ), carve(B0 + 512, 2, SEQ), carve(B0 + 1024, 2, SEQ)
        rt_r = carve(B0 + 1536, 4, SEQ)
        rt_t = carve(B0 + 2560, 4, SEQ)
        rt_v = carve(B0 + 3584, TILES, SEQ)
        rt_s = carve(B0 + 4096, MIX_HEADS, TILES, SEQ)
        rt_sq, rt_d, rt_g = carve(B0 + 6144, 2, SEQ), carve(B0 + 6656, 2, SEQ), carve(B0 + 7168, 2, SEQ)
        M0 = B0 + 7680
        ml_n = carve(M0, 4, SEQ)
        ml_d = carve(M0 + 1024, 2, SEQ)
        ml_q, ml_k = carve(M0 + 1536, MIX_HEADS, SEQ), carve(M0 + 2560, MIX_HEADS, SEQ)
        ml_t = carve(B0 + 2560, MIX_HEADS, SEQ)
        ml_kr = carve(B0, 2, SEQ)
        ml_v = carve(M0 + 3584, TILES, SEQ)
        ml_p = carve(B0 + 4096, MIX_HEADS, TILES, SEQ)
        ml_pT = carve(B0 + 1536, MIX_HEADS, TILES, SEQ)
        ml_m = carve(B0 + 3584, 4, 8)
        rw_mb = carve(B0, 16, 4 * P)
        rw_AR = carve(B0 + 8192, 4, TILES, 2, P)
        rw_B, rw_K = carve(B0 + 10240, 4, SEQ), carve(B0 + 11264, 4, SEQ)
        rw_g = carve(B0 + 12288, 2, SEQ)
        rw_y = carve(B0 + 12800, 2, SEQ)
        rw_T, rw_TT = carve(0, 16, P), carve(2048, 16, P)
        rw_Y = xT[:].rearrange("p k n -> p (k n)").rearrange("p (i n) -> p i n", i=16)
        rw_BK = xT[:].rearrange("p k n -> p (k n)").rearrange("p (d t w n) -> p d t w n", d=4, t=TILES, w=2)
        rowf = rowv[:].rearrange("p k n -> p (k n)")
        rw_v = rowf[:, 0:512].rearrange("p (t n) -> p t n", t=TILES)
        rw_kk = rowf[:, 512:1024].rearrange("p (c n) -> p c n", c=2)
        rw_S = rowf[:, 1024:1536].rearrange("p (d n) -> p d n", d=4)
        rw_G = rowf[:, 1536:2048].rearrange("p (d n) -> p d n", d=4)
        rw_ks = uT[:, 16:18, :]
        rw_U = uT[:, U_WD:U_WD + 2, :].rearrange("p c n -> p (c n)").rearrange("p (d n) -> p d n", d=4)
        rw_Sc = carve(18 * SEQ, 4, HD)
        rw_PC = place("rw_PC", plan["PC"], [P, 4, 4])[:]
        rw_om = place("rw_om", plan["om"], [P, 2])[:]
        pr_lw, pr_a = carve(B0, 4, SEQ), carve(B0 + 1024, 4, SEQ)
        pr_L, pr_E1 = carve(B0 + 2048, 4, SEQ), carve(B0 + 3072, 4, SEQ)
        pr_E2, pr_E3 = carve(B0 + 4096, 4, SEQ), carve(B0 + 5120, 4, SEQ)
        pr_kd, pr_t = carve(B0 + 6144, 4, SEQ), carve(B0 + 7168, 4, SEQ)

        pos_loaded, ang_ready, rope_ready = sem("pos_loaded"), sem("ang_ready"), sem("rope_ready")
        small_loaded, small_used = sem("small_loaded"), sem("small_used")
        u_ready, u_copied_v, u_copied_a = sem("u_ready"), sem("u_copied_v"), sem("u_copied_a")
        rt_turned, rt_vT, rt_v_copied, rt_roped = sem("rt_turned"), sem("rt_vT"), sem("rt_v_copied"), sem("rt_roped")
        rt_scores, rt_decayed, rt_o, rt_squared = sem("rt_scores"), sem("rt_decayed"), sem("rt_o"), sem("rt_squared")
        rt_summed, rt_dev, rt_done = sem("rt_summed"), sem("rt_dev"), sem("rt_done")
        ml_squared, ml_summed, ml_dev, ml_normed = sem("ml_squared"), sem("ml_summed"), sem("ml_dev"), sem("ml_normed")
        ml_qkv, ml_q_copied, ml_kv_copied = sem("ml_qkv"), sem("ml_q_copied"), sem("ml_kv_copied")
        ml_turned, ml_roped, ml_scores = sem("ml_turned"), sem("ml_roped"), sem("ml_scores")
        ml_max, ml_exp, ml_probs, ml_pT_ready = sem("ml_max"), sem("ml_exp"), sem("ml_probs"), sem("ml_pT_ready")
        ml_pT_copied, ml_o, ml_done = sem("ml_pT_copied"), sem("ml_o"), sem("ml_done")
        rw_act, rw_pre, rw_sig, rw_kraw = sem("rw_act"), sem("rw_pre"), sem("rw_sig"), sem("rw_kraw")
        rw_ksq, rw_knorm, rw_kdev = sem("rw_ksq"), sem("rw_knorm"), sem("rw_kdev")
        rw_L, rw_exps, rw_prep = sem("rw_L"), sem("rw_exps"), sem("rw_prep")
        rw_mats, rw_masked, rw_N, rw_T0 = sem("rw_mats"), sem("rw_masked"), sem("rw_N"), sem("rw_T0")
        rw_Yr, rw_Yc, rw_Z, rw_ZT, rw_Tn = sem("rw_Yr"), sem("rw_Yc"), sem("rw_Z"), sem("rw_ZT"), sem("rw_Tn")
        rw_BKr, rw_BKc = sem("rw_BKr"), sem("rw_BKc")
        rw_Gr, rw_Gc_v, rw_Gc_a = sem("rw_Gr"), sem("rw_Gc_v"), sem("rw_Gc_a")
        rw_Ur, rw_Uc_v, rw_Uc_a = sem("rw_Ur"), sem("rw_Uc_v"), sem("rw_Uc_a")
        rw_yr, rw_Sr, rw_Sn = sem("rw_yr"), sem("rw_Sr"), sem("rw_Sn")
        rw_sum, rw_cent, rw_csq, rw_css, rw_cdev = sem("rw_sum"), sem("rw_cent"), sem("rw_csq"), sem("rw_css"), sem("rw_cdev")
        rw_done, rw_T0s = sem("rw_done"), sem("rw_T0s")
        final_ready = sem("final_ready")

        def both(buf):
            return buf.unsqueeze(1)

        def col(l, c, n=1):
            return vec[:, l, c:c + n]

        TWO_PI = 2 * np.pi
        C1 = 6.28125
        C2 = float(np.floor((TWO_PI - C1) * 2 ** 21) / 2 ** 21)
        C3 = float(TWO_PI - C1 - C2)
        ROUND = 1.5 * 2 ** 23

        def dve_rope_tables():
            v = nc.vector
            v.wait_ge(pos_loaded, 16)
            v.tensor_copy(pos_f, pos_i)
            v.drain()
            for m in range(2):
                for w in range(2):
                    v.tensor_scalar(ang[:, 2 * m + w, :], pos_f, T["inv"][:, m:m + 1], None, ALU.mult)
            v.drain()
            for w in range(2):
                v.tensor_scalar(turns_n[:, w::2, :], ang[:, w::2, :], float(1 / TWO_PI), (0.25, 0.0)[w],
                                ALU.mult, ALU.add)
            v.drain()
            v.tensor_scalar(turns_n, turns_n, ROUND, -ROUND, ALU.add, ALU.add)
            for c in (C1, C2, C3):
                v.drain()
                v.scalar_tensor_tensor(out=ang, in0=turns_n, scalar=-c, in1=ang, op0=ALU.mult, op1=ALU.add)
            v.drain()
            for w in range(2):
                v.tensor_scalar(turns_n[:, w::2, :], ang[:, w::2, :], (float(np.pi / 2), 0.0)[w], 3.1415925,
                                ALU.add, ALU.min)
            v.drain()
            v.tensor_scalar(ang, turns_n, -3.1415925, None, ALU.max).then_inc(ang_ready, 1)

        def act_rope_tables():
            nc.scalar.wait_ge(ang_ready, 1)
            nc.scalar.activation(rope, ang, ACT.Sin).then_inc(rope_ready, 1)
            nc.scalar.drain()

        def pe_inputs(l):
            pe = nc.tensor

            def body(i, units, first, slots):
                for u in range(units):
                    s, turn = slots[u]
                    pe.wait_ge(ring_full[s], 16 * i + 16 * (turn + 1))
                    for c in range(3):
                        m = 3 * u + c
                        if first + m >= 28:
                            continue
                        if m >= 4:
                            pe.wait_ge((u_copied_v, u_copied_a)[m % 2], 6 * i + 14 * l + (first + m - 4) // 2 + 1)
                        for k in range(KC):
                            last = pe.matmul(psum[:, m % 4, 0:SEQ], ring[:, s, k * 384 + c * P:k * 384 + (c + 1) * P],
                                             xT[:, k, :], start=(k == 0), stop=(k == KC - 1))
                        last.then_inc(u_ready, 1)
                n = min(3 * units, 28 - first)
                pe.wait_ge(u_copied_v, 6 * i + 14 * l + (first + n) // 2)
                pe.wait_ge(u_copied_a, 6 * i + 14 * l + (first + n) // 2)
                for u in range(units):
                    pe.matmul(psum[0:1, 0, 0:1], xT[:, 0, 0:1], xT[:, 0, 0:1], start=True, stop=True)\
                      .then_inc(ring_free[slots[u][0]], 1)

            slots = pe_ring.take(SLOTS)
            with pe.Fori(0, 2) as i:
                body(i, SLOTS, 0, slots)
            pe_ring.skip([s for s, _ in slots], 1)
            body(0, 2, 24, pe_ring.take(2))

        def take_inputs(engine, copy, odd, copied, l):
            def body(i, n, first):
                for m in range(odd, n, 2):
                    engine.wait_ge(u_ready, 12 * i + 28 * l + first + m + 1)
                    dst = uT[:, first + m, :] if isinstance(i, int) else \
                        uT[:, bass.ds(i * 12 + m, 1), :].rearrange("p o n -> p (o n)")
                    copy(dst, psum[:, m % 4, 0:SEQ]).then_inc(copied, 1)
            with engine.Fori(0, 2) as i:
                body(i, 12, 0)
            body(0, 4, 24)

        def dve_conv(l):
            v = nc.vector
            v.wait_ge(rope_ready, 1)
            v.wait_ge(u_copied_a, 14 * (l + 1))
            v.drain()
            v.tensor_tensor(cv_u, uT[:, U_CC:U_CC + 2, :], uT[:, U_CX:U_CX + 2, :], ALU.mult)
            v.drain()
            tap = lambda k, c: col(l, V_CONV + 2 * k + c)
            for c in range(2):
                v.tensor_scalar(cv_y[:, c, :], cv_u[:, c, :], tap(1, c), None, ALU.mult)
            v.drain()
            for c in range(2):
                v.scalar_tensor_tensor(out=cv_y[:, c, 1:], in0=cv_u[:, c, 0:SEQ - 1], scalar=tap(0, c),
                                       in1=cv_y[:, c, 1:], op0=ALU.mult, op1=ALU.add)
            v.drain()
            for c in range(2):
                v.scalar_tensor_tensor(out=cv_y[:, c, 0:SEQ - 1], in0=cv_u[:, c, 1:], scalar=tap(2, c),
                                       in1=cv_y[:, c, 0:SEQ - 1], op0=ALU.mult, op1=ALU.add)
            v.drain()
            v.tensor_tensor(oT[:, 0:2, :], cv_y, uT[:, U_CB:U_CB + 2, :], ALU.mult)

        def pe_retention(l):
            pe = nc.tensor
            for n in range(4):
                last = pe.matmul(psum[:, n // 2, n % 2 * SEQ:(n % 2 + 1) * SEQ], T["turn_ret"], uT[:, U_RQ + n, :],
                                 start=True, stop=True)
            last.then_inc(rt_turned, 1)
            for c in range(2):
                for t in range(TILES):
                    last = pe.transpose(psum[:, 2, t * SEQ + c * P:t * SEQ + (c + 1) * P],
                                        uT[:, U_RV + c, t * P:(t + 1) * P], T["ident"])
            last.then_inc(rt_vT, 1)
            pe.wait_ge(rt_roped, l + 1)
            for h in range(MIX_HEADS):
                c, a = divmod(h, 2)
                rows = slice(a * HD, (a + 1) * HD)
                for kt in range(TILES):
                    last = pe.matmul(psum[:, 4 + h, kt * SEQ:(kt + 1) * SEQ], rt_r[rows, 2 + c, kt * P:(kt + 1) * P],
                                     rt_r[rows, c, :], start=True, stop=True)
                last.then_inc(rt_scores, 1)
            pe.wait_ge(rt_v_copied, l + 1)
            for h in range(MIX_HEADS):
                c, a = divmod(h, 2)
                pe.wait_ge(rt_decayed, MIX_HEADS * l + h + 1)
                for kt in range(TILES):
                    last = pe.matmul(psum[a * HD:(a + 1) * HD, c, 0:SEQ], rt_v[:, kt, h * HD:(h + 1) * HD],
                                     rt_s[:, h, kt, :], start=(kt == 0), stop=(kt == TILES - 1))
            last.then_inc(rt_o, 1)
            pe.wait_ge(rt_squared, l + 1)
            pe.matmul(psum[:, 2, :], T["ones_head"], rt_sq.rearrange("p c n -> p (c n)"), start=True, stop=True)\
              .then_inc(rt_summed, 1)

        def dve_retention(l):
            v = nc.vector
            cos, sin = both(rope[:, 0, :]), both(rope[:, 1, :])
            v.tensor_tensor(rt_r, uT[:, U_RQ:U_RQ + 4, :], cos.broadcast_to([P, 4, SEQ]), ALU.mult)
            v.wait_ge(rt_turned, l + 1)
            v.tensor_tensor(rt_t, psum[:, 0:2, :].rearrange("p b (c n) -> p (b c) n", c=2),
                            sin.broadcast_to([P, 4, SEQ]), ALU.mult)
            v.drain()
            v.tensor_tensor(rt_r, rt_r, rt_t, ALU.add).then_inc(rt_roped, 1)
            for h in range(MIX_HEADS):
                v.wait_ge(rt_scores, MIX_HEADS * l + h + 1)
                for kt in range(TILES):
                    at = h * 3 * P + (1 - kt) * P
                    last = v.tensor_tensor(rt_s[:, h, kt, :], psum[:, 4 + h, kt * SEQ:(kt + 1) * SEQ],
                                           T["decay"][:, at:at + SEQ], ALU.mult)
                last.then_inc(rt_decayed, 1)
            v.wait_ge(rt_dev, l + 1)
            v.reciprocal(rt_d, rt_d)
            v.drain()
            for c in range(2):
                v.scalar_tensor_tensor(out=rt_sq[:, c, :], in0=psum[:, c, 0:SEQ], scalar=col(l, V_GN + c),
                                       in1=rt_d[:, c, :], op0=ALU.mult, op1=ALU.mult)
            v.drain()
            v.tensor_tensor(oT[:, 4:6, :], rt_sq, rt_g, ALU.mult).then_inc(rt_done, 1)

        def act_retention(l):
            act = nc.scalar
            act.wait_ge(u_copied_v, 14 * (l + 1))
            act.drain()
            act.activation(rt_g, uT[:, U_RG:U_RG + 2, :], ACT.Silu)
            act.wait_ge(rt_vT, l + 1)
            act.copy(rt_v.rearrange("p t n -> p (t n)"), psum[:, 2, :]).then_inc(rt_v_copied, 1)
            act.wait_ge(rt_o, l + 1)
            act.activation(rt_sq, psum[:, 0:2, 0:SEQ], ACT.Square).then_inc(rt_squared, 1)
            act.wait_ge(rt_summed, l + 1)
            act.activation(rt_d, psum[:, 2, :].rearrange("p (c n) -> p c n", c=2), ACT.Sqrt, bias=eps["rms"],
                           scale=1.0 / HD).then_inc(rt_dev, 1)

        ML_SCALE = 96 ** -0.5
        RR = slice(64, 96)

        def pe_latent(l):
            pe = nc.tensor
            pe.wait_ge(ml_squared, l + 1)
            for k in range(3):
                pe.matmul(psum[:, 3, 0:SEQ], T["ones"][:, 0:P], ml_n[:, k, :], start=(k == 0), stop=(k == 2))
            pe.matmul(psum[:, 3, SEQ:2 * SEQ], T["ones"][:, 0:P], ml_n[:, 3, :], start=True, stop=True)\
              .then_inc(ml_summed, 1)
            pe.wait_ge(rt_done, l + 1)
            pe.wait_ge(small_loaded, 16 * (l + 1))
            pe.matmul(psum[:, 1, 0:SEQ], T["turn_mla"], uT[:, U_KR, :], start=True, stop=True)
            pe.wait_ge(ml_normed, l + 1)
            for h in range(MIX_HEADS):
                dst = slice(h % 2 * SEQ, (h % 2 + 1) * SEQ)
                for k in range(3):
                    pe.matmul(psum[:, 4 + h // 2, dst], small[:, W_QB + k * 512 + h * P:W_QB + k * 512 + (h + 1) * P],
                              ml_n[:, k, :], start=(k == 0), stop=(k == 2))
                pe.matmul(psum[0:HD, 6 + h // 2, dst], small[:, W_KB + h * HD:W_KB + (h + 1) * HD], ml_n[:, 3, :],
                          start=True, stop=True)
            for t in range(TILES):
                last = pe.matmul(psum[:, 0, t * SEQ:(t + 1) * SEQ], ml_n[:, 3, t * P:(t + 1) * P],
                                 small[:, W_VB:W_VB + SEQ], start=True, stop=True)
            last.then_inc(ml_qkv, 1)
            pe.wait_ge(ml_q_copied, l + 1)
            for h in range(MIX_HEADS):
                last = pe.matmul(psum[:, 2 + h // 2, h % 2 * SEQ:(h % 2 + 1) * SEQ], T["turn_mla"], ml_q[:, h, :],
                                 start=True, stop=True)
            last.then_inc(ml_turned, 1)
            pe.wait_ge(ml_roped, l + 1)
            for h in range(MIX_HEADS):
                for t in range(TILES):
                    last = pe.matmul(psum[:, 4 + h, t * SEQ:(t + 1) * SEQ], ml_q[0:96, h, t * P:(t + 1) * P],
                                     ml_k[0:96, h, :], start=True, stop=True)
                last.then_inc(ml_scores, 1)
            for h in range(MIX_HEADS):
                pe.wait_ge(ml_probs, MIX_HEADS * l + h + 1)
                for t in range(TILES):
                    for kt in range(TILES):
                        last = pe.transpose(psum[:, h, (2 * kt + t) * P:(2 * kt + t + 1) * P],
                                            ml_p[:, h, t, kt * P:(kt + 1) * P], T["ident"])
                last.then_inc(ml_pT_ready, 1)
            for h in range(MIX_HEADS):
                c, a = divmod(h, 2)
                pe.wait_ge(ml_pT_copied, MIX_HEADS * l + h + 1)
                for kt in range(TILES):
                    last = pe.matmul(psum[a * HD:(a + 1) * HD, 4 + c, 0:SEQ], ml_v[:, kt, h * HD:(h + 1) * HD],
                                     ml_pT[:, h, kt, :], start=(kt == 0), stop=(kt == TILES - 1))
            last.then_inc(ml_o, 1)

        def act_latent(l):
            act = nc.scalar
            act.activation(ml_n, uT[:, U_QA:U_QA + 4, :], ACT.Square).then_inc(ml_squared, 1)
            act.wait_ge(ml_summed, l + 1)
            act.activation(ml_d[:, 0, :], psum[:, 3, 0:SEQ], ACT.Sqrt, bias=eps["rms"], scale=1.0 / 384)
            act.activation(ml_d[:, 1, :], psum[:, 3, SEQ:2 * SEQ], ACT.Sqrt, bias=eps["rms"], scale=1.0 / P)\
               .then_inc(ml_dev, 1)
            act.wait_ge(ml_qkv, l + 1)
            act.copy(ml_q, psum[:, 4:6, :].rearrange("p b (h n) -> p (b h) n", h=2)).then_inc(ml_q_copied, 1)
            for h in range(MIX_HEADS):
                act.wait_ge(ml_max, MIX_HEADS * l + h + 1)
                for t in range(TILES):
                    i = 2 * h + t
                    last = act.activation(ml_p[:, h, t, :], psum[:, 4 + h, t * SEQ:(t + 1) * SEQ], ACT.Exp,
                                          bias=ml_m[:, 1, i:i + 1], scale=ML_SCALE, accum_out=ml_m[:, 2, i:i + 1])
                last.then_inc(ml_exp, 1)
            for h in range(MIX_HEADS):
                act.wait_ge(ml_pT_ready, MIX_HEADS * l + h + 1)
                act.copy(ml_pT[:, h, :, :].rearrange("p k n -> p (k n)"), psum[:, h, :]).then_inc(ml_pT_copied, 1)

        def dve_latent(l):
            v = nc.vector
            v.wait_ge(ml_dev, l + 1)
            v.reciprocal(ml_d, ml_d)
            v.drain()
            for k in range(4):
                last = v.scalar_tensor_tensor(out=ml_n[:, k, :], in0=uT[:, U_QA + k, :], scalar=col(l, V_QN + k),
                                              in1=ml_d[:, k // 3, :], op0=ALU.mult, op1=ALU.mult)
            last.then_inc(ml_normed, 1)
            cos, sin = both(rope[RR, 2, :]), both(rope[RR, 3, :])
            v.wait_ge(ml_qkv, l + 1)
            v.tensor_copy(ml_k[0:HD], psum[0:HD, 6:8, :].rearrange("p b (h n) -> p (b h) n", h=2))
            v.tensor_copy(ml_v.rearrange("p t n -> p (t n)"), psum[:, 0, :])
            v.tensor_tensor(ml_kr[RR, 0, :], uT[RR, U_KR, :], rope[RR, 2, :], ALU.mult)
            v.tensor_tensor(ml_kr[RR, 1, :], psum[RR, 1, 0:SEQ], rope[RR, 3, :], ALU.mult)
            v.drain()
            v.tensor_tensor(ml_k[RR], both(ml_kr[RR, 0, :]).broadcast_to([32, 4, SEQ]),
                            both(ml_kr[RR, 1, :]).broadcast_to([32, 4, SEQ]), ALU.add)
            v.wait_ge(ml_turned, l + 1)
            v.tensor_tensor(ml_t[RR], psum[RR, 2:4, :].rearrange("p b (h n) -> p (b h) n", h=2),
                            sin.broadcast_to([32, 4, SEQ]), ALU.mult)
            v.tensor_tensor(ml_q[RR], ml_q[RR], cos.broadcast_to([32, 4, SEQ]), ALU.mult)
            v.drain()
            v.tensor_tensor(ml_q[RR], ml_q[RR], ml_t[RR], ALU.add).then_inc(ml_roped, 1)
            for h in range(MIX_HEADS):
                v.wait_ge(ml_scores, MIX_HEADS * l + h + 1)
                v.tensor_reduce(ml_m[:, 0, 2 * h:2 * h + 2], psum[:, 4 + h, :].rearrange("p (t n) -> p t n", t=2),
                                AX_X, ALU.max)
                v.drain()
                v.tensor_scalar(ml_m[:, 1, 2 * h:2 * h + 2], ml_m[:, 0, 2 * h:2 * h + 2], -ML_SCALE, None, ALU.mult)\
                 .then_inc(ml_max, 1)
            for h in range(MIX_HEADS):
                v.wait_ge(ml_exp, MIX_HEADS * l + h + 1)
                v.reciprocal(ml_m[:, 3, 2 * h:2 * h + 2], ml_m[:, 2, 2 * h:2 * h + 2])
                v.drain()
                for t in range(TILES):
                    last = v.tensor_scalar(ml_p[:, h, t, :], ml_p[:, h, t, :], ml_m[:, 3, 2 * h + t:2 * h + t + 1],
                                           None, ALU.mult)
                last.then_inc(ml_probs, 1)
            v.wait_ge(ml_o, l + 1)
            v.tensor_copy(oT[:, 6:8, :], psum[:, 4:6, 0:SEQ]).then_inc(ml_done, 1)

        def cell(s):
            return [(d, c4, c4 // 2, c4 % 2) for d, c4 in ((0, s), (1, 3 - s))]

        def index(a, dp, t):
            return 8 * a + 2 * dp + t

        def pe_rwkv(l):
            pe = nc.tensor
            pe.wait_ge(rw_act, l + 1)
            for dd in range(2):
                rows = slice(dd * HD, (dd + 1) * HD)
                for c in range(2):
                    dst = slice(c * SEQ, (c + 1) * SEQ)
                    pe.matmul(psum[:, dd, dst], small[rows, W_W2 + c * P:W_W2 + (c + 1) * P], uT[rows, U_WD, :],
                              start=True, stop=True)
                    pe.matmul(psum[:, 2 + dd, dst], small[rows, W_A2 + c * P:W_A2 + (c + 1) * P], uT[rows, U_AD, :],
                              start=True, stop=True)
            pe.wait_ge(ml_done, l + 1)
            for c in range(2):
                last = pe.matmul(psum[:, 4, c * SEQ:(c + 1) * SEQ], small[:, W_G2 + c * P:W_G2 + (c + 1) * P],
                                 uT[:, U_GD, :], start=True, stop=True)
            last.then_inc(rw_pre, 1)
            pe.wait_ge(rw_ksq, l + 1)
            pe.matmul(psum[:, 5, :], T["ones_head"], pr_t[:, 0:2, :].rearrange("p c n -> p (c n)"),
                      start=True, stop=True).then_inc(rw_knorm, 1)
            for c in range(2):
                for t in range(TILES):
                    last = pe.transpose(psum[:, 6, t * SEQ + c * P:t * SEQ + (c + 1) * P],
                                        uT[:, U_V + c, t * P:(t + 1) * P], T["ident"])
            pe.wait_ge(rw_prep, l + 1)
            for g in range(4):
                a, dd = divmod(g, 2)
                rows = slice(a * HD, (a + 1) * HD)
                for j in range(4):
                    dp, t = 2 * dd + j // 2, j % 2
                    last = pe.matmul(psum[:, g, j * P:(j + 1) * P], rw_AR[rows, dp, t, 0, :],
                                     rw_B[rows, dp, t * P:(t + 1) * P], start=True, stop=True)
                last.then_inc(rw_N, 1)
            pe.wait_ge(rw_T0, 4 * l + 4)
            for i in range(16):
                a, dp, t = i // 8, i % 8 // 2, i % 2
                rows = slice(a * HD, (a + 1) * HD)
                if i >= 4:
                    pe.wait_ge(rw_masked, 16 * l + i - 3)
                for n, src in enumerate((rw_B, rw_K)):
                    last = pe.matmul(psum[:, i % 4, n * SEQ:(n + 1) * SEQ], src[rows, dp, t * P:(t + 1) * P],
                                     rw_AR[rows, dp, t, :, :].rearrange("p w n -> p (w n)"), start=True, stop=True)
                last.then_inc(rw_mats, 1)
            for lv in range(1, 6):
                for g in range(4):
                    if g == 0 and lv == 1:
                        pe.wait_ge(rw_T0s, l + 1)
                    if lv > 1:
                        pe.wait_ge(rw_Tn, 20 * l + 4 * (lv - 2) + g + 1)
                    for j in range(4):
                        i = 4 * g + j
                        last = pe.matmul(psum[:, g, j * P:(j + 1) * P], rw_mb[:, i, 0:P], rw_T[:, i, :],
                                         start=True, stop=True)
                    last.then_inc(rw_Yr, 1)
                for g in range(4):
                    pe.wait_ge(rw_Yc, 20 * l + 4 * (lv - 1) + g + 1)
                    for j in range(4 if lv < 5 else 0):
                        i = 4 * g + j
                        last = pe.matmul(psum[:, 4 + g, j * P:(j + 1) * P], rw_TT[:, i, :], rw_Y[:, i, :],
                                         start=True, stop=True)
                    for j in range(4):
                        i = 4 * g + j
                        last = pe.matmul(psum[:, g, j * P:(j + 1) * P], rw_Y[:, i, :], rw_TT[:, i, :],
                                         start=True, stop=True)
                    last.then_inc(rw_ZT, 1)
            pe.wait_ge(rw_Tn, 20 * (l + 1))
            for dp in range(4):
                for t in range(TILES):
                    for w, src in enumerate((rw_B, rw_K)):
                        n = 4 * dp + 2 * t + w
                        last = pe.transpose(psum[:, 4 + n // 4, n % 4 * P:(n % 4 + 1) * P],
                                            src[:, dp, t * P:(t + 1) * P], T["ident"])
            last.then_inc(rw_BKr, 1)
            for s in range(4):
                if s == 0:
                    pe.wait_ge(rw_BKc, l + 1)
                else:
                    pe.wait_ge(rw_Sn, 4 * l + s)
                for dd, c4, t, o in cell(s):
                    tok = slice(o * HD, (o + 1) * HD)
                    for c in range(2):
                        dp = 2 * dd + c
                        for a in range(2):
                            i, hv = index(a, dp, t), slice(a * HD, (a + 1) * HD)
                            dst = psum[tok, 0, dp * P + a * HD:dp * P + (a + 1) * HD]
                            pe.matmul(dst, rw_AR[:, dp, t, 0, tok], rw_S[:, dp, hv], start=True, stop=False)
                            last = pe.matmul(dst, rw_mb[:, i, 2 * P + o * HD:2 * P + (o + 1) * HD],
                                             rw_v[:, t, c * P + a * HD:c * P + (a + 1) * HD], start=False, stop=True)
                last.then_inc(rw_Gr, 1)
                pe.wait_ge(rw_Gc_v, 4 * l + s + 1)
                pe.wait_ge(rw_Gc_a, 4 * l + s + 1)
                for dd, c4, t, o in cell(s):
                    tok = slice(o * HD, (o + 1) * HD)
                    for c in range(2):
                        dp = 2 * dd + c
                        for a in range(2):
                            i, hv = index(a, dp, t), slice(a * HD, (a + 1) * HD)
                            last = pe.matmul(psum[tok, 1, dp * P + a * HD:dp * P + (a + 1) * HD],
                                             rw_TT[:, i, tok], rw_G[:, dp, hv], start=True, stop=True)
                last.then_inc(rw_Ur, 1)
                pe.wait_ge(rw_Uc_v, 4 * l + s + 1)
                pe.wait_ge(rw_Uc_a, 4 * l + s + 1)
                if s < 3:
                    for dd, c4, t, o in cell(s):
                        tok = slice(o * HD, (o + 1) * HD)
                        for c in range(2):
                            dp = 2 * dd + c
                            for a in range(2):
                                hv = slice(a * HD, (a + 1) * HD)
                                dst = psum[hv, 3 + dd, c * HD:(c + 1) * HD]
                                pe.matmul(dst, rw_BK[tok, dp, t, 0, hv], rw_U[tok, dp, hv], start=True, stop=False)
                                last = pe.matmul(dst, rw_BK[tok, dp, t, 1, hv],
                                                 rw_v[tok, t, c * P + a * HD:c * P + (a + 1) * HD],
                                                 start=False, stop=True)
                    last.then_inc(rw_Sr, 1)
                for dd, c4, t, o in cell(s):
                    tok = slice(o * HD, (o + 1) * HD)
                    for c in range(2):
                        dp = 2 * dd + c
                        for a in range(2):
                            i, hv = index(a, dp, t), slice(a * HD, (a + 1) * HD)
                            dst = psum[hv, 2, dp * HD:(dp + 1) * HD]
                            pe.matmul(dst, rw_S[:, dp, hv], rw_AR[:, dp, t, 1, tok], start=True, stop=False)
                            pe.matmul(dst, rw_U[:, dp, hv], rw_mb[:, i, P + o * HD:P + (o + 1) * HD],
                                      start=False, stop=False)
                            last = pe.matmul(dst, rw_v[:, t, c * P + a * HD:c * P + (a + 1) * HD],
                                             rw_mb[:, i, 3 * P + o * HD:3 * P + (o + 1) * HD], start=False, stop=True)
                last.then_inc(rw_yr, 1)
            pe.wait_ge(rw_sum, l + 1)
            pe.matmul(psum[:, 5, :], T["ones_head"], rw_y.rearrange("p c n -> p (c n)"), start=True, stop=True)
            pe.matmul(psum[:, 6, :], T["ones_head"], rw_ks.rearrange("p c n -> p (c n)"), start=True, stop=True)\
              .then_inc(rw_css, 1)
            pe.wait_ge(rw_csq, l + 1)
            pe.matmul(psum[:, 7, :], T["ones_head"], pr_t2.rearrange("p c n -> p (c n)"), start=True, stop=True)\
              .then_inc(rw_css, 1)

        pr_t2 = rw_G.rearrange("p d n -> p (d n)").rearrange("p (c n) -> p c n", c=2)

        def act_rwkv(l):
            act = nc.scalar
            act.activation(uT[:, U_WD, :], uT[:, U_WD, :], ACT.Tanh)
            act.activation(uT[:, U_GD, :], uT[:, U_GD, :], ACT.Sigmoid).then_inc(rw_act, 1)
            act.wait_ge(rw_pre, l + 1)
            act.wait_ge(ml_done, l + 1)
            for dd in range(2):
                for c in range(2):
                    dp, src = 2 * dd + c, slice(c * SEQ, (c + 1) * SEQ)
                    act.activation(pr_lw[:, dp, :], psum[:, dd, src], ACT.Sigmoid, bias=col(l, V_W0 + dp))
                    last = act.activation(pr_a[:, dp, :], psum[:, 2 + dd, src], ACT.Sigmoid, bias=col(l, V_A0 + dp))
            last.then_inc(rw_sig, 1)
            act.copy(rw_g.rearrange("p c n -> p (c n)"), psum[:, 4, :])
            act.wait_ge(rw_kraw, l + 1)
            act.activation(pr_t[:, 0:2, :], rw_kk, ACT.Square).then_inc(rw_ksq, 1)
            act.wait_ge(rw_knorm, l + 1)
            act.activation(pr_t[:, 2:4, :], psum[:, 5, :].rearrange("p (c n) -> p c n", c=2), ACT.Sqrt)\
               .then_inc(rw_kdev, 1)
            act.wait_ge(rw_L, l + 1)
            act.activation(pr_E1, pr_L, ACT.Exp)
            act.activation(pr_E2, pr_L, ACT.Exp, scale=-1.0)
            act.activation(pr_E3, pr_lw, ACT.Exp).then_inc(rw_exps, 1)
            for lv in range(1, 6):
                for g in range(4):
                    act.wait_ge(rw_Yr, 20 * l + 4 * (lv - 1) + g + 1)
                    if lv > 1:
                        act.wait_ge(rw_ZT, 20 * l + 4 * (lv - 2) + g + 1)
                    act.copy(rw_Y[:, 4 * g:4 * g + 4, :].rearrange("p i n -> p (i n)"), psum[:, g, :])\
                       .then_inc(rw_Yc, 1)
            act.wait_ge(rw_BKr, l + 1)
            act.copy(rw_BK.rearrange("p d t w n -> p (d t w n)"), psum[:, 4:8, :].rearrange("p b n -> p (b n)"))\
               .then_inc(rw_BKc, 1)
            for s in range(4):
                dd, c4, t, o = cell(s)[1]
                tok = slice(o * HD, (o + 1) * HD)
                act.wait_ge(rw_Gr, 4 * l + s + 1)
                act.copy(rw_G[tok, 2:4, :].rearrange("p d n -> p (d n)"), psum[tok, 0, 2 * P:4 * P]).then_inc(rw_Gc_a, 1)
                act.wait_ge(rw_Ur, 4 * l + s + 1)
                act.copy(rw_U[tok, 2:4, :].rearrange("p d n -> p (d n)"), psum[tok, 1, 2 * P:4 * P]).then_inc(rw_Uc_a, 1)
            act.wait_ge(rw_cent, l + 1)
            act.activation(pr_t2, rw_y, ACT.Square).then_inc(rw_csq, 1)
            act.wait_ge(rw_css, 2 * l + 2)
            act.activation(rw_kk, psum[:, 7, :].rearrange("p (c n) -> p c n", c=2), ACT.Sqrt, bias=eps["gn"],
                           scale=1.0 / HD).then_inc(rw_cdev, 1)

        def dve_rwkv(l):
            v = nc.vector
            HALF = float(np.exp(-0.5))
            for c in range(2):
                last = v.tensor_scalar(rw_kk[:, c, :], uT[:, U_K + c, :], col(l, V_KK + c), None, ALU.mult)
            last.then_inc(rw_kraw, 1)
            v.tensor_scalar(rw_om, col(l, V_KA, 2), -1.0, 1.0, ALU.mult, ALU.add)
            v.wait_ge(rw_sig, l + 1)
            v.tensor_scalar(pr_lw, pr_lw, -HALF, None, ALU.mult)
            v.drain()
            for dp in range(4):
                if dp < 2:
                    v.tensor_tensor_scan(pr_L[:, dp, :], T["keep"][:, 0:SEQ], pr_lw[:, dp, :], 0.0, ALU.mult, ALU.add)
                else:
                    v.tensor_tensor_scan(pr_L[:, dp, ::-1], T["keep"][:, SEQ:2 * SEQ][:, ::-1], pr_lw[:, dp, ::-1],
                                         0.0, ALU.mult, ALU.add)
            v.drain()
            v.tensor_tensor(pr_lw, pr_L, pr_lw, ALU.subtract).then_inc(rw_L, 1)
            v.wait_ge(rw_kdev, l + 1)
            v.tensor_scalar(pr_t[:, 2:4, :], pr_t[:, 2:4, :], 1e-12, None, ALU.max)
            for dp in range(4):
                c = dp % 2
                v.tensor_scalar(pr_kd[:, dp, :], pr_a[:, dp, :], col(l, V_KA + c), rw_om[:, c:c + 1],
                                ALU.mult, ALU.add)
            v.drain()
            v.reciprocal(pr_t[:, 2:4, :], pr_t[:, 2:4, :])
            for dd in range(2):
                kd = pr_kd[:, 2 * dd:2 * dd + 2, :]
                v.tensor_tensor(kd, kd, uT[:, U_K:U_K + 2, :], ALU.mult)
            v.drain()
            v.tensor_tensor(rw_kk, rw_kk, pr_t[:, 2:4, :], ALU.mult)
            v.tensor_tensor(rw_ks, pr_kd[:, 0:2, :], pr_kd[:, 2:4, :], ALU.add)
            v.drain()
            for dd in range(2):
                a = pr_a[:, 2 * dd:2 * dd + 2, :]
                v.tensor_tensor(a, a, rw_kk, ALU.mult)
            v.wait_ge(rw_exps, l + 1)
            v.drain()
            v.tensor_tensor(rw_B, pr_a, pr_E2, ALU.mult)
            v.tensor_tensor(rw_K, pr_kd, pr_E2, ALU.mult)
            for dp in range(4):
                c = dp % 2
                v.scalar_tensor_tensor(out=rw_AR[:, dp, :, 0, :], in0=rw_kk[:, c, :].rearrange("p (t n) -> p t n", t=2),
                                       scalar=-1.0, in1=pr_E3[:, dp, :].rearrange("p (t n) -> p t n", t=2),
                                       op0=ALU.mult, op1=ALU.mult)
                v.tensor_tensor(rw_AR[:, dp, :, 1, :], uT[:, U_R + c, :].rearrange("p (t n) -> p t n", t=2),
                                pr_E1[:, dp, :].rearrange("p (t n) -> p t n", t=2), ALU.mult)
                end = CH - 1 if dp < 2 else 0
                v.tensor_copy(rw_PC[:, dp, :], pr_E1[:, dp, end::CH])
            v.memset(rw_S, 0.0)
            v.memset(rw_Sc, 0.0)
            ident = T["ident"].unsqueeze(1).broadcast_to([P, 16, P])
            v.tensor_copy(rw_T, ident)
            v.tensor_copy(rw_TT, ident)
            v.drain()
            v.sem_inc(rw_prep, 1)
            lower = lambda lv, low: T["levels"][:, ((0 if low else 6) + lv) * P:((0 if low else 6) + lv + 1) * P]\
                .bitcast(U32).unsqueeze(1).broadcast_to([P, 4, P])
            for g in range(4):
                v.wait_ge(rw_N, 4 * l + g + 1)
                v.copy_predicated(rw_T[:, 4 * g:4 * g + 4, :], lower(0, g % 2 == 0),
                                  psum[:, g, :].rearrange("p (i n) -> p i n", i=4)).then_inc(rw_T0, 1)
            v.tensor_copy(rw_v.rearrange("p t n -> p (t n)"), psum[:, 6, :])
            for i in range(16):
                dd = i % 8 // 4
                v.wait_ge(rw_mats, 16 * l + i + 1)
                v.tensor_tensor(rw_mb[:, i, :].rearrange("p (w n) -> p w n", w=2),
                                psum[:, i % 4, :].rearrange("p (w n) -> p w n", w=2),
                                T["tri"][:, dd * SEQ:(dd + 1) * SEQ].unsqueeze(1).broadcast_to([P, 2, SEQ]), ALU.mult)\
                 .then_inc(rw_masked, 1)
            v.drain()
            for g in range(4):
                v.copy_predicated(rw_TT[:, 4 * g:4 * g + 4, :], lower(0, g % 2 == 1), rw_mb[:, 4 * g:4 * g + 4, 0:P])
            v.drain()
            v.sem_inc(rw_T0s, 1)
            for lv in range(1, 6):
                for g in range(4):
                    v.wait_ge(rw_ZT, 20 * l + 4 * (lv - 1) + g + 1)
                    if lv < 5:
                        v.copy_predicated(rw_T[:, 4 * g:4 * g + 4, :], lower(lv, g % 2 == 0),
                                          psum[:, 4 + g, :].rearrange("p (i n) -> p i n", i=4))
                    v.copy_predicated(rw_TT[:, 4 * g:4 * g + 4, :], lower(lv, g % 2 == 1),
                                      psum[:, g, :].rearrange("p (i n) -> p i n", i=4)).then_inc(rw_Tn, 1)
            for s in range(4):
                dd, c4, t, o = cell(s)[0]
                tok = slice(o * HD, (o + 1) * HD)
                v.wait_ge(rw_Gr, 4 * l + s + 1)
                v.tensor_copy(rw_G[tok, 0:2, :].rearrange("p d n -> p (d n)"), psum[tok, 0, 0:2 * P]).then_inc(rw_Gc_v, 1)
                v.wait_ge(rw_Ur, 4 * l + s + 1)
                v.tensor_copy(rw_U[tok, 0:2, :].rearrange("p d n -> p (d n)"), psum[tok, 1, 0:2 * P]).then_inc(rw_Uc_v, 1)
                if s < 3:
                    v.wait_ge(rw_Sr, 3 * l + s + 1)
                    for dd, c4, t, o in cell(s):
                        sc = rw_Sc[:, 2 * dd:2 * dd + 2, :]
                        v.tensor_tensor(sc, sc, psum[:, 3 + dd, 0:2 * HD].rearrange("p (c n) -> p c n", c=2), ALU.add)
                    v.drain()
                    for dd, c4, t, o in cell(s):
                        sc = rw_Sc[:, 2 * dd:2 * dd + 2, :]
                        v.tensor_tensor(sc, sc, rw_PC[:, 2 * dd:2 * dd + 2, c4:c4 + 1].broadcast_to([P, 2, HD]), ALU.mult)
                    v.drain()
                v.wait_ge(rw_yr, 4 * l + s + 1)
                if s < 3:
                    for a in range(2):
                        hv = slice(a * HD, (a + 1) * HD)
                        v.tensor_copy(rw_S[hv, :, hv], rw_Sc[hv, :, :])
                for dd, c4, t, o in cell(s):
                    dst = rw_y[:, :, c4 * CH:(c4 + 1) * CH]
                    src = psum[:, 2, 2 * dd * HD:(2 * dd + 2) * HD].rearrange("p (c n) -> p c n", c=2)
                    if s < 2:
                        last = v.tensor_copy(dst, src)
                    else:
                        last = v.tensor_tensor(dst, dst, src, ALU.add)
                last.then_inc(rw_Sn, 1)
            for c in range(2):
                v.scalar_tensor_tensor(out=rw_ks[:, c, :], in0=rw_ks[:, c, :], scalar=col(l, V_RK + c),
                                       in1=uT[:, U_R + c, :], op0=ALU.mult, op1=ALU.mult)
            v.drain()
            v.sem_inc(rw_sum, 1)
            v.wait_ge(rw_css, 2 * l + 1)
            flat = lambda b: b.rearrange("p c n -> p (c n)")
            v.scalar_tensor_tensor(out=flat(rw_y), in0=psum[:, 5, :], scalar=-1.0 / HD, in1=flat(rw_y),
                                   op0=ALU.mult, op1=ALU.add).then_inc(rw_cent, 1)
            v.tensor_tensor(rw_ks, psum[:, 6, :].rearrange("p (c n) -> p c n", c=2), uT[:, U_V:U_V + 2, :], ALU.mult)
            v.wait_ge(rw_cdev, l + 1)
            v.reciprocal(rw_kk, rw_kk)
            v.drain()
            for c in range(2):
                v.scalar_tensor_tensor(out=rw_y[:, c, :], in0=rw_y[:, c, :], scalar=col(l, V_LG + c),
                                       in1=rw_kk[:, c, :], op0=ALU.mult, op1=ALU.mult)
            v.drain()
            for c in range(2):
                v.scalar_tensor_tensor(out=rw_y[:, c, :], in0=rw_y[:, c, :], scalar=col(l, V_LB + c),
                                       in1=rw_ks[:, c, :], op0=ALU.add, op1=ALU.add)
            v.drain()
            v.tensor_tensor(oT[:, 2:4, :], rw_y, rw_g, ALU.mult).then_inc(rw_done, 1)

        def sync_second_block(sp):
            for l in range(DEPTH):
                load_units(sp, d["ff_w"][2 * l], FF_CHUNKS, UNIT)
                load_units(sp, d["mix_w"][l], U_CHUNKS // 3, UNIT)
                load_units(sp, d["proj_w"][2 + l], 4, 2 * D)
                load_units(sp, d["ff_w"][2 * l + 1], FF_CHUNKS, UNIT)
            sp.wait_ge(final_ready, 1)
            sp.dma_start(out[0].rearrange("(t p) n -> p t n", p=P), hn).then_inc(stored, 16)
            sp.wait_ge(stored, 16)

        def pool_second_block():
            pool = nc.gpsimd
            pool.wait_ge(rowv_used, 4)
            pool.dma_start(pos_i, d["positions"].partition_broadcast(P)).then_inc(pos_loaded, 16)
            for l in range(DEPTH):
                if l:
                    pool.wait_ge(rw_done, l)
                pool.dma_start(small[:], d["small_w"][l]).then_inc(small_loaded, 16)
            pool.wait_ge(rw_done, DEPTH)
            pool.dma_start(rowv[:, 0:1, :], d["row_vectors"][8:9].partition_broadcast(P)).then_inc(rowv_full, 16)

        def pe_second_block():
            for l in range(DEPTH):
                pe_glu(FF_CHUNKS)
                pe_turn(hn)
                nc.tensor.wait_ge(turned_used, pe_u.turned)
                pe_inputs(l)
                pe_retention(l)
                pe_latent(l)
                pe_rwkv(l)
                pe_project(oT, rw_done, l + 1)
                pe_turn(hn)
                nc.tensor.wait_ge(turned_used, pe_u.turned)
                pe_glu(FF_CHUNKS)
                if l < DEPTH - 1:
                    pe_turn(hn)
                    nc.tensor.wait_ge(turned_used, pe_u.turned)

        def dve_second_block():
            dve_rope_tables()
            for l in range(DEPTH):
                dve_glu(FF_CHUNKS, False)
                dve_norm(0.5, rms=True, gain=col(l, V_MIX, KC))
                take_inputs(nc.vector, nc.vector.tensor_copy, 0, u_copied_v, l)
                dve_conv(l)
                dve_retention(l)
                dve_latent(l)
                dve_rwkv(l)
                dve_ring.take(U_CHUNKS // 3 + 4)
                dve_norm(1.0, rms=True, gain=col(l, V_F2, KC), parts=True)
                dve_glu(FF_CHUNKS, False)
                if l < DEPTH - 1:
                    dve_norm(0.5, rms=True, gain=col(l + 1, V_F1, KC), parts=True)
            dve_norm(0.5, rms=True, turn=False)
            nc.vector.wait_ge(rowv_full, 16 * 5)
            for t in range(TILES):
                last = nc.vector.tensor_tensor(hn[:, t, :], hn[:, t, :], rowv[:, 0, :], ALU.mult)
            last.then_inc(final_ready, 1)

        def act_second_block():
            act_rope_tables()
            for l in range(DEPTH):
                act_glu(FF_CHUNKS)
                act_norm(rms=True)
                take_inputs(nc.scalar, nc.scalar.copy, 1, u_copied_a, l)
                act_retention(l)
                act_latent(l)
                act_rwkv(l)
                act_ring.take(U_CHUNKS // 3 + 4)
                act_norm(rms=True, gain=col(l, V_F2, KC), parts=True)
                act_glu(FF_CHUNKS)
                if l < DEPTH - 1:
                    act_norm(rms=True, gain=col(l + 1, V_F1, KC), parts=True)
            act_norm(rms=True, turns=0)


        block = ctx.enter_context(nc.Block())
        @block.sync
        def _(sp):
            sp.dma_start(x[:], d["x"].rearrange("(t p) n -> p t n", p=P)).then_inc(x_loaded, 16)
            sp.dma_start(tab[:], d["tables"]).then_inc(tables_loaded, 16)
            load_dilated(sp)
            load_units(sp, d["proj_w"][0], 4, 2 * D)
            load_units(sp, d["moe_w"][0], MOE_CHUNKS, UNIT)
            load_units(sp, d["sb_w"], PAIRS, UNIT)
            load_units(sp, d["proj_w"][1], 4, 2 * D)
            load_units(sp, d["moe_w"][1], MOE_CHUNKS, UNIT)
            sync_second_block(sp)

        @block.gpsimd
        def _(pool):
            pool.dma_start(hot[0:BUCKETS + 1, :], d["early_tables"][0:BUCKETS + 1, 0:GROUPS * 3 * P])\
                .then_inc(early_loaded, 16)
            pool.dma_start(rel_tab[0:BUCKETS, :], d["rel_table"]).then_inc(early_loaded, 16)
            pool.dma_start(pick[0:EXPERTS], d["early_tables"][0:EXPERTS, GROUPS * 3 * P:]
                           .rearrange("p (e n) -> p e n", e=EXPERTS)).then_inc(early_loaded, 16)
            pool.dma_start(router_w[:], d["router_w"]).then_inc(router_loaded, 16)
            pool.dma_start(router_b, d["router_b"].partition_broadcast(P)).then_inc(router_loaded, 16)
            pool.dma_start(vec[:], d["vectors"].rearrange("l p n -> p l n")).then_inc(vec_loaded, 16)
            pool.wait_ge(rel_copied, 1)
            pool.dma_start(rel_dram, rel_rows[0:HEADS, :]).then_inc(rel_stored, 16)
            pool_rows(0)
            pool_bias()
            pool_rows(1)
            pool_rows(2)
            pool_rows(3)
            pool_second_block()

        @block.tensor
        def _(pe):
            pe.wait_ge(x_loaded, 16)
            pe.wait_ge(tables_loaded, 16)
            pe_turn(x, counted=False)
            pe.wait_ge(early_loaded, 48)
            pe.wait_ge(zero_ready, 1)
            for g in range(GROUPS):
                last = pe.matmul(psum[0:HEADS, 4 + g, 0:3 * P], rel_tab[0:BUCKETS + 1, :],
                                 hot[0:BUCKETS + 1, g * 3 * P:(g + 1) * 3 * P], start=True, stop=True)
            last.then_inc(rel_ready, 1)
            pe.wait_ge(rel_copied, 1)
            pe_dilated()
            pe_project(oT, o_copied, PAIRS)
            pe_turn(x)
            pe_router(0)
            pe_glu(MOE_CHUNKS)
            pe_turn(x, flip=True)
            pe_sticks()
            pe_project(oT, sb_o_copied, PAIRS)
            pe_turn(x)
            pe_router(1)
            pe_glu(MOE_CHUNKS)
            pe_turn(hn)
            nc.tensor.wait_ge(turned_used, pe_u.turned)
            pe_second_block()

        @block.vector
        def _(v):
            v.memset(zero[:], 0.0)
            v.memset(rel_tab[BUCKETS:BUCKETS + 1, :], NEG).then_inc(zero_ready, 1)
            dve_norm(None)
            v.wait_ge(rel_ready, 1)
            v.tensor_copy(rel_rows[0:HEADS, :].rearrange("p (g n) -> p g n", g=GROUPS),
                          psum[0:HEADS, 4:7, 0:3 * P]).then_inc(rel_copied, 1)
            dve_dilated()
            dve_ring.take(4)
            dve_norm("norm", ln=True, parts=True)
            dve_router(0)
            dve_glu(MOE_CHUNKS, True)
            dve_norm("norm", ln=True, flip=True)
            dve_sticks()
            dve_ring.take(PAIRS + 4)
            dve_norm("norm", ln=True, parts=True)
            dve_router(1)
            dve_glu(MOE_CHUNKS, True)
            dve_norm("norm", ln=True, rms=True, gain=vec[:, 0, V_F1:V_F1 + KC], parts=True)
            dve_second_block()

        @block.scalar
        def _(act):
            act.wait_ge(tables_loaded, 16)
            act_u.turned = 4
            act_dilated()
            act_ring.skip(range(GROUPS), PAIRS)
            act_ring.take(4)
            act_norm(ln=True, parts=True)
            act_router(0)
            act_glu(MOE_CHUNKS)
            act_norm(ln=True, turns=8)
            act_sticks()
            act_ring.take(PAIRS + 4)
            act_norm(ln=True, parts=True)
            act_router(1)
            act_glu(MOE_CHUNKS)
            act_norm(ln=True, rms=True, gain=vec[:, 0, V_F1:V_F1 + KC], parts=True)
            act_second_block()


_OUT = (1, SEQ, D)


def kernel(**inputs):
    import concourse.bacc as bacc
    from concourse.bass_utils import run_bass_kernel_spmd as run

    arrays = layout(inputs)
    nc = bacc.Bacc("TRN2", target_bir_lowering=False, num_devices=1)
    d = {k: nc.dram_tensor(k, v.shape, mybir.dt.from_np(v.dtype), kind="ExternalInput").ap()
         for k, v in arrays.items()}
    out = nc.dram_tensor("out", _OUT, F32, kind="ExternalOutput").ap()
    build_kernel(nc, d, out)
    r = run(nc, [arrays], core_ids=[0])
    return r.results[0]["out"]
```

```python
from contextlib import ExitStack

import concourse.bass as bass
import numpy as np
from concourse import mybir

F32 = mybir.dt.float32
F32R = mybir.dt.float32r
I32 = mybir.dt.int32
U32 = mybir.dt.uint32
ALU = mybir.AluOpType
ACT = mybir.ActivationFunctionType
AX_X = mybir.AxisListType.X

P = 128
SEQ = 256
TILES = SEQ // P
D = 1024
KC = D // P
HD = 64
HEADS = 16
PAIRS = HEADS // 2
GROUPS = 3
DILATION = (1, 4, 16)
SPAN = (128, 512, 2048)
BUCKETS, BUCKET_DIST = 32, 2048
EXPERTS, EXPERT_FF = 16, 256
MOE_CHUNKS = EXPERTS * EXPERT_FF // P
FF_CHUNKS = 2816 // P
DEPTH = 2
ALPHA = (2 * DEPTH) ** 0.25
UNIT = 3 * KC * P
SLOTS = 4
NEG = -1e30
SB_CLIP = 60.0
CH = 64
MIX_HEADS = 4
U_CHUNKS = 30
(U_CX, U_CB, U_CC, U_RQ, U_RK, U_RV, U_RG, U_QA, U_CKV, U_KR, U_R, U_K, U_V, U_WD, U_AD, U_GD) = (
    0, 2, 4, 6, 8, 10, 12, 14, 17, 18, 19, 21, 23, 25, 26, 27)
(V_F1, V_MIX, V_F2, V_CONV, V_W0, V_A0, V_KK, V_KA, V_RK, V_LG, V_LB, V_GN, V_QN, V_KVN) = (
    0, 8, 16, 24, 30, 34, 38, 40, 42, 44, 46, 48, 50, 53)
N_VEC = 54
W_W2, W_A2, W_G2, W_QB, W_KB, W_VB = 0, 256, 512, 768, 768 + 3 * 512, 768 + 3 * 512 + 256
N_SMALL = W_VB + 256


def bucket(dist):
    n = np.maximum(dist, 0)
    exact = BUCKETS // 2
    logf = np.log(np.maximum(n, 1).astype(np.float32) / np.float32(exact)) / np.float32(
        np.log(BUCKET_DIST / exact))
    large = np.minimum(exact + (logf * np.float32(BUCKETS - exact)).astype(np.int32), BUCKETS - 1)
    return np.where(n < exact, n, large)


def constants():
    r, c = np.arange(P)[:, None], np.arange(P)[None, :]
    out = {"ident": (r == c) * 1.0, "flip": (r + c == P - 1) * 1.0}
    def turn(half, lo, hi):
        m = np.zeros((P, P))
        for t in range(lo, hi):
            j = (t - lo) % (2 * half)
            if j < half:
                m[t + half, t] = -1.0
            else:
                m[t - half, t] = 1.0
        return m
    out["turn_ret"] = turn(32, 0, 128)
    out["turn_mla"] = turn(16, 64, 96)
    same = (r // HD) == (c // HD)
    out["ones_head"] = same * 1.0
    out["ones"] = np.ones((P, SEQ))
    out["sb_mask"] = (c > P - 1 - r) * 1.0
    gamma = 1.0 - 2.0 ** (-5.0 - np.arange(MIX_HEADS))
    dist = np.abs(np.arange(3 * P)[None, :] - P - r)
    out["decay"] = np.concatenate([g ** dist / 8.0 for g in gamma], 1)
    out["tri"] = np.concatenate([same * (r < c), same * (r <= c), same * (r > c), same * (r >= c)], 1)
    levels = []
    for lower in (True, False):
        for lv in range(6):
            b = 1 << lv
            a, z = (r, c) if lower else (c, r)
            levels.append(((a // (2 * b)) == (z // (2 * b))) & (a // b % 2 == 1) & (z // b % 2 == 0))
    out["levels"] = np.concatenate(levels, 1) * 1.0
    t = np.arange(SEQ)
    out["keep"] = np.tile(np.concatenate([t % CH != 0, t % CH != CH - 1])[None] * 1.0, (P, 1))
    inv_r = 10000.0 ** (-(np.arange(32, dtype=np.float32)) / np.float32(32))
    inv_m = 10000.0 ** (-(np.arange(16, dtype=np.float32)) / np.float32(16))
    out["inv"] = np.stack([np.tile(inv_r.astype(np.float32), 4), np.tile(inv_m.astype(np.float32), 8)], 1)
    out["eps"] = np.tile(np.array([[1e-5, 1e-6, 64e-5, 1.0, 0.0]]), (P, 1))
    dist = 255 - np.arange(3 * P)
    hot = np.zeros((P, GROUPS, 3 * P))
    for g in range(GROUPS):
        seen = (dist >= 0) & (dist % DILATION[g] == 0) & (dist <= SPAN[g])
        hot[bucket(dist), g, np.arange(3 * P)] = 8.0
        hot[:, g, ~seen] = 0.0
        hot[BUCKETS, g, ~seen] = 1.0
    out["hot"] = hot.reshape(P, -1)
    pick = np.zeros((P, EXPERTS, P))
    pick[np.arange(EXPERTS), np.arange(EXPERTS), :] = 1.0
    out["pick"] = pick.reshape(P, -1)
    lower4 = np.tril(np.ones((4, 4)), -1)
    out["before"] = np.tile(lower4.reshape(1, 16), (P, 1))
    return {k: np.ascontiguousarray(v, np.float32) for k, v in out.items()}


CONST_ORDER = ["ident", "flip", "turn_ret", "turn_mla", "ones_head", "ones", "sb_mask", "decay", "tri",
               "levels", "keep", "inv", "eps", "before"]
EARLY_ORDER = ["hot", "pick"]


def layout(inputs):
    f = {k: np.asarray(v) for k, v in inputs.items()}

    def rows(w):
        return w.reshape(-1, P, w.shape[-1]).transpose(1, 0, 2)

    def glu(gate, up, down):
        n = gate.shape[1] // P
        g = gate.reshape(KC, P, n, P).transpose(2, 1, 0, 3).reshape(n, P, -1)
        u = up.reshape(KC, P, n, P).transpose(2, 1, 0, 3).reshape(n, P, -1)
        return np.concatenate([g, u, down.reshape(n, P, D)], 2)

    out = {"x": f["x"][0], "rel_table": f["rel_table"], "router_b": f["router_b"],
           "router_w": rows(f["router_w"]), "positions": f["positions_2"].astype(np.int32)}
    w = f["dil_w_in"][0].reshape(KC, P, GROUPS, 3, PAIRS, P)
    out["dil_w"] = w.transpose(4, 2, 1, 0, 3, 5).reshape(PAIRS, GROUPS, P, UNIT)
    w = f["sb_w_in"][0].reshape(KC, P, 3, PAIRS, P)
    out["sb_w"] = w.transpose(3, 1, 0, 2, 4).reshape(PAIRS, P, UNIT)
    out["proj_w"] = np.stack([rows(w).reshape(P, 4, 2 * D).transpose(1, 0, 2)
                              for w in (f["dil_w_out"][0], f["sb_w_out"][0], f["w_out_2"][0], f["w_out_2"][1])])
    moe = []
    for l in range(DEPTH):
        g = f["exp_w_gate"][l].transpose(1, 0, 2).reshape(D, -1)
        u = f["exp_w_up"][l].transpose(1, 0, 2).reshape(D, -1)
        moe.append(glu(g, u, f["exp_w_down"][l].reshape(-1, D)))
    out["moe_w"] = np.stack(moe)
    out["ff_w"] = np.stack([glu(f[f"ffn{n}_w_gate_2"][l], f[f"ffn{n}_w_up_2"][l], f[f"ffn{n}_w_down_2"][l])
                            for l in range(DEPTH) for n in (1, 2)])
    mix, small, vec = [], [], []
    for l in range(DEPTH):
        w = f["w_in_2"][l]
        cut = np.cumsum([256] * 6 + [64, 64, 64, 64, 128] + [256] * 4 + [384, 160])[:-1]
        (cx, cb, cc, r, k, v, wdf, wdb, adf, adb, gd, rq, rk, rv, rg, qa, kva) = np.split(w, cut, axis=1)
        z64 = np.zeros((D, 64), np.float32)
        kr = np.concatenate([z64, kva[:, 128:], np.zeros((D, 32), np.float32)], 1)
        u = np.concatenate([cx, cb, cc, rq, rk, rv, rg, qa, kva[:, :128], kr, r, k, v, wdf, wdb, adf, adb, gd,
                            np.zeros((D, 256), np.float32)], 1)
        mix.append(u.reshape(KC, P, U_CHUNKS // 3, 3 * P).transpose(2, 1, 0, 3).reshape(U_CHUNKS // 3, P, UNIT))
        qb = f["mla_q_b_2"][l].reshape(384, 4, 96)
        qb = np.concatenate([qb, np.zeros((384, 4, 32), np.float32)], 2).reshape(384, 512)
        kvb = f["mla_kv_b_2"][l].reshape(P, 4, 128)
        small.append(np.concatenate([
            np.concatenate([f["rwkv_w2_f_2"][l], f["rwkv_w2_b_2"][l]], 0),
            np.concatenate([f["rwkv_a2_f_2"][l], f["rwkv_a2_b_2"][l]], 0),
            f["rwkv_g2_2"][l], rows(qb).reshape(P, -1),
            kvb[:, :, :64].reshape(P, 256), kvb[:, :, 64:].reshape(P, 256)], 1))
        col = lambda a: a.reshape(-1, P).T
        vec.append(np.concatenate([
            col(f["ffn1_norm_2"][l]), col(f["mix_norm_2"][l]), col(f["ffn2_norm_2"][l]),
            col(f["conv_w_2"][l]), col(f["rwkv_w0_f_2"][l]), col(f["rwkv_w0_b_2"][l]),
            col(f["rwkv_a0_f_2"][l]), col(f["rwkv_a0_b_2"][l]), col(f["rwkv_k_k_2"][l]), col(f["rwkv_k_a_2"][l]),
            col(f["rwkv_r_k_2"][l].reshape(-1)), col(f["rwkv_lnx_g_2"][l]), col(f["rwkv_lnx_b_2"][l]),
            col(f["ret_gn_g_2"][l]), col(f["mla_q_a_norm_2"][l]), col(f["mla_kv_a_norm_2"][l])], 1))
    out["mix_w"] = np.stack(mix)
    out["small_w"] = np.stack(small)
    out["vectors"] = np.stack(vec)
    out["row_vectors"] = np.stack([f["ln1_g"][0], f["ln1_b"][0], f["ln2_g"][0], f["ln2_b"][0],
                                   f["ln1_g"][1], f["ln1_b"][1], f["ln2_g"][1], f["ln2_b"][1],
                                   f["final_norm_2"]])
    c = constants()
    out["tables"] = np.concatenate([c[k] for k in CONST_ORDER], 1)
    out["early_tables"] = np.concatenate([c[k] for k in EARLY_ORDER], 1)
    return {k: np.ascontiguousarray(v) for k, v in out.items()}


class Ring:

    def __init__(self):
        self.count = [0] * SLOTS
        self.silent = [0] * SLOTS
        self.next = 0
        self.units = 0

    def take(self, n, parts=True):
        out = []
        self.units += n if parts else 0
        for _ in range(n):
            out.append((self.next, self.count[self.next]))
            self.count[self.next] += 1
            self.next = (self.next + 1) % SLOTS
        return out

    def skip(self, slots, turns):
        for s in slots:
            self.count[s] += turns


def build_kernel(nc, d, out):
    ctx = ExitStack()
    consts = constants()

    with ctx:
        def sb(name, shape, dt=F32):
            return ctx.enter_context(nc.sbuf_tensor(name, shape, dt))

        def sem(name):
            return ctx.enter_context(nc.semaphore(name))

        base = nc.sbuf_base + -nc.sbuf_base % 32

        def place(name, at, shape, dt=F32):
            return nc.alloc_sbuf_tensor_at(name, shape, dt, offset=base + 4 * at)

        n_tab = sum(consts[k].shape[1] for k in CONST_ORDER)
        plan, at = {}, 0
        for name, size in (("x", TILES * D), ("xT_hi", KC * SEQ), ("xT_lo", KC * SEQ), ("oT", KC * SEQ),
                           ("ring", SLOTS * UNIT), ("small", N_SMALL), ("rowv", 2 * D), ("zero", 256), ("stat", 32),
                           ("lead", 8), ("PC", 16), ("om", 8), ("scratch", 22016), ("vec", DEPTH * N_VEC + 4),
                           ("tab", n_tab)):
            plan[name] = at
            at += size
        x = place("x_rows", plan["x"], [P, TILES, D])
        xT_hi = place("xT_hi", plan["xT_hi"], [P, KC, SEQ], F32R)
        xT_lo = place("xT_lo", plan["xT_lo"], [P, KC, SEQ], F32R)
        oT = place("oT", plan["oT"], [P, KC, SEQ])
        ring = place("ring", plan["ring"], [P, SLOTS, UNIT])
        ring_lo = place("ring_lo", plan["ring"], [P, SLOTS, UNIT], F32R)
        ring_hi = place("ring_hi", plan["scratch"] + 8192, [P, SLOTS, UNIT], F32R)
        tab = place("tab_sb", plan["tab"], [P, n_tab])
        small = place("small", plan["small"], [P, N_SMALL])
        early = place("early", plan["small"], [P, N_SMALL])
        vec = place("vec", plan["vec"], [P, DEPTH, N_VEC])
        rowv = place("rowv", plan["rowv"], [P, 2, D])
        stat = place("stat", plan["stat"], [P, TILES, 16])
        lead = place("lead", plan["lead"], [P, TILES, 4])
        zero = place("zero", plan["zero"], [P, 512], mybir.dt.bfloat16)
        scratch = place("scratch", plan["scratch"], [P, 22016])
        psum = ctx.enter_context(nc.psum_tensor("psum", [P, 8, 512], F32))
        rel_dram = nc.dram_tensor("rel_dram", [HEADS, GROUPS * 3 * P], F32, kind="Internal").ap()

        at, T = 0, {}
        for k in CONST_ORDER:
            T[k] = tab[:, at:at + consts[k].shape[1]]
            at += consts[k].shape[1]
        eps = {k: T["eps"][:, i:i + 1] for i, k in enumerate(("ln", "rms", "gn", "one", "zero"))}

        def carve(at, *shape):
            size = int(np.prod(shape))
            v = scratch[:, at:at + size]
            names = "abcd"[:len(shape)]
            if len(shape) == 1:
                return v
            return v.rearrange(f"p ({' '.join(names)}) -> p {' '.join(names)}",
                               **{n: s for n, s in zip(names[1:], shape[1:])})

        glu_s = carve(0, SLOTS, SEQ)
        glu_t = carve(1024, SLOTS, SEQ)
        glu_hi = place("glu_hi", plan["scratch"] + 2048, [P, SLOTS, SEQ], F32R)
        glu_lo = place("glu_lo", plan["scratch"] + 3072, [P, SLOTS, SEQ], F32R)
        hn = carve(4096, TILES, D)
        route_w = carve(4096, EXPERTS, SEQ)
        pick = early[:, 0:2048].rearrange("p (e n) -> p e n", e=EXPERTS)
        router_w = early[:, 2048:2176].rearrange("p (k e) -> p k e", k=KC)
        router_b = early[:, 2176:2192]
        rt = carve(0, 1024)
        hot = carve(19712, GROUPS * 3 * P)
        rel_tab = carve(20864, HEADS)
        rel_rows = carve(17408, GROUPS * 3 * P)
        xTr_hi = place("xTr_hi", plan["scratch"] + 5376, [P, KC, SEQ], F32R)
        xTr_lo = place("xTr_lo", plan["rowv"], [P, KC, SEQ], F32R)
        qk_sb = carve(0, 2, GROUPS, 2 * SEQ)
        v_sb = carve(3072, 2, GROUPS, TILES * P)
        bias_sb = carve(4608, 2, 2, GROUPS * SEQ)
        probs = carve(17408, 2, GROUPS * 3 * P)
        probsT = carve(19712, 2, GROUPS * 3 * P)
        soft = carve(7680, 4, 4)
        sb_qk = carve(0, 2, 2 * SEQ)
        sb_v = carve(1024, 2, SEQ)
        sb_z = carve(1536, 2, 3 * P)
        sb_a2 = (carve(2304, 2, 3 * P), carve(7424, 2, 3 * P))
        sb_p = carve(3072, 2, 3 * P)
        sb_r = carve(3840, 2, 3 * P)
        sb_aT = carve(4608, 2, 3 * P)

        ring_full = [sem(f"ring_full{i}") for i in range(SLOTS)]
        ring_free = [sem(f"ring_free{i}") for i in range(SLOTS)]
        x_loaded, tables_loaded = sem("x_loaded"), sem("tables_loaded")
        early_loaded, router_loaded = sem("early_loaded"), sem("router_loaded")
        rel_ready, rel_copied, rel_stored = sem("rel_ready"), sem("rel_copied"), sem("rel_stored")
        bias_full = [sem("bias_full0"), sem("bias_full1")]
        rowv_full, rowv_used = sem("rowv_full"), sem("rowv_used")
        acc_ready = sem("acc_ready")
        acc_used = sem("acc_used")
        var_ready, dev_ready = sem("var_ready"), sem("dev_ready")
        rows_ready = sem("rows_ready")
        turned, turned_used = sem("turned"), sem("turned_used")
        high_ready, low_ready = sem("high_ready"), sem("low_ready")
        o_high, o_low = sem("o_high"), sem("o_low")
        turned_high = sem("turned_high")
        gate_up, silu_ready, hidden_ready = sem("gate_up"), sem("silu_ready"), sem("hidden_ready")
        logits_ready, router_sig = sem("logits_ready"), sem("router_sig")
        gates_ready, gatesT_ready, gatesT_copied = sem("gates_ready"), sem("gatesT_ready"), sem("gatesT_copied")
        spread_ready, spread_copied = sem("spread_ready"), sem("spread_copied")
        qk_ready, qk_copied = sem("qk_ready"), sem("qk_copied")
        v_ready, v_copied = sem("v_ready"), sem("v_copied")
        scores_ready, max_ready, exp_ready = sem("scores_ready"), sem("max_ready"), sem("exp_ready")
        probs_ready, probsT_ready, probsT_copied = sem("probs_ready"), sem("probsT_ready"), sem("probsT_copied")
        o_ready, o_copied = sem("o_ready"), sem("o_copied")
        sb_qk_ready, sb_qk_copied = sem("sb_qk_ready"), sem("sb_qk_copied")
        sb_v_ready, sb_v_copied = sem("sb_v_ready"), sem("sb_v_copied")
        sb_scores, sb_clipped, sb_exp1, sb_soft = sem("sb_scores"), sem("sb_clipped"), sem("sb_exp1"), sem("sb_soft")
        sb_minus, sb_exp2, sb_att = sem("sb_minus"), sem("sb_exp2"), sem("sb_att")
        sb_aT_ready, sb_aT_copied = sem("sb_aT_ready"), sem("sb_aT_copied")
        sb_o_ready, sb_o_copied = sem("sb_o_ready"), sem("sb_o_copied")
        vec_loaded = sem("vec_loaded")
        dumped, zero_ready = sem("dumped"), sem("zero_ready")
        stored = sem("stored")

        acc = psum[:, 4:8, :].rearrange("p (t n) c -> p t (n c)", t=TILES)

        def load_units(sp, units, n, floats):
            r = sync_ring
            turns = n // SLOTS
            first = r.next
            lanes = [(first + k) % SLOTS for k in range(SLOTS)]

            def load(k, s, value, src):
                if not isinstance(value, int) or value > 0:
                    sp.wait_ge(ring_free[s], value)
                sp.dma_start(ring[:, s, 0:floats], src).then_inc(ring_full[s], 16)

            freed = lambda s: r.count[s] - r.silent[s]
            start = 1 if min(freed(s) for s in lanes) < 1 else 0
            for k in range(start * SLOTS):
                load(k, lanes[k], freed(lanes[k]), units[k])
                r.count[lanes[k]] += 1
            if turns - start > 1:
                with sp.Fori(0, turns - start) as i:
                    for k, s in enumerate(lanes):
                        src = units[bass.ds(i * SLOTS + (start * SLOTS + k), 1)].rearrange("o p n -> (o p) n")
                        load(k, s, i + freed(s), src)
                r.skip(lanes, turns - start)
                start = turns
            for k in range(start * SLOTS, n):
                s = lanes[k % SLOTS]
                load(k, s, freed(s), units[k])
                r.count[s] += 1
            r.next = (first + n) % SLOTS

        def load_dilated(sp):
            for g in range(GROUPS):
                sp.dma_start(ring[:, g, :], d["dil_w"][0, g]).then_inc(ring_full[g], 16)
            with sp.Fori(1, PAIRS) as p:
                for g in range(GROUPS):
                    sp.wait_ge(v_copied, p * GROUPS + (g + 1 - GROUPS))
                    src = d["dil_w"].rearrange("a g p n -> (a g) p n")[bass.ds(p * GROUPS + g, 1)]
                    sp.dma_start(ring[:, g, :], src.rearrange("o p n -> (o p) n")).then_inc(ring_full[g], 16)
            sync_ring.skip(range(GROUPS), PAIRS)
            for g in range(GROUPS):
                sync_ring.silent[g] = PAIRS
            sp.wait_ge(v_copied, PAIRS * GROUPS)

        sync_ring, pe_ring, act_ring, dve_ring = Ring(), Ring(), Ring(), Ring()

        def products(dst, w_hi, w_lo, m_hi, m_lo, start, stop, **kw):
            nc.tensor.matmul(dst, w_hi, m_hi, start=start, stop=False, **kw)
            nc.tensor.matmul(dst, w_hi, m_lo, start=False, stop=False, **kw)
            return nc.tensor.matmul(dst, w_lo, m_hi, start=False, stop=stop, **kw)

        def act_split(j, i=0, floats=UNIT):
            s = (act_ring.next + j) % SLOTS
            nc.scalar.wait_ge(ring_full[s], i * 16 + 16 * (act_ring.count[s] + j // SLOTS + 1))
            nc.scalar.copy(ring_hi[:, s, 0:floats], ring[:, s, 0:floats]).then_inc(high_ready, 1)

        def dve_split(j, i=0, floats=UNIT):
            s = (dve_ring.next + j) % SLOTS
            nc.vector.wait_ge(high_ready, i * SLOTS + (dve_ring.units + j + 1))
            nc.vector.tensor_tensor(ring_lo[:, s, 0:floats], ring[:, s, 0:floats],
                                    ring_hi[:, s, 0:floats].bitcast(F32), ALU.subtract).then_inc(low_ready, 1)

        def act_ahead():
            act_split(0)
            act_split(1)

        def dve_ahead():
            dve_split(0)
            dve_split(1)

        n_norm = [0, 0, 0, 0]

        class Uses:
            def __init__(self):
                self.acc = self.var = self.dev = self.rows = self.turned = self.rowv = self.o = 0
        pe_u, dve_u, act_u = Uses(), Uses(), Uses()

        def dve_norm(update, ln=False, rms=False, gain=None, turn=True, flip=False):
            u, v = dve_u, nc.vector
            if update is not None:
                v.wait_ge(acc_ready, u.acc + 1)
                u.acc += 1
                for t in range(TILES):
                    if update == "norm":
                        v.scalar_tensor_tensor(out=x[:, t, :], in0=x[:, t, :], scalar=ALPHA, in1=acc[:, t, :],
                                               op0=ALU.mult, op1=ALU.add).then_inc(acc_used, 1)
                    else:
                        v.scalar_tensor_tensor(out=x[:, t, :], in0=acc[:, t, :], scalar=update, in1=x[:, t, :],
                                               op0=ALU.mult, op1=ALU.add).then_inc(acc_used, 1)
                v.drain()
            if ln:
                for t in range(TILES):
                    for h in range(2):
                        v.bn_stats(stat[:, t, 6 * h:6 * h + 6], x[:, t, 512 * h:512 * h + 512])
                v.drain()
                for t in range(TILES):
                    last = v.bn_aggr(lead[:, t, 0:2], stat[:, t, 0:12])
                last.then_inc(var_ready, 1)
                v.wait_ge(rowv_full, 16 * (u.rowv + 1))
                u.rowv += 1
                v.drain()
                for t in range(TILES):
                    v.scalar_tensor_tensor(out=x[:, t, :], in0=x[:, t, :], scalar=lead[:, t, 0:1],
                                           in1=rowv[:, 0, :], op0=ALU.subtract, op1=ALU.mult)
                v.wait_ge(dev_ready, u.dev + 1)
                u.dev += 1
                v.reciprocal(lead[:, :, 3:4], lead[:, :, 2:3])
                v.drain()
                for t in range(TILES):
                    v.scalar_tensor_tensor(out=x[:, t, :], in0=x[:, t, :], scalar=lead[:, t, 3:4],
                                           in1=rowv[:, 1, :], op0=ALU.mult, op1=ALU.add)\
                     .then_inc(var_ready if rms else rows_ready, 1)
                v.drain()
                v.sem_inc(rowv_used, 1)
            rows = x
            if rms:
                rows = hn
                for t in range(TILES):
                    v.wait_ge(dev_ready, u.dev + 1)
                    u.dev += 1
                    v.reciprocal(lead[:, t, 3:4], lead[:, t, 2:3])
                    v.drain()
                    v.tensor_scalar(hn[:, t, :], x[:, t, :], lead[:, t, 3:4], None, ALU.mult)\
                     .then_inc(rows_ready, 1)
            if not turn:
                v.drain()
                return
            for side in range(2 if flip else 1):
                x_hi, x_lo = ((xT_hi, xT_lo), (xTr_hi, xTr_lo))[side]
                for b in range(4):
                    u.turned += 1
                    v.wait_ge(turned_high, u.turned)
                    for c in range(2):
                        lo, hi = x_lo[:, 2 * b + c, :], x_hi[:, 2 * b + c, :].bitcast(F32)
                        src = psum[:, b, c * SEQ:(c + 1) * SEQ]
                        if gain is None:
                            last = v.tensor_tensor(lo, src, hi, ALU.subtract)
                        else:
                            last = v.scalar_tensor_tensor(out=lo, in0=src, scalar=gain[:, 2 * b + c:2 * b + c + 1],
                                                          in1=hi, op0=ALU.mult, op1=ALU.subtract)
                    last.then_inc(turned_used, 1)

        def act_norm(ln=False, rms=False, gain=None, turn=True, flip=False):
            u = act_u
            if ln:
                nc.scalar.wait_ge(var_ready, u.var + 1)
                u.var += 1
                nc.scalar.activation(lead[:, :, 2:3], lead[:, :, 1:2], ACT.Sqrt, bias=eps["ln"]).then_inc(dev_ready, 1)
            if rms:
                for t in range(TILES):
                    if ln:
                        nc.scalar.wait_ge(var_ready, u.var + 1)
                        u.var += 1
                    else:
                        nc.scalar.wait_ge(acc_used, 2 * u.acc + t + 1)
                    nc.scalar.activation(hn[:, t, :], x[:, t, :], ACT.Square, accum_out=lead[:, t, 0:1])
                    nc.scalar.drain()
                    nc.scalar.activation(lead[:, t, 2:3], lead[:, t, 0:1], ACT.Sqrt, bias=eps["rms"],
                                         scale=1.0 / D).then_inc(dev_ready, 1)
            if ln or rms:
                u.acc += 1
            for side in range((2 if flip else 1) if turn else 0):
                x_hi = (xT_hi, xTr_hi)[side]
                for b in range(4):
                    u.turned += 1
                    nc.scalar.wait_ge(turned, u.turned)
                    if gain is None:
                        last = nc.scalar.copy(x_hi[:, 2 * b:2 * b + 2, :].rearrange("p c n -> p (c n)"), psum[:, b, :])
                    else:
                        for c in range(2):
                            last = nc.scalar.activation(x_hi[:, 2 * b + c, :], psum[:, b, c * SEQ:(c + 1) * SEQ],
                                                        ACT.Copy, scale=gain[:, 2 * b + c:2 * b + c + 1])
                    last.then_inc(turned_high, 1)

        def pe_turn(rows, flip=False, counted=True):
            u = pe_u
            for side in range(2 if flip else 1):
                for t in range(TILES):
                    if counted and side == 0:
                        u.rows += 1
                        nc.tensor.wait_ge(rows_ready, u.rows)
                    for b in range(4):
                        if side and t == 0:
                            nc.tensor.wait_ge(turned_used, u.turned - 3 + b)
                        for c in range(2):
                            src = rows[:, t, (2 * b + c) * P:(2 * b + c + 1) * P]
                            dst = psum[:, b, c * SEQ + t * P:c * SEQ + (t + 1) * P]
                            if side:
                                dst = psum[:, b, c * SEQ + (1 - t) * P:c * SEQ + (2 - t) * P]
                                last = nc.tensor.matmul(dst, src, T["flip"], start=True, stop=True)
                            else:
                                last = nc.tensor.transpose(dst, src, T["ident"])
                        if t == TILES - 1:
                            last.then_inc(turned, 1)
                u.turned += 4

        def pe_project(ready, value):
            nc.tensor.wait_ge(ready, value)
            for u, (s, _) in enumerate(pe_ring.take(4)):
                nc.tensor.wait_ge(low_ready, pe_ring.units - 3 + u)
                nc.tensor.wait_ge(o_low, pe_u.o + u + 1)
                if u == 0 and pe_u.acc:
                    nc.tensor.wait_ge(acc_used, 2 * pe_u.acc)
                for c in range(2):
                    k = 2 * u + c
                    for t in range(TILES):
                        tok = slice(t * P, (t + 1) * P)
                        for n in range(2):
                            cols = slice(c * D + n * 512, c * D + (n + 1) * 512)
                            last = products(psum[:, 4 + 2 * t + n, :], xT_hi[:, k, tok], xT_lo[:, k, tok],
                                            ring_hi[:, s, cols], ring_lo[:, s, cols],
                                            start=(k == 0), stop=(k == KC - 1))
                last.then_inc(ring_free[s], 1)
            pe_u.o += 4
            end_project()

        def pe_project_whole(ready, value):
            nc.tensor.wait_ge(ready, value)
            for u, (s, turn) in enumerate(pe_ring.take(4, parts=False)):
                nc.tensor.wait_ge(ring_full[s], 16 * (turn + 1))
                if u == 0:
                    nc.tensor.wait_ge(acc_used, 2 * pe_u.acc)
                for c in range(2):
                    k = 2 * u + c
                    for t in range(TILES):
                        for n in range(2):
                            last = nc.tensor.matmul(
                                psum[:, 4 + 2 * t + n, :], oT[:, k, t * P:(t + 1) * P],
                                ring[:, s, c * D + n * 512:c * D + (n + 1) * 512],
                                start=(k == 0), stop=(k == KC - 1))
                last.then_inc(ring_free[s], 1)
            end_project()

        def end_project():
            nc.tensor.matmul(psum[0:1, 0, 0:1], zero[:, 0:1], zero[:, 0:1], start=True, stop=True)\
              .then_inc(acc_ready, 1)
            pe_u.acc += 1

        def act_output(u, ready, value):
            nc.scalar.wait_ge(ready, value)
            nc.scalar.copy(xT_hi[:, 2 * u:2 * u + 2, :], oT[:, 2 * u:2 * u + 2, :]).then_inc(o_high, 1)
            act_u.o += 1

        def dve_output(u):
            dve_u.o += 1
            nc.vector.wait_ge(o_high, dve_u.o)
            nc.vector.tensor_tensor(xT_lo[:, 2 * u:2 * u + 2, :], oT[:, 2 * u:2 * u + 2, :],
                                    xT_hi[:, 2 * u:2 * u + 2, :].bitcast(F32), ALU.subtract).then_inc(o_low, 1)

        glu_done = {"pe": 0, "act": 0, "dve": 0}

        def steps(engine, n, body):
            turns, rest = divmod(n, SLOTS)
            with engine.Fori(0, turns) as i:
                for j in range(SLOTS):
                    body(i, j)
            for j in range(rest):
                body(0, turns * SLOTS + j)

        def pe_glu(chunks):
            base, s0, units = glu_done["pe"], pe_ring.next, pe_ring.units

            def gates(i, j):
                s = (s0 + j) % SLOTS
                nc.tensor.wait_ge(low_ready, i * SLOTS + (units + j + 1))
                for part in range(2):
                    for k in range(KC):
                        cols = slice(part * D + k * P, part * D + (k + 1) * P)
                        last = products(psum[:, j % SLOTS, part * SEQ:(part + 1) * SEQ],
                                        ring_hi[:, s, cols], ring_lo[:, s, cols], xT_hi[:, k, :], xT_lo[:, k, :],
                                        start=(k == 0), stop=(k == KC - 1))
                last.then_inc(gate_up, 1)

            def down(i, j):
                s = (s0 + j) % SLOTS
                nc.tensor.wait_ge(hidden_ready, i * SLOTS + (base + j + 1))
                for t in range(TILES):
                    tok = slice(t * P, (t + 1) * P)
                    for h in range(2):
                        cols = slice(2 * D + h * 512, 2 * D + (h + 1) * 512)
                        last = products(psum[:, 4 + 2 * t + h, :], glu_hi[:, j % SLOTS, tok], glu_lo[:, j % SLOTS, tok],
                                        ring_hi[:, s, cols], ring_lo[:, s, cols],
                                        start=False, stop=False, skip_group_check=True)
                last.then_inc(ring_free[s], 1)

            def step(i, j):
                gates(i, j + 1)
                down(i, j)

            if pe_u.acc:
                nc.tensor.wait_ge(acc_used, 2 * pe_u.acc)
            for b in range(4):
                nc.tensor.matmul(psum[:, 4 + b, :], zero[:, 0:P], zero[:, 0:512], start=True, stop=False)
            gates(0, 0)
            steps(nc.tensor, chunks - 1, step)
            down(0, chunks - 1)
            for b in range(4):
                last = nc.tensor.matmul(psum[:, 4 + b, :], zero[:, 0:P], zero[:, 0:512], start=False, stop=True)
            last.then_inc(acc_ready, 1)
            pe_ring.take(chunks)
            pe_u.acc += 1
            glu_done["pe"] += chunks

        def act_glu(chunks, more=True):
            base = glu_done["act"]

            def silu(i, j):
                b = j % SLOTS
                nc.scalar.wait_ge(gate_up, i * SLOTS + (base + j + 1))
                nc.scalar.activation(glu_s[:, b, :], psum[:, b, 0:SEQ], ACT.Silu).then_inc(silu_ready, 1)

            def step(i, j):
                silu(i, j)
                act_split(j + 2, i)

            steps(nc.scalar, chunks - 2, step)
            silu(0, chunks - 2)
            act_ring.take(chunks)
            if more:
                act_split(0)
            silu(0, chunks - 1)
            if more:
                act_split(1)
            glu_done["act"] += chunks

        def dve_glu(chunks, weighted, more=True):
            base, v = glu_done["dve"], nc.vector

            def hidden(i, j):
                b = j % SLOTS
                v.wait_ge(silu_ready, i * SLOTS + (base + j + 1))
                v.tensor_tensor(glu_t[:, b, :], psum[:, b, SEQ:2 * SEQ], glu_s[:, b, :], ALU.mult)
                v.drain()
                if weighted:
                    w = route_w[:, bass.ds(i * (SLOTS // 2) + j // 2, 1), :].rearrange("p o n -> p (o n)")
                    v.tensor_tensor(glu_t[:, b, :], glu_t[:, b, :], w, ALU.mult)
                    v.drain()
                v.tensor_copy(glu_hi[:, b, :], glu_t[:, b, :])
                v.drain()
                v.tensor_tensor(glu_lo[:, b, :], glu_t[:, b, :], glu_hi[:, b, :].bitcast(F32), ALU.subtract)\
                 .then_inc(hidden_ready, 1)

            def step(i, j):
                hidden(i, j)
                dve_split(j + 2, i)

            steps(v, chunks - 2, step)
            hidden(0, chunks - 2)
            dve_ring.take(chunks)
            if more:
                dve_split(0)
            hidden(0, chunks - 1)
            if more:
                dve_split(1)
            glu_done["dve"] += chunks

        R = lambda at, *shape: rt[:, at:at + int(np.prod(shape))].rearrange(
            "p (" + " ".join("abcd"[:len(shape)]) + ") -> p " + " ".join("abcd"[:len(shape)]),
            **{n: s for n, s in zip("bcd"[:len(shape) - 1], shape[1:])}) if len(shape) > 1 else rt[:, at:at + shape[0]]
        G4 = TILES * 4
        score = R(0, TILES, EXPERTS)
        biased = R(32, TILES, EXPERTS)
        b_grp = R(32, G4, 4)
        later_ge, later_gt = R(64, G4, 4, 4), R(192, G4, 4, 4)
        rank = R(320, G4, 4)
        pair_sum = R(352, G4, 6)
        best2 = R(400, G4)
        g_ge, g_gt = R(408, TILES, 4, 4), R(440, TILES, 4, 4)
        g_rank = R(472, TILES, 4)
        chosen = R(480, G4, 4)
        gate_w = R(512, TILES, EXPERTS)
        gate_sum = R(544, TILES)
        gateT = rt[:, 560:560 + SEQ]

        def pe_router(l):
            if l == 0:
                nc.tensor.wait_ge(router_loaded, 32)
                nc.tensor.wait_ge(early_loaded, 48)
            for t in range(TILES):
                for k in range(KC):
                    if t == 0 and k == 0:
                        nc.tensor.wait_ge(turned_used, pe_u.turned)
                    for part, half in enumerate((xT_hi, xT_lo)):
                        last = nc.tensor.matmul(psum[:, 0, t * EXPERTS:(t + 1) * EXPERTS],
                                                half[:, k, t * P:(t + 1) * P].bitcast(F32), router_w[:, k, :],
                                                start=(k == 0 and part == 0), stop=(k == KC - 1 and part == 1))
            last.then_inc(logits_ready, 1)
            nc.tensor.wait_ge(gates_ready, l + 1)
            for t in range(TILES):
                last = nc.tensor.transpose(psum[0:EXPERTS, 1, t * P:(t + 1) * P], gate_w[:, t, :], T["ident"])
            last.then_inc(gatesT_ready, 1)
            nc.tensor.wait_ge(gatesT_copied, l + 1)
            for e in range(EXPERTS):
                if e >= 8 and e % 4 == 0:
                    nc.tensor.wait_ge(spread_copied, 8 * l + e // 2 - 2)
                last = nc.tensor.matmul(psum[:, e // 2 % 4, e % 2 * SEQ:(e % 2 + 1) * SEQ],
                                        pick[0:EXPERTS, e, :], gateT[0:EXPERTS, :], start=True, stop=True)
                if e % 2:
                    last.then_inc(spread_ready, 1)
            nc.tensor.wait_ge(spread_copied, 8 * l + EXPERTS // 2)

        def act_router(l):
            nc.scalar.wait_ge(logits_ready, l + 1)
            nc.scalar.activation(score, psum[:, 0, 0:TILES * EXPERTS].rearrange("p (t e) -> p t e", t=TILES),
                                 ACT.Sigmoid).then_inc(router_sig, 1)

        def dve_router(l):
            v = nc.vector
            v.wait_ge(router_sig, l + 1)
            if l == 0:
                v.wait_ge(router_loaded, 32)
            v.tensor_tensor(biased, score, router_b.unsqueeze(1).broadcast_to([P, TILES, EXPERTS]), ALU.add)
            v.drain()
            other = b_grp.unsqueeze(2).broadcast_to([P, G4, 4, 4])
            own = b_grp.unsqueeze(3).broadcast_to([P, G4, 4, 4])
            before = T["before"].rearrange("p (i j) -> p i j", i=4).unsqueeze(1)
            v.tensor_tensor(later_ge, other, own, ALU.is_ge)
            v.tensor_tensor(later_gt, other, own, ALU.is_gt)
            n = 0
            for i in range(4):
                for j in range(i + 1, 4):
                    v.tensor_tensor(pair_sum[:, :, n:n + 1], b_grp[:, :, i:i + 1], b_grp[:, :, j:j + 1], ALU.add)
                    n += 1
            v.drain()
            v.tensor_tensor(later_ge, later_ge, later_gt, ALU.subtract)
            v.tensor_reduce(best2, pair_sum, AX_X, ALU.max)
            v.drain()
            v.tensor_tensor(later_ge, later_ge, before.broadcast_to([P, G4, 4, 4]), ALU.mult)
            g_own = best2.rearrange("p (t g) -> p t g", t=TILES)
            v.tensor_tensor(g_ge, g_own.unsqueeze(2).broadcast_to([P, TILES, 4, 4]),
                            g_own.unsqueeze(3).broadcast_to([P, TILES, 4, 4]), ALU.is_ge)
            v.tensor_tensor(g_gt, g_own.unsqueeze(2).broadcast_to([P, TILES, 4, 4]),
                            g_own.unsqueeze(3).broadcast_to([P, TILES, 4, 4]), ALU.is_gt)
            v.drain()
            v.tensor_tensor(later_ge, later_ge, later_gt, ALU.add)
            v.tensor_tensor(g_ge, g_ge, g_gt, ALU.subtract)
            v.drain()
            v.tensor_reduce(rank, later_ge, AX_X, ALU.add)
            v.tensor_tensor(g_ge, g_ge, before.broadcast_to([P, TILES, 4, 4]), ALU.mult)
            v.drain()
            v.tensor_tensor(g_ge, g_ge, g_gt, ALU.add)
            v.drain()
            v.tensor_reduce(g_rank, g_ge, AX_X, ALU.add)
            v.drain()
            v.tensor_scalar(g_rank, g_rank, 0.5, None, ALU.is_lt)
            v.drain()
            v.scalar_tensor_tensor(out=chosen, in0=rank, scalar=1.5,
                                   in1=g_rank.rearrange("p t g -> p (t g)").unsqueeze(2).broadcast_to([P, G4, 4]),
                                   op0=ALU.is_lt, op1=ALU.mult)
            v.drain()
            v.tensor_tensor(gate_w, score, chosen.rearrange("p (t g) e -> p t (g e)", t=TILES), ALU.mult)
            v.drain()
            v.tensor_reduce(gate_sum, gate_w, AX_X, ALU.add)
            v.drain()
            v.reciprocal(gate_sum, gate_sum)
            v.drain()
            v.tensor_tensor(gate_w, gate_w, gate_sum.unsqueeze(2).broadcast_to([P, TILES, EXPERTS]), ALU.mult)\
             .then_inc(gates_ready, 1)
            v.wait_ge(gatesT_ready, l + 1)
            v.tensor_copy(gateT[0:EXPERTS, :], psum[0:EXPERTS, 1, 0:SEQ]).then_inc(gatesT_copied, 1)
            for b in range(EXPERTS // 2):
                v.wait_ge(spread_ready, 8 * l + b + 1)
                v.tensor_copy(route_w[:, 2 * b:2 * b + 2, :], psum[:, b % 4, :].rearrange("p (e n) -> p e n", e=2))\
                 .then_inc(spread_copied, 1)

        def width(t):
            return P * (t + 1)

        def pe_dilated():
            pe = nc.tensor

            def project_qk(p, g, par, turn):
                pe.wait_ge(low_ready, 3 * p + (3 * turn + g + 1))
                if not (isinstance(p, int) and p == 0 and g == 0):
                    pe.wait_ge(qk_copied, 3 * p + g)
                for part in range(2):
                    for k in range(KC):
                        cols = slice(k * 384 + part * P, k * 384 + (part + 1) * P)
                        last = products(psum[:, 0, part * SEQ:(part + 1) * SEQ], ring_hi[:, g, cols],
                                        ring_lo[:, g, cols], xT_hi[:, k, :], xT_lo[:, k, :],
                                        start=(k == 0), stop=(k == KC - 1))
                last.then_inc(qk_ready, 1)

            def project_v(p, g, par):
                if not (isinstance(p, int) and p == 0 and g == 0):
                    pe.wait_ge(v_copied, 3 * p + g)
                for t in range(TILES):
                    for k in range(KC):
                        tok, cols = slice(t * P, (t + 1) * P), slice(k * 384 + 2 * P, k * 384 + 3 * P)
                        last = products(psum[:, 1, tok], xT_hi[:, k, tok], xT_lo[:, k, tok],
                                        ring_hi[:, g, cols], ring_lo[:, g, cols],
                                        start=(k == 0), stop=(k == KC - 1))
                last.then_inc(v_ready, 1)

            def scores(p, u, par):
                a, t = divmod(u, 2)
                if u == 0:
                    pe.wait_ge(qk_copied, 3 * p + 3)
                if u >= 2 or not isinstance(p, int) or p:
                    pe.wait_ge(max_ready, 4 * p + u - 1)
                for g in range(GROUPS):
                    dst = psum[:, 4, g * P:(g + 1) * P] if t == 0 else psum[:, 2 + g // 2, g % 2 * SEQ:(g % 2 + 1) * SEQ]
                    last = pe.matmul(dst, qk_sb[a * HD:(a + 1) * HD, par, g, t * P:(t + 1) * P],
                                     qk_sb[a * HD:(a + 1) * HD, par, g, SEQ:SEQ + width(t)], start=True, stop=True)
                last.then_inc(scores_ready, 1)

            def turn_probs(p, u, par):
                a, t = divmod(u, 2)
                pe.wait_ge(probs_ready, 4 * p + u + 1)
                for b in range(GROUPS * (t + 1)):
                    last = pe.transpose(psum[:, 5 + b // 4, b % 4 * P:(b % 4 + 1) * P],
                                        probs[:, a, (3 * t + b) * P:(3 * t + b + 1) * P], T["ident"])
                last.then_inc(probsT_ready, 1)

            def weigh(p, u, par):
                a, t = divmod(u, 2)
                if u == 0:
                    pe.wait_ge(v_copied, 3 * p + 3)
                    if not isinstance(p, int) or p:
                        pe.wait_ge(o_copied, p)
                pe.wait_ge(probsT_copied, 4 * p + u + 1)
                n = GROUPS * (t + 1)
                for b in range(n):
                    g, kt = divmod(b, t + 1)
                    last = pe.matmul(psum[a * HD:(a + 1) * HD, 7, t * P:(t + 1) * P],
                                     v_sb[:, par, g, kt * P + a * HD:kt * P + (a + 1) * HD],
                                     probsT[:, a, (3 * t + b) * P:(3 * t + b + 1) * P],
                                     start=(b == 0), stop=(b == n - 1))
                if u == 3:
                    last.then_inc(o_ready, 1)

            def body(p, par, more):
                qk = lambda g: more and project_qk(p + 1, g, 1 - par, 0)
                vv = lambda g: more and project_v(p + 1, g, 1 - par)
                scores(p, 0, par); scores(p, 1, par); qk(0)
                turn_probs(p, 0, par); scores(p, 2, par); vv(0)
                weigh(p, 0, par); turn_probs(p, 1, par); qk(1)
                scores(p, 3, par); weigh(p, 1, par); turn_probs(p, 2, par); vv(1)
                weigh(p, 2, par); qk(2)
                turn_probs(p, 3, par); vv(2); weigh(p, 3, par)

            pe.wait_ge(turned_used, pe_u.turned)
            for g in range(GROUPS):
                project_qk(0, g, 0, 0)
                project_v(0, g, 0)
            body(0, 0, True)
            body(1, 1, True)
            with pe.Fori(1, PAIRS // 2 - 1) as i:
                body(i * 2, 0, True)
                body(i * 2 + 1, 1, True)
            body(PAIRS - 2, 0, True)
            body(PAIRS - 1, 1, False)
            pe_ring.skip(range(GROUPS), PAIRS)
            pe_ring.units += GROUPS * PAIRS

        def loop_pairs(engine, body):
            body(0, 0, True, True)
            body(1, 1, True, True)
            with engine.Fori(1, PAIRS // 2 - 1) as i:
                body(i * 2, 0, True, True)
                body(i * 2 + 1, 1, True, True)
            body(PAIRS - 2, 0, True, False)
            body(PAIRS - 1, 1, False, False)

        def unit_cols(t):
            return slice(3 * P * t, 3 * P * t + GROUPS * width(t))

        def dve_dilated():
            v = nc.vector

            def take_v(p, g, par):
                v.wait_ge(v_ready, 3 * p + g + 1)
                v.tensor_copy(v_sb[:, par, g, :], psum[:, 1, 0:SEQ]).then_inc(v_copied, 1)

            def biased_max(p, u, par):
                a, t = divmod(u, 2)
                if u == 0:
                    v.wait_ge(bias_full[par], bias_count(p, par))
                v.wait_ge(scores_ready, 4 * p + u + 1)
                v.memset(soft[:, u, 3:4], 0.0)
                if t == 0:
                    src = psum[:, 4, 0:3 * P].rearrange("p (g c) -> p g c", g=GROUPS)
                    bias = bias_sb[:, par, a, :].rearrange("p (g c) -> p g c", g=GROUPS)[:, :, P:SEQ]
                else:
                    src = psum[:, 2:4, :].rearrange("p b c -> p (b c)")[:, 0:3 * SEQ]
                    bias = bias_sb[:, par, a, :]
                dst = probs[:, a, unit_cols(t)]
                if t == 0:
                    dst = dst.rearrange("p (g c) -> p g c", g=GROUPS)
                v.tensor_tensor_reduce(dst, src, bias, 0.125, NEG * 4, ALU.add, ALU.max, soft[:, u, 0:1])
                v.drain()
                v.tensor_scalar(soft[:, u, 1:2], soft[:, u, 0:1], -1.0, None, ALU.mult).then_inc(max_ready, 1)

            def normalise(p, u, par):
                a, t = divmod(u, 2)
                v.wait_ge(exp_ready, 4 * p + u + 1)
                v.reciprocal(soft[:, u, 3:4], soft[:, u, 2:3])
                v.drain()
                v.tensor_scalar(probs[:, a, unit_cols(t)], probs[:, a, unit_cols(t)], soft[:, u, 3:4], None,
                                ALU.mult).then_inc(probs_ready, 1)

            def split(p, g):
                v.wait_ge(high_ready, 3 * p + (g + 1))
                v.tensor_tensor(ring_lo[:, g, :], ring[:, g, :], ring_hi[:, g, :].bitcast(F32), ALU.subtract)\
                 .then_inc(low_ready, 1)

            def body(p, par, more, more2):
                vv = lambda g: more and take_v(p + 1, g, 1 - par)
                biased_max(p, 0, par); biased_max(p, 1, par)
                normalise(p, 0, par); normalise(p, 1, par); more and split(p + 1, 1)
                biased_max(p, 2, par); vv(0); normalise(p, 2, par); more and split(p + 1, 2)
                biased_max(p, 3, par); vv(1); normalise(p, 3, par); more2 and split(p + 2, 0); vv(2)
                if not more:
                    for u in range(3):
                        dve_split(u, floats=2 * D)
                        dve_output(u)
                v.wait_ge(o_ready, p + 1)
                dst = oT[:, bass.ds(p, 1), :].rearrange("p o (t n) -> p (o t) n", t=TILES)
                v.tensor_copy(dst, psum[:, 7, 0:SEQ].rearrange("p (t n) -> p t n", t=TILES)[:, :, ::-1])\
                 .then_inc(o_copied, 1)

            for g in range(GROUPS):
                split(0, g)
            for g in range(GROUPS):
                take_v(0, g, 0)
            split(1, 0)
            dve_ring.skip(range(GROUPS), PAIRS)
            dve_ring.units += GROUPS * PAIRS
            loop_pairs(v, body)
            dve_split(3, floats=2 * D)
            dve_output(3)
            dve_ring.take(4)

        def bias_count(p, par):
            if isinstance(p, int):
                return 32 * (p // 2 + 1)
            return p * 16 + (32 if par == 0 else 16)

        def act_dilated():
            act = nc.scalar

            def take_qk(p, g, par):
                act.wait_ge(qk_ready, 3 * p + g + 1)
                act.copy(qk_sb[:, par, g, 0:SEQ].rearrange("p (t n) -> p t n", t=TILES),
                         psum[:, 0, 0:SEQ].rearrange("p (t n) -> p t n", t=TILES)[:, :, ::-1])
                act.copy(qk_sb[:, par, g, SEQ:2 * SEQ], psum[:, 0, SEQ:2 * SEQ]).then_inc(qk_copied, 1)

            def exps(p, u, par):
                a, t = divmod(u, 2)
                act.wait_ge(max_ready, 4 * p + u + 1)
                act.activation(probs[:, a, unit_cols(t)], probs[:, a, unit_cols(t)], ACT.Exp,
                               bias=soft[:, u, 1:2], accum_out=soft[:, u, 2:3]).then_inc(exp_ready, 1)

            def take_probs(p, u, par):
                a, t = divmod(u, 2)
                act.wait_ge(probsT_ready, 4 * p + u + 1)
                src = psum[:, 5:7, :].rearrange("p b c -> p (b c)")[:, 0:GROUPS * width(t)]
                act.copy(probsT[:, a, unit_cols(t)], src).then_inc(probsT_copied, 1)

            def split(p, g):
                act.wait_ge(ring_full[g], 16 * p + 16)
                act.copy(ring_hi[:, g, :], ring[:, g, :]).then_inc(high_ready, 1)

            def body(p, par, more, more2):
                qk = lambda g: more and take_qk(p + 1, g, 1 - par)
                exps(p, 0, par); exps(p, 1, par); more and split(p + 1, 1); qk(0)
                take_probs(p, 0, par); exps(p, 2, par); take_probs(p, 1, par); more and split(p + 1, 2); qk(1)
                take_probs(p, 2, par); exps(p, 3, par); more2 and split(p + 2, 0); qk(2)
                if not more:
                    for u in range(3):
                        act_split(u, floats=2 * D)
                        act_output(u, v_copied, GROUPS * PAIRS)
                take_probs(p, 3, par)

            for g in range(GROUPS):
                split(0, g)
            for g in range(GROUPS):
                take_qk(0, g, 0)
            split(1, 0)
            act_ring.skip(range(GROUPS), PAIRS)
            act_ring.units += GROUPS * PAIRS
            loop_pairs(act, body)
            act_split(3, floats=2 * D)
            act_output(3, o_copied, PAIRS)
            act_ring.take(4)

        def pool_rows(n, rows=2):
            if n:
                nc.gpsimd.wait_ge(rowv_used, n)
            nc.gpsimd.dma_start(rowv[:, 0:rows, :], d["row_vectors"][2 * n:2 * n + rows].partition_broadcast(P))\
                .then_inc(rowv_full, 16)

        def pool_bias():
            pool = nc.gpsimd
            pool.wait_ge(rel_stored, 16)

            def load(p, par):
                for a in range(2):
                    src = bass.AP(tensor=rel_dram.tensor, offset=p * (2 * GROUPS * 3 * P) + a * GROUPS * 3 * P,
                                  ap=[[1, P], [3 * P, GROUPS], [1, SEQ]])
                    pool.dma_start(bias_sb[:, par, a, :].rearrange("p (g c) -> p g c", g=GROUPS), src)\
                        .then_inc(bias_full[par], 16)

            load(0, 0)
            load(1, 1)
            with pool.Fori(1, PAIRS // 2) as i:
                for par in range(2):
                    pool.wait_ge(max_ready, i * 8 + 4 * (par - 1))
                    load(i * 2 + par, par)

        def pe_sticks():
            pe = nc.tensor
            units = pe_ring.units
            slots = pe_ring.take(PAIRS)[:SLOTS]

            def project_qk(p):
                s, _ = slots[p % SLOTS]
                pe.wait_ge(low_ready, units + p + 1)
                if not (isinstance(p, int) and p == 0):
                    pe.wait_ge(sb_qk_copied, p)
                for part, (hi, lo) in enumerate(((xT_hi, xT_lo), (xTr_hi, xTr_lo))):
                    for k in range(KC):
                        cols = slice(k * 384 + part * P, k * 384 + (part + 1) * P)
                        last = products(psum[:, 0, part * SEQ:(part + 1) * SEQ], ring_hi[:, s, cols],
                                        ring_lo[:, s, cols], hi[:, k, :], lo[:, k, :],
                                        start=(k == 0), stop=(k == KC - 1))
                last.then_inc(sb_qk_ready, 1)

            def project_v(p):
                s, _ = slots[p % SLOTS]
                if not (isinstance(p, int) and p == 0):
                    pe.wait_ge(sb_v_copied, p)
                for t in range(TILES):
                    for k in range(KC):
                        tok, cols = slice(t * P, (t + 1) * P), slice(k * 384 + 2 * P, k * 384 + 3 * P)
                        last = products(psum[:, 1, tok], xTr_hi[:, k, tok], xTr_lo[:, k, tok],
                                        ring_hi[:, s, cols], ring_lo[:, s, cols],
                                        start=(k == 0), stop=(k == KC - 1))
                last.then_inc(sb_v_ready, 1)

            def scores(p, a):
                par = p % 2
                if a == 0:
                    pe.wait_ge(sb_qk_copied, p + 1)
                q, k = sb_qk[a * HD:(a + 1) * HD, par, 0:SEQ], sb_qk[a * HD:(a + 1) * HD, par, SEQ:2 * SEQ]
                if p:
                    pe.wait_ge(sb_clipped, p * 2 + a - 1)
                first = pe.matmul(psum[:, 2 + a, 0:P], q[:, 0:P], k[:, P:SEQ], start=True, stop=True)
                if a == 0:
                    first.then_inc(ring_free[slots[p % SLOTS][0]], 1)
                pe.matmul(psum[:, 2 + a, P:3 * P], q[:, P:SEQ], k, start=True, stop=True).then_inc(sb_scores, 1)

            def turn_att(p, a):
                pe.wait_ge(sb_att, p * 2 + (a + 1))
                for b in range(3):
                    last = pe.transpose(psum[:, 4 + a, b * P:(b + 1) * P], sb_a2[p % 2][:, a, b * P:(b + 1) * P], T["ident"])
                last.then_inc(sb_aT_ready, 1)

            def weigh(p, a):
                par = p % 2
                if a == 0:
                    pe.wait_ge(sb_v_copied, p + 1)
                    if not isinstance(p, int) or p:
                        pe.wait_ge(sb_o_copied, p)
                pe.wait_ge(sb_aT_copied, p * 2 + (a + 1))
                for t, blocks in enumerate((((0, 1),), ((1, 0), (2, 1)))):
                    for n, (b, kt) in enumerate(blocks):
                        last = pe.matmul(psum[a * HD:(a + 1) * HD, 7, t * P:(t + 1) * P],
                                         sb_v[:, par, kt * P + a * HD:kt * P + (a + 1) * HD],
                                         sb_aT[:, a, b * P:(b + 1) * P], start=(n == 0), stop=(n == len(blocks) - 1))
                if a == 1:
                    last.then_inc(sb_o_ready, 1)

            pe.wait_ge(turned_used, pe_u.turned)
            for p in range(2):
                project_qk(p)
                project_v(p)
            scores(0, 0); scores(0, 1)
            for p in range(PAIRS):
                if p + 1 < PAIRS:
                    scores(p + 1, 0); scores(p + 1, 1)
                turn_att(p, 0); turn_att(p, 1)
                if p + 2 < PAIRS:
                    project_qk(p + 2)
                weigh(p, 0); weigh(p, 1)
                if p + 2 < PAIRS:
                    project_v(p + 2)

        def dve_sticks():
            v = nc.vector

            def take_v(p, par):
                v.wait_ge(sb_v_ready, p + 1)
                v.tensor_copy(sb_v[:, par, :], psum[:, 1, 0:SEQ]).then_inc(sb_v_copied, 1)

            def clip(p, a):
                v.wait_ge(sb_scores, p * 2 + (a + 1))
                z, sb_a = sb_z[:, a, :], sb_a2[p % 2]
                v.tensor_scalar(z, psum[:, 2 + a, 0:3 * P], 0.125, SB_CLIP, ALU.mult, ALU.min)
                v.drain()
                v.tensor_scalar(z, z, -SB_CLIP, None, ALU.max)
                v.drain()
                v.scalar_tensor_tensor(out=sb_a[:, a, :], in0=z, scalar=-1.0, in1=z, op0=ALU.mult, op1=ALU.min)\
                 .then_inc(sb_clipped, 1)

            mask = T["sb_mask"].unsqueeze(1).broadcast_to([P, 2, P])

            def own(buf, a):
                return buf[:, a, 0:2 * P].rearrange("p (b c) -> p b c", b=2)

            def suffix(p, a):
                v.wait_ge(sb_exp1, p * 2 + (a + 1))
                v.scalar_tensor_tensor(out=sb_p[:, a, :], in0=sb_z[:, a, :], scalar=0.0, in1=sb_a2[p % 2][:, a, :],
                                       op0=ALU.max, op1=ALU.add)
                v.drain()
                v.tensor_tensor(own(sb_p, a), own(sb_p, a), mask, ALU.mult)
                v.drain()
                v.tensor_tensor_scan(sb_r[:, a, 0:P], T["ones"][:, 0:P], sb_p[:, a, 0:P], 0.0, ALU.mult, ALU.add)
                v.tensor_tensor_scan(sb_r[:, a, P:3 * P], T["ones"], sb_p[:, a, P:3 * P], 0.0, ALU.mult, ALU.add)
                v.drain()
                v.tensor_tensor(sb_p[:, a, :], sb_z[:, a, :], sb_r[:, a, :], ALU.subtract).then_inc(sb_minus, 1)

            def strict(p, a):
                v.wait_ge(sb_exp2, p * 2 + (a + 1))
                att = own(sb_a2[p % 2], a)
                v.tensor_tensor(att, att, mask, ALU.mult).then_inc(sb_att, 1)

            def chain(p, low=None):
                clip(p, 0); clip(p, 1)
                if low is not None:
                    split(low)
                suffix(p, 0); suffix(p, 1); strict(p, 0); strict(p, 1)

            def split(u):
                dve_split(u, floats=UNIT if u < PAIRS else 2 * D)

            take_v(0, 0)
            split(2)
            take_v(1, 1)
            chain(0)
            for p in range(PAIRS):
                if p + 1 < PAIRS:
                    chain(p + 1, p + 3)
                else:
                    split(p + 3)
                    for u in range(3):
                        dve_output(u)
                v.wait_ge(sb_o_ready, p + 1)
                v.tensor_copy(oT[:, p, :], psum[:, 7, 0:SEQ]).then_inc(sb_o_copied, 1)
                if p + 2 < PAIRS:
                    take_v(p + 2, p % 2)
            dve_output(3)
            split(PAIRS + 3)
            dve_ring.take(PAIRS + 4)

        def act_sticks():
            act = nc.scalar

            def take_qk(p, par):
                act.wait_ge(sb_qk_ready, p + 1)
                act.copy(sb_qk[:, par, :], psum[:, 0, :]).then_inc(sb_qk_copied, 1)

            def logs(p):
                for func, bias in ((ACT.Exp, eps["zero"]), (ACT.Ln, eps["one"])):
                    for a in range(2):
                        if func == ACT.Exp:
                            act.wait_ge(sb_clipped, p * 2 + (a + 1))
                        z = sb_a2[p % 2][:, a, :]
                        last = act.activation(z, z, func, bias=bias)
                        if func == ACT.Ln:
                            last.then_inc(sb_exp1, 1)
                    act.drain()

            def weights(p):
                for a in range(2):
                    act.wait_ge(sb_minus, p * 2 + (a + 1))
                    act.activation(sb_a2[p % 2][:, a, :], sb_p[:, a, :], ACT.Exp).then_inc(sb_exp2, 1)

            def split(u):
                act_split(u, floats=UNIT if u < PAIRS else 2 * D)

            take_qk(0, 0)
            split(2)
            take_qk(1, 1)
            logs(0)
            split(3)
            weights(0)
            for p in range(PAIRS):
                if p + 1 < PAIRS:
                    logs(p + 1)
                for a in range(2):
                    act.wait_ge(sb_aT_ready, p * 2 + (a + 1))
                    act.copy(sb_aT[:, a, :], psum[:, 4 + a, 0:3 * P]).then_inc(sb_aT_copied, 1)
                if p + 1 < PAIRS:
                    weights(p + 1)
                if p + 2 < PAIRS:
                    take_qk(p + 2, p % 2)
                if p + 1 == PAIRS:
                    for u in range(3):
                        act_output(u, sb_o_copied, PAIRS - 1)
                split(p + 4)
            act_output(3, sb_o_copied, PAIRS)
            act_ring.take(PAIRS + 4)


        uT = carve(0, 28, SEQ)
        rope = carve(20736, 4, SEQ)
        B0 = 28 * SEQ
        pos_i = scratch[:, 0:SEQ].bitcast(I32)
        pos_f, ang, turns_n = carve(256, SEQ), carve(512, 4, SEQ), carve(1536, 4, SEQ)
        cv_u, cv_y, cv_t = carve(B0, 2, SEQ), carve(B0 + 512, 2, SEQ), carve(B0 + 1024, 2, SEQ)
        rt_r = carve(B0 + 1536, 4, SEQ)
        rt_t = carve(B0 + 2560, 4, SEQ)
        rt_v = carve(B0 + 3584, TILES, SEQ)
        rt_s = carve(B0 + 4096, MIX_HEADS, TILES, SEQ)
        rt_sq, rt_d, rt_g = carve(B0 + 6144, 2, SEQ), carve(B0 + 6656, 2, SEQ), carve(B0 + 7168, 2, SEQ)
        M0 = B0 + 7680
        ml_n = carve(M0, 4, SEQ)
        ml_d = carve(M0 + 1024, 2, SEQ)
        ml_q, ml_k = carve(M0 + 1536, MIX_HEADS, SEQ), carve(M0 + 2560, MIX_HEADS, SEQ)
        ml_t = carve(B0 + 2560, MIX_HEADS, SEQ)
        ml_kr = carve(B0, 2, SEQ)
        ml_v = carve(M0 + 3584, TILES, SEQ)
        ml_p = carve(B0 + 4096, MIX_HEADS, TILES, SEQ)
        ml_pT = carve(B0 + 1536, MIX_HEADS, TILES, SEQ)
        ml_m = carve(B0 + 3584, 4, 8)
        rw_mb = carve(B0, 16, 4 * P)
        rw_AR = carve(B0 + 8192, 4, TILES, 2, P)
        rw_B, rw_K = carve(B0 + 10240, 4, SEQ), carve(B0 + 11264, 4, SEQ)
        rw_g = carve(B0 + 12288, 2, SEQ)
        rw_y = carve(B0 + 12800, 2, SEQ)
        rw_T, rw_TT = carve(0, 16, P), carve(2048, 16, P)
        xT = place("xT_free", plan["xT_hi"], [P, KC, SEQ])
        rw_Y = xT[:].rearrange("p k n -> p (k n)").rearrange("p (i n) -> p i n", i=16)
        rw_BK = xT[:].rearrange("p k n -> p (k n)").rearrange("p (d t w n) -> p d t w n", d=4, t=TILES, w=2)
        rowf = rowv[:].rearrange("p k n -> p (k n)")
        rw_v = rowf[:, 0:512].rearrange("p (t n) -> p t n", t=TILES)
        rw_kk = rowf[:, 512:1024].rearrange("p (c n) -> p c n", c=2)
        rw_S = rowf[:, 1024:1536].rearrange("p (d n) -> p d n", d=4)
        rw_G = rowf[:, 1536:2048].rearrange("p (d n) -> p d n", d=4)
        rw_ks = uT[:, 16:18, :]
        rw_U = uT[:, U_WD:U_WD + 2, :].rearrange("p c n -> p (c n)").rearrange("p (d n) -> p d n", d=4)
        rw_Sc = carve(18 * SEQ, 4, HD)
        rw_PC = place("rw_PC", plan["PC"], [P, 4, 4])[:]
        rw_om = place("rw_om", plan["om"], [P, 2])[:]
        pr_lw, pr_a = carve(B0, 4, SEQ), carve(B0 + 1024, 4, SEQ)
        pr_L, pr_E1 = carve(B0 + 2048, 4, SEQ), carve(B0 + 3072, 4, SEQ)
        pr_E2, pr_E3 = carve(B0 + 4096, 4, SEQ), carve(B0 + 5120, 4, SEQ)
        pr_kd, pr_t = carve(B0 + 6144, 4, SEQ), carve(B0 + 7168, 4, SEQ)

        pos_loaded, ang_ready, rope_ready = sem("pos_loaded"), sem("ang_ready"), sem("rope_ready")
        small_loaded, small_used = sem("small_loaded"), sem("small_used")
        u_ready, u_copied_v, u_copied_a = sem("u_ready"), sem("u_copied_v"), sem("u_copied_a")
        rt_turned, rt_vT, rt_v_copied, rt_roped = sem("rt_turned"), sem("rt_vT"), sem("rt_v_copied"), sem("rt_roped")
        rt_scores, rt_decayed, rt_o, rt_squared = sem("rt_scores"), sem("rt_decayed"), sem("rt_o"), sem("rt_squared")
        rt_summed, rt_dev, rt_done = sem("rt_summed"), sem("rt_dev"), sem("rt_done")
        ml_squared, ml_summed, ml_dev, ml_normed = sem("ml_squared"), sem("ml_summed"), sem("ml_dev"), sem("ml_normed")
        ml_qkv, ml_q_copied, ml_kv_copied = sem("ml_qkv"), sem("ml_q_copied"), sem("ml_kv_copied")
        ml_turned, ml_roped, ml_scores = sem("ml_turned"), sem("ml_roped"), sem("ml_scores")
        ml_max, ml_exp, ml_probs, ml_pT_ready = sem("ml_max"), sem("ml_exp"), sem("ml_probs"), sem("ml_pT_ready")
        ml_pT_copied, ml_o, ml_done = sem("ml_pT_copied"), sem("ml_o"), sem("ml_done")
        rw_act, rw_pre, rw_sig, rw_kraw = sem("rw_act"), sem("rw_pre"), sem("rw_sig"), sem("rw_kraw")
        rw_ksq, rw_knorm, rw_kdev = sem("rw_ksq"), sem("rw_knorm"), sem("rw_kdev")
        rw_L, rw_exps, rw_prep = sem("rw_L"), sem("rw_exps"), sem("rw_prep")
        rw_mats, rw_masked, rw_N, rw_T0 = sem("rw_mats"), sem("rw_masked"), sem("rw_N"), sem("rw_T0")
        rw_Yr, rw_Yc, rw_Z, rw_ZT, rw_Tn = sem("rw_Yr"), sem("rw_Yc"), sem("rw_Z"), sem("rw_ZT"), sem("rw_Tn")
        rw_BKr, rw_BKc = sem("rw_BKr"), sem("rw_BKc")
        rw_Gr, rw_Gc_v, rw_Gc_a = sem("rw_Gr"), sem("rw_Gc_v"), sem("rw_Gc_a")
        rw_Ur, rw_Uc_v, rw_Uc_a = sem("rw_Ur"), sem("rw_Uc_v"), sem("rw_Uc_a")
        rw_yr, rw_Sr, rw_Sn = sem("rw_yr"), sem("rw_Sr"), sem("rw_Sn")
        rw_sum, rw_cent, rw_csq, rw_css, rw_cdev = sem("rw_sum"), sem("rw_cent"), sem("rw_csq"), sem("rw_css"), sem("rw_cdev")
        rw_done, rw_T0s = sem("rw_done"), sem("rw_T0s")
        final_ready = sem("final_ready")

        def both(buf):
            return buf.unsqueeze(1)

        def col(l, c, n=1):
            return vec[:, l, c:c + n]

        TWO_PI = 2 * np.pi
        C1 = 6.28125
        C2 = float(np.floor((TWO_PI - C1) * 2 ** 21) / 2 ** 21)
        C3 = float(TWO_PI - C1 - C2)
        ROUND = 1.5 * 2 ** 23

        def dve_rope_tables():
            v = nc.vector
            v.wait_ge(pos_loaded, 16)
            v.tensor_copy(pos_f, pos_i)
            v.drain()
            for m in range(2):
                for w in range(2):
                    v.tensor_scalar(ang[:, 2 * m + w, :], pos_f, T["inv"][:, m:m + 1], None, ALU.mult)
            v.drain()
            for w in range(2):
                v.tensor_scalar(turns_n[:, w::2, :], ang[:, w::2, :], float(1 / TWO_PI), (0.25, 0.0)[w],
                                ALU.mult, ALU.add)
            v.drain()
            v.tensor_scalar(turns_n, turns_n, ROUND, -ROUND, ALU.add, ALU.add)
            for c in (C1, C2, C3):
                v.drain()
                v.scalar_tensor_tensor(out=ang, in0=turns_n, scalar=-c, in1=ang, op0=ALU.mult, op1=ALU.add)
            v.drain()
            for w in range(2):
                v.tensor_scalar(turns_n[:, w::2, :], ang[:, w::2, :], (float(np.pi / 2), 0.0)[w], 3.1415925,
                                ALU.add, ALU.min)
            v.drain()
            v.tensor_scalar(ang, turns_n, -3.1415925, None, ALU.max).then_inc(ang_ready, 1)

        def act_rope_tables():
            nc.scalar.wait_ge(ang_ready, 1)
            nc.scalar.activation(rope, ang, ACT.Sin).then_inc(rope_ready, 1)
            nc.scalar.drain()

        def pe_inputs(l):
            pe = nc.tensor

            def body(i, units, first, slots):
                for u in range(units):
                    s, turn = slots[u]
                    pe.wait_ge(low_ready, 4 * i + (base + first // 3 + u + 1))
                    for c in range(3):
                        m = 3 * u + c
                        if first + m >= 28:
                            continue
                        if m >= 4:
                            pe.wait_ge((u_copied_v, u_copied_a)[m % 2], 6 * i + 14 * l + (first + m - 4) // 2 + 1)
                        for k in range(KC):
                            cols = slice(k * 384 + c * P, k * 384 + (c + 1) * P)
                            last = products(psum[:, m % 4, 0:SEQ], ring_hi[:, s, cols], ring_lo[:, s, cols],
                                            xT_hi[:, k, :], xT_lo[:, k, :], start=(k == 0), stop=(k == KC - 1))
                        last.then_inc(u_ready, 1)
                    pe.matmul(psum[0:1, 4, 0:1], zero[:, 0:1], zero[:, 0:1], start=True, stop=True)\
                      .then_inc(ring_free[s], 1)
                n = min(3 * units, 28 - first)
                pe.wait_ge(u_copied_v, 6 * i + 14 * l + (first + n) // 2)
                pe.wait_ge(u_copied_a, 6 * i + 14 * l + (first + n) // 2)

            base = pe_ring.units
            slots = pe_ring.take(U_CHUNKS // 3)
            with pe.Fori(0, 2) as i:
                body(i, SLOTS, 0, slots)
            body(0, 2, 24, slots[8:])

        def take_inputs(engine, copy, odd, copied, split, l):
            def body(i, n, first):
                for m in range(odd, n, 2):
                    engine.wait_ge(u_ready, 12 * i + 28 * l + first + m + 1)
                    dst = uT[:, first + m, :] if isinstance(i, int) else \
                        uT[:, bass.ds(i * 12 + m, 1), :].rearrange("p o n -> p (o n)")
                    copy(dst, psum[:, m % 4, 0:SEQ]).then_inc(copied, 1)
                    if n == 12 and m + 2 >= m // 3 * 3 + 3:
                        split(m // 3 + 2, i)
            with engine.Fori(0, 2) as i:
                body(i, 12, 0)
            body(0, 4, 24)

        def dve_conv(l):
            v = nc.vector
            v.wait_ge(rope_ready, 1)
            v.wait_ge(u_copied_a, 14 * (l + 1))
            v.drain()
            v.tensor_tensor(cv_u, uT[:, U_CC:U_CC + 2, :], uT[:, U_CX:U_CX + 2, :], ALU.mult)
            v.drain()
            tap = lambda k, c: col(l, V_CONV + 2 * k + c)
            for c in range(2):
                v.tensor_scalar(cv_y[:, c, :], cv_u[:, c, :], tap(1, c), None, ALU.mult)
            v.drain()
            for c in range(2):
                v.scalar_tensor_tensor(out=cv_y[:, c, 1:], in0=cv_u[:, c, 0:SEQ - 1], scalar=tap(0, c),
                                       in1=cv_y[:, c, 1:], op0=ALU.mult, op1=ALU.add)
            v.drain()
            for c in range(2):
                v.scalar_tensor_tensor(out=cv_y[:, c, 0:SEQ - 1], in0=cv_u[:, c, 1:], scalar=tap(2, c),
                                       in1=cv_y[:, c, 0:SEQ - 1], op0=ALU.mult, op1=ALU.add)
            v.drain()
            v.tensor_tensor(oT[:, 0:2, :], cv_y, uT[:, U_CB:U_CB + 2, :], ALU.mult)

        def pe_retention(l):
            pe = nc.tensor
            for n in range(4):
                last = pe.matmul(psum[:, n // 2, n % 2 * SEQ:(n % 2 + 1) * SEQ], T["turn_ret"], uT[:, U_RQ + n, :],
                                 start=True, stop=True)
            last.then_inc(rt_turned, 1)
            for c in range(2):
                for t in range(TILES):
                    last = pe.transpose(psum[:, 2, t * SEQ + c * P:t * SEQ + (c + 1) * P],
                                        uT[:, U_RV + c, t * P:(t + 1) * P], T["ident"])
            last.then_inc(rt_vT, 1)
            pe.wait_ge(rt_roped, l + 1)
            for h in range(MIX_HEADS):
                c, a = divmod(h, 2)
                rows = slice(a * HD, (a + 1) * HD)
                for kt in range(TILES):
                    last = pe.matmul(psum[:, 4 + h, kt * SEQ:(kt + 1) * SEQ], rt_r[rows, 2 + c, kt * P:(kt + 1) * P],
                                     rt_r[rows, c, :], start=True, stop=True)
                last.then_inc(rt_scores, 1)
            pe.wait_ge(rt_v_copied, l + 1)
            for h in range(MIX_HEADS):
                c, a = divmod(h, 2)
                pe.wait_ge(rt_decayed, MIX_HEADS * l + h + 1)
                for kt in range(TILES):
                    last = pe.matmul(psum[a * HD:(a + 1) * HD, c, 0:SEQ], rt_v[:, kt, h * HD:(h + 1) * HD],
                                     rt_s[:, h, kt, :], start=(kt == 0), stop=(kt == TILES - 1))
            last.then_inc(rt_o, 1)
            pe.wait_ge(rt_squared, l + 1)
            pe.matmul(psum[:, 2, :], T["ones_head"], rt_sq.rearrange("p c n -> p (c n)"), start=True, stop=True)\
              .then_inc(rt_summed, 1)

        def dve_retention(l):
            v = nc.vector
            cos, sin = both(rope[:, 0, :]), both(rope[:, 1, :])
            v.tensor_tensor(rt_r, uT[:, U_RQ:U_RQ + 4, :], cos.broadcast_to([P, 4, SEQ]), ALU.mult)
            v.wait_ge(rt_turned, l + 1)
            v.tensor_tensor(rt_t, psum[:, 0:2, :].rearrange("p b (c n) -> p (b c) n", c=2),
                            sin.broadcast_to([P, 4, SEQ]), ALU.mult)
            v.drain()
            v.tensor_tensor(rt_r, rt_r, rt_t, ALU.add).then_inc(rt_roped, 1)
            for h in range(MIX_HEADS):
                v.wait_ge(rt_scores, MIX_HEADS * l + h + 1)
                for kt in range(TILES):
                    at = h * 3 * P + (1 - kt) * P
                    last = v.tensor_tensor(rt_s[:, h, kt, :], psum[:, 4 + h, kt * SEQ:(kt + 1) * SEQ],
                                           T["decay"][:, at:at + SEQ], ALU.mult)
                last.then_inc(rt_decayed, 1)
            v.wait_ge(rt_dev, l + 1)
            v.reciprocal(rt_d, rt_d)
            v.drain()
            for c in range(2):
                v.scalar_tensor_tensor(out=rt_sq[:, c, :], in0=psum[:, c, 0:SEQ], scalar=col(l, V_GN + c),
                                       in1=rt_d[:, c, :], op0=ALU.mult, op1=ALU.mult)
            v.drain()
            v.tensor_tensor(oT[:, 4:6, :], rt_sq, rt_g, ALU.mult).then_inc(rt_done, 1)

        def act_retention(l):
            act = nc.scalar
            act.wait_ge(u_copied_v, 14 * (l + 1))
            act.drain()
            act.activation(rt_g, uT[:, U_RG:U_RG + 2, :], ACT.Silu)
            act.wait_ge(rt_vT, l + 1)
            act.copy(rt_v.rearrange("p t n -> p (t n)"), psum[:, 2, :]).then_inc(rt_v_copied, 1)
            act.wait_ge(rt_o, l + 1)
            act.activation(rt_sq, psum[:, 0:2, 0:SEQ], ACT.Square).then_inc(rt_squared, 1)
            act.wait_ge(rt_summed, l + 1)
            act.activation(rt_d, psum[:, 2, :].rearrange("p (c n) -> p c n", c=2), ACT.Sqrt, bias=eps["rms"],
                           scale=1.0 / HD).then_inc(rt_dev, 1)

        ML_SCALE = 96 ** -0.5
        RR = slice(64, 96)

        def pe_latent(l):
            pe = nc.tensor
            pe.wait_ge(ml_squared, l + 1)
            for k in range(3):
                pe.matmul(psum[:, 3, 0:SEQ], T["ones"][:, 0:P], ml_n[:, k, :], start=(k == 0), stop=(k == 2))
            pe.matmul(psum[:, 3, SEQ:2 * SEQ], T["ones"][:, 0:P], ml_n[:, 3, :], start=True, stop=True)\
              .then_inc(ml_summed, 1)
            pe.wait_ge(rt_done, l + 1)
            pe.wait_ge(small_loaded, 16 * (l + 1))
            pe.matmul(psum[:, 1, 0:SEQ], T["turn_mla"], uT[:, U_KR, :], start=True, stop=True)
            pe.wait_ge(ml_normed, l + 1)
            for h in range(MIX_HEADS):
                dst = slice(h % 2 * SEQ, (h % 2 + 1) * SEQ)
                for k in range(3):
                    pe.matmul(psum[:, 4 + h // 2, dst], small[:, W_QB + k * 512 + h * P:W_QB + k * 512 + (h + 1) * P],
                              ml_n[:, k, :], start=(k == 0), stop=(k == 2))
                pe.matmul(psum[0:HD, 6 + h // 2, dst], small[:, W_KB + h * HD:W_KB + (h + 1) * HD], ml_n[:, 3, :],
                          start=True, stop=True)
            for t in range(TILES):
                last = pe.matmul(psum[:, 0, t * SEQ:(t + 1) * SEQ], ml_n[:, 3, t * P:(t + 1) * P],
                                 small[:, W_VB:W_VB + SEQ], start=True, stop=True)
            last.then_inc(ml_qkv, 1)
            pe.wait_ge(ml_q_copied, l + 1)
            for h in range(MIX_HEADS):
                last = pe.matmul(psum[:, 2 + h // 2, h % 2 * SEQ:(h % 2 + 1) * SEQ], T["turn_mla"], ml_q[:, h, :],
                                 start=True, stop=True)
            last.then_inc(ml_turned, 1)
            pe.wait_ge(ml_roped, l + 1)
            for h in range(MIX_HEADS):
                for t in range(TILES):
                    last = pe.matmul(psum[:, 4 + h, t * SEQ:(t + 1) * SEQ], ml_q[0:96, h, t * P:(t + 1) * P],
                                     ml_k[0:96, h, :], start=True, stop=True)
                last.then_inc(ml_scores, 1)
            for h in range(MIX_HEADS):
                pe.wait_ge(ml_probs, MIX_HEADS * l + h + 1)
                for t in range(TILES):
                    for kt in range(TILES):
                        last = pe.transpose(psum[:, h, (2 * kt + t) * P:(2 * kt + t + 1) * P],
                                            ml_p[:, h, t, kt * P:(kt + 1) * P], T["ident"])
                last.then_inc(ml_pT_ready, 1)
            for h in range(MIX_HEADS):
                c, a = divmod(h, 2)
                pe.wait_ge(ml_pT_copied, MIX_HEADS * l + h + 1)
                for kt in range(TILES):
                    last = pe.matmul(psum[a * HD:(a + 1) * HD, 4 + c, 0:SEQ], ml_v[:, kt, h * HD:(h + 1) * HD],
                                     ml_pT[:, h, kt, :], start=(kt == 0), stop=(kt == TILES - 1))
            last.then_inc(ml_o, 1)

        def act_latent(l):
            act = nc.scalar
            act.activation(ml_n, uT[:, U_QA:U_QA + 4, :], ACT.Square).then_inc(ml_squared, 1)
            act.wait_ge(ml_summed, l + 1)
            act.activation(ml_d[:, 0, :], psum[:, 3, 0:SEQ], ACT.Sqrt, bias=eps["rms"], scale=1.0 / 384)
            act.activation(ml_d[:, 1, :], psum[:, 3, SEQ:2 * SEQ], ACT.Sqrt, bias=eps["rms"], scale=1.0 / P)\
               .then_inc(ml_dev, 1)
            act.wait_ge(ml_qkv, l + 1)
            act.copy(ml_q, psum[:, 4:6, :].rearrange("p b (h n) -> p (b h) n", h=2)).then_inc(ml_q_copied, 1)
            for h in range(MIX_HEADS):
                act.wait_ge(ml_max, MIX_HEADS * l + h + 1)
                for t in range(TILES):
                    i = 2 * h + t
                    last = act.activation(ml_p[:, h, t, :], psum[:, 4 + h, t * SEQ:(t + 1) * SEQ], ACT.Exp,
                                          bias=ml_m[:, 1, i:i + 1], scale=ML_SCALE, accum_out=ml_m[:, 2, i:i + 1])
                last.then_inc(ml_exp, 1)
            for h in range(MIX_HEADS):
                act.wait_ge(ml_pT_ready, MIX_HEADS * l + h + 1)
                act.copy(ml_pT[:, h, :, :].rearrange("p k n -> p (k n)"), psum[:, h, :]).then_inc(ml_pT_copied, 1)

        def dve_latent(l):
            v = nc.vector
            v.wait_ge(ml_dev, l + 1)
            v.reciprocal(ml_d, ml_d)
            v.drain()
            for k in range(4):
                last = v.scalar_tensor_tensor(out=ml_n[:, k, :], in0=uT[:, U_QA + k, :], scalar=col(l, V_QN + k),
                                              in1=ml_d[:, k // 3, :], op0=ALU.mult, op1=ALU.mult)
            last.then_inc(ml_normed, 1)
            cos, sin = both(rope[RR, 2, :]), both(rope[RR, 3, :])
            v.wait_ge(ml_qkv, l + 1)
            v.tensor_copy(ml_k[0:HD], psum[0:HD, 6:8, :].rearrange("p b (h n) -> p (b h) n", h=2))
            v.tensor_copy(ml_v.rearrange("p t n -> p (t n)"), psum[:, 0, :])
            v.tensor_tensor(ml_kr[RR, 0, :], uT[RR, U_KR, :], rope[RR, 2, :], ALU.mult)
            v.tensor_tensor(ml_kr[RR, 1, :], psum[RR, 1, 0:SEQ], rope[RR, 3, :], ALU.mult)
            v.drain()
            v.tensor_tensor(ml_k[RR], both(ml_kr[RR, 0, :]).broadcast_to([32, 4, SEQ]),
                            both(ml_kr[RR, 1, :]).broadcast_to([32, 4, SEQ]), ALU.add)
            v.wait_ge(ml_turned, l + 1)
            v.tensor_tensor(ml_t[RR], psum[RR, 2:4, :].rearrange("p b (h n) -> p (b h) n", h=2),
                            sin.broadcast_to([32, 4, SEQ]), ALU.mult)
            v.tensor_tensor(ml_q[RR], ml_q[RR], cos.broadcast_to([32, 4, SEQ]), ALU.mult)
            v.drain()
            v.tensor_tensor(ml_q[RR], ml_q[RR], ml_t[RR], ALU.add).then_inc(ml_roped, 1)
            for h in range(MIX_HEADS):
                v.wait_ge(ml_scores, MIX_HEADS * l + h + 1)
                v.tensor_reduce(ml_m[:, 0, 2 * h:2 * h + 2], psum[:, 4 + h, :].rearrange("p (t n) -> p t n", t=2),
                                AX_X, ALU.max)
                v.drain()
                v.tensor_scalar(ml_m[:, 1, 2 * h:2 * h + 2], ml_m[:, 0, 2 * h:2 * h + 2], -ML_SCALE, None, ALU.mult)\
                 .then_inc(ml_max, 1)
            for h in range(MIX_HEADS):
                v.wait_ge(ml_exp, MIX_HEADS * l + h + 1)
                v.reciprocal(ml_m[:, 3, 2 * h:2 * h + 2], ml_m[:, 2, 2 * h:2 * h + 2])
                v.drain()
                for t in range(TILES):
                    last = v.tensor_scalar(ml_p[:, h, t, :], ml_p[:, h, t, :], ml_m[:, 3, 2 * h + t:2 * h + t + 1],
                                           None, ALU.mult)
                last.then_inc(ml_probs, 1)
            v.wait_ge(ml_o, l + 1)
            v.tensor_copy(oT[:, 6:8, :], psum[:, 4:6, 0:SEQ]).then_inc(ml_done, 1)

        def cell(s):
            return [(d, c4, c4 // 2, c4 % 2) for d, c4 in ((0, s), (1, 3 - s))]

        def index(a, dp, t):
            return 8 * a + 2 * dp + t

        def pe_rwkv(l):
            pe = nc.tensor
            pe.wait_ge(rw_act, l + 1)
            for dd in range(2):
                rows = slice(dd * HD, (dd + 1) * HD)
                for c in range(2):
                    dst = slice(c * SEQ, (c + 1) * SEQ)
                    pe.matmul(psum[:, dd, dst], small[rows, W_W2 + c * P:W_W2 + (c + 1) * P], uT[rows, U_WD, :],
                              start=True, stop=True)
                    pe.matmul(psum[:, 2 + dd, dst], small[rows, W_A2 + c * P:W_A2 + (c + 1) * P], uT[rows, U_AD, :],
                              start=True, stop=True)
            pe.wait_ge(ml_done, l + 1)
            for c in range(2):
                last = pe.matmul(psum[:, 4, c * SEQ:(c + 1) * SEQ], small[:, W_G2 + c * P:W_G2 + (c + 1) * P],
                                 uT[:, U_GD, :], start=True, stop=True)
            last.then_inc(rw_pre, 1)
            pe.wait_ge(rw_ksq, l + 1)
            pe.matmul(psum[:, 5, :], T["ones_head"], pr_t[:, 0:2, :].rearrange("p c n -> p (c n)"),
                      start=True, stop=True).then_inc(rw_knorm, 1)
            for c in range(2):
                for t in range(TILES):
                    last = pe.transpose(psum[:, 6, t * SEQ + c * P:t * SEQ + (c + 1) * P],
                                        uT[:, U_V + c, t * P:(t + 1) * P], T["ident"])
            pe.wait_ge(rw_prep, l + 1)
            for g in range(4):
                a, dd = divmod(g, 2)
                rows = slice(a * HD, (a + 1) * HD)
                for j in range(4):
                    dp, t = 2 * dd + j // 2, j % 2
                    last = pe.matmul(psum[:, g, j * P:(j + 1) * P], rw_AR[rows, dp, t, 0, :],
                                     rw_B[rows, dp, t * P:(t + 1) * P], start=True, stop=True)
                last.then_inc(rw_N, 1)
            pe.wait_ge(rw_T0, 4 * l + 4)
            for i in range(16):
                a, dp, t = i // 8, i % 8 // 2, i % 2
                rows = slice(a * HD, (a + 1) * HD)
                if i >= 4:
                    pe.wait_ge(rw_masked, 16 * l + i - 3)
                for n, src in enumerate((rw_B, rw_K)):
                    last = pe.matmul(psum[:, i % 4, n * SEQ:(n + 1) * SEQ], src[rows, dp, t * P:(t + 1) * P],
                                     rw_AR[rows, dp, t, :, :].rearrange("p w n -> p (w n)"), start=True, stop=True)
                last.then_inc(rw_mats, 1)
            for lv in range(1, 6):
                for g in range(4):
                    if g == 0 and lv == 1:
                        pe.wait_ge(rw_T0s, l + 1)
                    if lv > 1:
                        pe.wait_ge(rw_Tn, 20 * l + 4 * (lv - 2) + g + 1)
                    for j in range(4):
                        i = 4 * g + j
                        last = pe.matmul(psum[:, g, j * P:(j + 1) * P], rw_mb[:, i, 0:P], rw_T[:, i, :],
                                         start=True, stop=True)
                    last.then_inc(rw_Yr, 1)
                for g in range(4):
                    pe.wait_ge(rw_Yc, 20 * l + 4 * (lv - 1) + g + 1)
                    for j in range(4 if lv < 5 else 0):
                        i = 4 * g + j
                        last = pe.matmul(psum[:, 4 + g, j * P:(j + 1) * P], rw_TT[:, i, :], rw_Y[:, i, :],
                                         start=True, stop=True)
                    for j in range(4):
                        i = 4 * g + j
                        last = pe.matmul(psum[:, g, j * P:(j + 1) * P], rw_Y[:, i, :], rw_TT[:, i, :],
                                         start=True, stop=True)
                    last.then_inc(rw_ZT, 1)
            pe.wait_ge(rw_Tn, 20 * (l + 1))
            for dp in range(4):
                for t in range(TILES):
                    for w, src in enumerate((rw_B, rw_K)):
                        n = 4 * dp + 2 * t + w
                        last = pe.transpose(psum[:, 4 + n // 4, n % 4 * P:(n % 4 + 1) * P],
                                            src[:, dp, t * P:(t + 1) * P], T["ident"])
            last.then_inc(rw_BKr, 1)
            for s in range(4):
                if s == 0:
                    pe.wait_ge(rw_BKc, l + 1)
                else:
                    pe.wait_ge(rw_Sn, 4 * l + s)
                for dd, c4, t, o in cell(s):
                    tok = slice(o * HD, (o + 1) * HD)
                    for c in range(2):
                        dp = 2 * dd + c
                        for a in range(2):
                            i, hv = index(a, dp, t), slice(a * HD, (a + 1) * HD)
                            dst = psum[tok, 0, dp * P + a * HD:dp * P + (a + 1) * HD]
                            pe.matmul(dst, rw_AR[:, dp, t, 0, tok], rw_S[:, dp, hv], start=True, stop=False)
                            last = pe.matmul(dst, rw_mb[:, i, 2 * P + o * HD:2 * P + (o + 1) * HD],
                                             rw_v[:, t, c * P + a * HD:c * P + (a + 1) * HD], start=False, stop=True)
                last.then_inc(rw_Gr, 1)
                pe.wait_ge(rw_Gc_v, 4 * l + s + 1)
                pe.wait_ge(rw_Gc_a, 4 * l + s + 1)
                for dd, c4, t, o in cell(s):
                    tok = slice(o * HD, (o + 1) * HD)
                    for c in range(2):
                        dp = 2 * dd + c
                        for a in range(2):
                            i, hv = index(a, dp, t), slice(a * HD, (a + 1) * HD)
                            last = pe.matmul(psum[tok, 1, dp * P + a * HD:dp * P + (a + 1) * HD],
                                             rw_TT[:, i, tok], rw_G[:, dp, hv], start=True, stop=True)
                last.then_inc(rw_Ur, 1)
                pe.wait_ge(rw_Uc_v, 4 * l + s + 1)
                pe.wait_ge(rw_Uc_a, 4 * l + s + 1)
                if s < 3:
                    for dd, c4, t, o in cell(s):
                        tok = slice(o * HD, (o + 1) * HD)
                        for c in range(2):
                            dp = 2 * dd + c
                            for a in range(2):
                                hv = slice(a * HD, (a + 1) * HD)
                                dst = psum[hv, 3 + dd, c * HD:(c + 1) * HD]
                                pe.matmul(dst, rw_BK[tok, dp, t, 0, hv], rw_U[tok, dp, hv], start=True, stop=False)
                                last = pe.matmul(dst, rw_BK[tok, dp, t, 1, hv],
                                                 rw_v[tok, t, c * P + a * HD:c * P + (a + 1) * HD],
                                                 start=False, stop=True)
                    last.then_inc(rw_Sr, 1)
                for dd, c4, t, o in cell(s):
                    tok = slice(o * HD, (o + 1) * HD)
                    for c in range(2):
                        dp = 2 * dd + c
                        for a in range(2):
                            i, hv = index(a, dp, t), slice(a * HD, (a + 1) * HD)
                            dst = psum[hv, 2, dp * HD:(dp + 1) * HD]
                            pe.matmul(dst, rw_S[:, dp, hv], rw_AR[:, dp, t, 1, tok], start=True, stop=False)
                            pe.matmul(dst, rw_U[:, dp, hv], rw_mb[:, i, P + o * HD:P + (o + 1) * HD],
                                      start=False, stop=False)
                            last = pe.matmul(dst, rw_v[:, t, c * P + a * HD:c * P + (a + 1) * HD],
                                             rw_mb[:, i, 3 * P + o * HD:3 * P + (o + 1) * HD], start=False, stop=True)
                last.then_inc(rw_yr, 1)
            pe.wait_ge(rw_sum, l + 1)
            pe.matmul(psum[:, 5, :], T["ones_head"], rw_y.rearrange("p c n -> p (c n)"), start=True, stop=True)
            pe.matmul(psum[:, 6, :], T["ones_head"], rw_ks.rearrange("p c n -> p (c n)"), start=True, stop=True)\
              .then_inc(rw_css, 1)
            pe.wait_ge(rw_csq, l + 1)
            pe.matmul(psum[:, 7, :], T["ones_head"], pr_t2.rearrange("p c n -> p (c n)"), start=True, stop=True)\
              .then_inc(rw_css, 1)

        pr_t2 = rw_G.rearrange("p d n -> p (d n)").rearrange("p (c n) -> p c n", c=2)

        def act_rwkv(l):
            act = nc.scalar
            act.activation(uT[:, U_WD, :], uT[:, U_WD, :], ACT.Tanh)
            act.activation(uT[:, U_GD, :], uT[:, U_GD, :], ACT.Sigmoid).then_inc(rw_act, 1)
            act.wait_ge(rw_pre, l + 1)
            act.wait_ge(ml_done, l + 1)
            for dd in range(2):
                for c in range(2):
                    dp, src = 2 * dd + c, slice(c * SEQ, (c + 1) * SEQ)
                    act.activation(pr_lw[:, dp, :], psum[:, dd, src], ACT.Sigmoid, bias=col(l, V_W0 + dp))
                    last = act.activation(pr_a[:, dp, :], psum[:, 2 + dd, src], ACT.Sigmoid, bias=col(l, V_A0 + dp))
            last.then_inc(rw_sig, 1)
            act.copy(rw_g.rearrange("p c n -> p (c n)"), psum[:, 4, :])
            act.wait_ge(rw_kraw, l + 1)
            act.activation(pr_t[:, 0:2, :], rw_kk, ACT.Square).then_inc(rw_ksq, 1)
            act.wait_ge(rw_knorm, l + 1)
            act.activation(pr_t[:, 2:4, :], psum[:, 5, :].rearrange("p (c n) -> p c n", c=2), ACT.Sqrt)\
               .then_inc(rw_kdev, 1)
            act.wait_ge(rw_L, l + 1)
            act.activation(pr_E1, pr_L, ACT.Exp)
            act.activation(pr_E2, pr_L, ACT.Exp, scale=-1.0)
            act.activation(pr_E3, pr_lw, ACT.Exp).then_inc(rw_exps, 1)
            for lv in range(1, 6):
                for g in range(4):
                    act.wait_ge(rw_Yr, 20 * l + 4 * (lv - 1) + g + 1)
                    if lv > 1:
                        act.wait_ge(rw_ZT, 20 * l + 4 * (lv - 2) + g + 1)
                    act.copy(rw_Y[:, 4 * g:4 * g + 4, :].rearrange("p i n -> p (i n)"), psum[:, g, :])\
                       .then_inc(rw_Yc, 1)
            act.wait_ge(rw_BKr, l + 1)
            act.copy(rw_BK.rearrange("p d t w n -> p (d t w n)"), psum[:, 4:8, :].rearrange("p b n -> p (b n)"))\
               .then_inc(rw_BKc, 1)
            for s in range(4):
                dd, c4, t, o = cell(s)[1]
                tok = slice(o * HD, (o + 1) * HD)
                act.wait_ge(rw_Gr, 4 * l + s + 1)
                act.copy(rw_G[tok, 2:4, :].rearrange("p d n -> p (d n)"), psum[tok, 0, 2 * P:4 * P]).then_inc(rw_Gc_a, 1)
                act.wait_ge(rw_Ur, 4 * l + s + 1)
                act.copy(rw_U[tok, 2:4, :].rearrange("p d n -> p (d n)"), psum[tok, 1, 2 * P:4 * P]).then_inc(rw_Uc_a, 1)
            act.wait_ge(rw_cent, l + 1)
            act.activation(pr_t2, rw_y, ACT.Square).then_inc(rw_csq, 1)
            act.wait_ge(rw_css, 2 * l + 2)
            act.activation(rw_kk, psum[:, 7, :].rearrange("p (c n) -> p c n", c=2), ACT.Sqrt, bias=eps["gn"],
                           scale=1.0 / HD).then_inc(rw_cdev, 1)

        def dve_rwkv(l):
            v = nc.vector
            HALF = float(np.exp(-0.5))
            for c in range(2):
                last = v.tensor_scalar(rw_kk[:, c, :], uT[:, U_K + c, :], col(l, V_KK + c), None, ALU.mult)
            last.then_inc(rw_kraw, 1)
            v.tensor_scalar(rw_om, col(l, V_KA, 2), -1.0, 1.0, ALU.mult, ALU.add)
            v.wait_ge(rw_sig, l + 1)
            v.tensor_scalar(pr_lw, pr_lw, -HALF, None, ALU.mult)
            v.drain()
            for dp in range(4):
                if dp < 2:
                    v.tensor_tensor_scan(pr_L[:, dp, :], T["keep"][:, 0:SEQ], pr_lw[:, dp, :], 0.0, ALU.mult, ALU.add)
                else:
                    v.tensor_tensor_scan(pr_L[:, dp, ::-1], T["keep"][:, SEQ:2 * SEQ][:, ::-1], pr_lw[:, dp, ::-1],
                                         0.0, ALU.mult, ALU.add)
            v.drain()
            v.tensor_tensor(pr_lw, pr_L, pr_lw, ALU.subtract).then_inc(rw_L, 1)
            v.wait_ge(rw_kdev, l + 1)
            v.tensor_scalar(pr_t[:, 2:4, :], pr_t[:, 2:4, :], 1e-12, None, ALU.max)
            for dp in range(4):
                c = dp % 2
                v.tensor_scalar(pr_kd[:, dp, :], pr_a[:, dp, :], col(l, V_KA + c), rw_om[:, c:c + 1],
                                ALU.mult, ALU.add)
            v.drain()
            v.reciprocal(pr_t[:, 2:4, :], pr_t[:, 2:4, :])
            for dd in range(2):
                kd = pr_kd[:, 2 * dd:2 * dd + 2, :]
                v.tensor_tensor(kd, kd, uT[:, U_K:U_K + 2, :], ALU.mult)
            v.drain()
            v.tensor_tensor(rw_kk, rw_kk, pr_t[:, 2:4, :], ALU.mult)
            v.tensor_tensor(rw_ks, pr_kd[:, 0:2, :], pr_kd[:, 2:4, :], ALU.add)
            v.drain()
            for dd in range(2):
                a = pr_a[:, 2 * dd:2 * dd + 2, :]
                v.tensor_tensor(a, a, rw_kk, ALU.mult)
            v.wait_ge(rw_exps, l + 1)
            v.drain()
            v.tensor_tensor(rw_B, pr_a, pr_E2, ALU.mult)
            v.tensor_tensor(rw_K, pr_kd, pr_E2, ALU.mult)
            for dp in range(4):
                c = dp % 2
                v.scalar_tensor_tensor(out=rw_AR[:, dp, :, 0, :], in0=rw_kk[:, c, :].rearrange("p (t n) -> p t n", t=2),
                                       scalar=-1.0, in1=pr_E3[:, dp, :].rearrange("p (t n) -> p t n", t=2),
                                       op0=ALU.mult, op1=ALU.mult)
                v.tensor_tensor(rw_AR[:, dp, :, 1, :], uT[:, U_R + c, :].rearrange("p (t n) -> p t n", t=2),
                                pr_E1[:, dp, :].rearrange("p (t n) -> p t n", t=2), ALU.mult)
                end = CH - 1 if dp < 2 else 0
                v.tensor_copy(rw_PC[:, dp, :], pr_E1[:, dp, end::CH])
            v.memset(rw_S, 0.0)
            v.memset(rw_Sc, 0.0)
            ident = T["ident"].unsqueeze(1).broadcast_to([P, 16, P])
            v.tensor_copy(rw_T, ident)
            v.tensor_copy(rw_TT, ident)
            v.drain()
            v.sem_inc(rw_prep, 1)
            lower = lambda lv, low: T["levels"][:, ((0 if low else 6) + lv) * P:((0 if low else 6) + lv + 1) * P]\
                .bitcast(U32).unsqueeze(1).broadcast_to([P, 4, P])
            for g in range(4):
                v.wait_ge(rw_N, 4 * l + g + 1)
                v.copy_predicated(rw_T[:, 4 * g:4 * g + 4, :], lower(0, g % 2 == 0),
                                  psum[:, g, :].rearrange("p (i n) -> p i n", i=4)).then_inc(rw_T0, 1)
            v.tensor_copy(rw_v.rearrange("p t n -> p (t n)"), psum[:, 6, :])
            for i in range(16):
                dd = i % 8 // 4
                v.wait_ge(rw_mats, 16 * l + i + 1)
                v.tensor_tensor(rw_mb[:, i, :].rearrange("p (w n) -> p w n", w=2),
                                psum[:, i % 4, :].rearrange("p (w n) -> p w n", w=2),
                                T["tri"][:, dd * SEQ:(dd + 1) * SEQ].unsqueeze(1).broadcast_to([P, 2, SEQ]), ALU.mult)\
                 .then_inc(rw_masked, 1)
            v.drain()
            for g in range(4):
                v.copy_predicated(rw_TT[:, 4 * g:4 * g + 4, :], lower(0, g % 2 == 1), rw_mb[:, 4 * g:4 * g + 4, 0:P])
            v.drain()
            v.sem_inc(rw_T0s, 1)
            for lv in range(1, 6):
                for g in range(4):
                    v.wait_ge(rw_ZT, 20 * l + 4 * (lv - 1) + g + 1)
                    if lv < 5:
                        v.copy_predicated(rw_T[:, 4 * g:4 * g + 4, :], lower(lv, g % 2 == 0),
                                          psum[:, 4 + g, :].rearrange("p (i n) -> p i n", i=4))
                    v.copy_predicated(rw_TT[:, 4 * g:4 * g + 4, :], lower(lv, g % 2 == 1),
                                      psum[:, g, :].rearrange("p (i n) -> p i n", i=4)).then_inc(rw_Tn, 1)
            for s in range(4):
                dd, c4, t, o = cell(s)[0]
                tok = slice(o * HD, (o + 1) * HD)
                v.wait_ge(rw_Gr, 4 * l + s + 1)
                v.tensor_copy(rw_G[tok, 0:2, :].rearrange("p d n -> p (d n)"), psum[tok, 0, 0:2 * P]).then_inc(rw_Gc_v, 1)
                v.wait_ge(rw_Ur, 4 * l + s + 1)
                v.tensor_copy(rw_U[tok, 0:2, :].rearrange("p d n -> p (d n)"), psum[tok, 1, 0:2 * P]).then_inc(rw_Uc_v, 1)
                if s < 3:
                    v.wait_ge(rw_Sr, 3 * l + s + 1)
                    for dd, c4, t, o in cell(s):
                        sc = rw_Sc[:, 2 * dd:2 * dd + 2, :]
                        v.tensor_tensor(sc, sc, psum[:, 3 + dd, 0:2 * HD].rearrange("p (c n) -> p c n", c=2), ALU.add)
                    v.drain()
                    for dd, c4, t, o in cell(s):
                        sc = rw_Sc[:, 2 * dd:2 * dd + 2, :]
                        v.tensor_tensor(sc, sc, rw_PC[:, 2 * dd:2 * dd + 2, c4:c4 + 1].broadcast_to([P, 2, HD]), ALU.mult)
                    v.drain()
                v.wait_ge(rw_yr, 4 * l + s + 1)
                if s < 3:
                    for a in range(2):
                        hv = slice(a * HD, (a + 1) * HD)
                        v.tensor_copy(rw_S[hv, :, hv], rw_Sc[hv, :, :])
                for dd, c4, t, o in cell(s):
                    dst = rw_y[:, :, c4 * CH:(c4 + 1) * CH]
                    src = psum[:, 2, 2 * dd * HD:(2 * dd + 2) * HD].rearrange("p (c n) -> p c n", c=2)
                    if s < 2:
                        last = v.tensor_copy(dst, src)
                    else:
                        last = v.tensor_tensor(dst, dst, src, ALU.add)
                last.then_inc(rw_Sn, 1)
            for c in range(2):
                v.scalar_tensor_tensor(out=rw_ks[:, c, :], in0=rw_ks[:, c, :], scalar=col(l, V_RK + c),
                                       in1=uT[:, U_R + c, :], op0=ALU.mult, op1=ALU.mult)
            v.drain()
            v.sem_inc(rw_sum, 1)
            v.wait_ge(rw_css, 2 * l + 1)
            flat = lambda b: b.rearrange("p c n -> p (c n)")
            v.scalar_tensor_tensor(out=flat(rw_y), in0=psum[:, 5, :], scalar=-1.0 / HD, in1=flat(rw_y),
                                   op0=ALU.mult, op1=ALU.add).then_inc(rw_cent, 1)
            v.tensor_tensor(rw_ks, psum[:, 6, :].rearrange("p (c n) -> p c n", c=2), uT[:, U_V:U_V + 2, :], ALU.mult)
            v.wait_ge(rw_cdev, l + 1)
            v.reciprocal(rw_kk, rw_kk)
            v.drain()
            for c in range(2):
                v.scalar_tensor_tensor(out=rw_y[:, c, :], in0=rw_y[:, c, :], scalar=col(l, V_LG + c),
                                       in1=rw_kk[:, c, :], op0=ALU.mult, op1=ALU.mult)
            v.drain()
            for c in range(2):
                v.scalar_tensor_tensor(out=rw_y[:, c, :], in0=rw_y[:, c, :], scalar=col(l, V_LB + c),
                                       in1=rw_ks[:, c, :], op0=ALU.add, op1=ALU.add)
            v.drain()
            v.tensor_tensor(oT[:, 2:4, :], rw_y, rw_g, ALU.mult).then_inc(rw_done, 1)

        def sync_second_block(sp):
            for l in range(DEPTH):
                load_units(sp, d["ff_w"][2 * l], FF_CHUNKS, UNIT)
                load_units(sp, d["mix_w"][l], U_CHUNKS // 3, UNIT)
                load_units(sp, d["proj_w"][2 + l], 4, 2 * D)
                load_units(sp, d["ff_w"][2 * l + 1], FF_CHUNKS, UNIT)
            sp.wait_ge(final_ready, 1)
            sp.dma_start(out[0].rearrange("(t p) n -> p t n", p=P), hn).then_inc(stored, 16)
            sp.wait_ge(stored, 16)

        def pool_second_block():
            pool = nc.gpsimd
            pool.wait_ge(rowv_used, 4)
            pool.dma_start(pos_i, d["positions"].partition_broadcast(P)).then_inc(pos_loaded, 16)
            for l in range(DEPTH):
                if l:
                    pool.wait_ge(rw_done, l)
                pool.dma_start(small[:], d["small_w"][l]).then_inc(small_loaded, 16)
            pool.wait_ge(rw_done, DEPTH)
            pool.dma_start(rowv[:, 0:1, :], d["row_vectors"][8:9].partition_broadcast(P)).then_inc(rowv_full, 16)

        def pe_second_block():
            for l in range(DEPTH):
                pe_glu(FF_CHUNKS)
                pe_turn(hn)
                nc.tensor.wait_ge(turned_used, pe_u.turned)
                pe_inputs(l)
                pe_retention(l)
                pe_latent(l)
                pe_rwkv(l)
                pe_project_whole(rw_done, l + 1)
                pe_turn(hn)
                nc.tensor.wait_ge(turned_used, pe_u.turned)
                pe_glu(FF_CHUNKS)
                if l < DEPTH - 1:
                    pe_turn(hn)
                    nc.tensor.wait_ge(turned_used, pe_u.turned)

        def dve_second_block():
            dve_rope_tables()
            for l in range(DEPTH):
                dve_glu(FF_CHUNKS, False)
                dve_norm(0.5, rms=True, gain=col(l, V_MIX, KC))
                take_inputs(nc.vector, nc.vector.tensor_copy, 0, u_copied_v, dve_split, l)
                dve_ring.take(U_CHUNKS // 3)
                dve_conv(l)
                dve_retention(l)
                dve_latent(l)
                dve_rwkv(l)
                dve_ring.take(4, parts=False)
                dve_ahead()
                dve_norm(1.0, rms=True, gain=col(l, V_F2, KC))
                dve_glu(FF_CHUNKS, False, l < DEPTH - 1)
                if l < DEPTH - 1:
                    dve_norm(0.5, rms=True, gain=col(l + 1, V_F1, KC))
            dve_norm(0.5, rms=True, turn=False)
            nc.vector.wait_ge(rowv_full, 16 * 5)
            for t in range(TILES):
                last = nc.vector.tensor_tensor(hn[:, t, :], hn[:, t, :], rowv[:, 0, :], ALU.mult)
            last.then_inc(final_ready, 1)

        def act_second_block():
            act_rope_tables()
            for l in range(DEPTH):
                act_glu(FF_CHUNKS)
                act_norm(rms=True, gain=col(l, V_MIX, KC))
                take_inputs(nc.scalar, nc.scalar.copy, 1, u_copied_a, act_split, l)
                act_ring.take(U_CHUNKS // 3)
                act_retention(l)
                act_latent(l)
                act_rwkv(l)
                act_ring.take(4, parts=False)
                nc.scalar.wait_ge(rw_done, l + 1)
                act_ahead()
                act_norm(rms=True, gain=col(l, V_F2, KC))
                act_glu(FF_CHUNKS, l < DEPTH - 1)
                if l < DEPTH - 1:
                    act_norm(rms=True, gain=col(l + 1, V_F1, KC))
            act_norm(rms=True, turn=False)


        block = ctx.enter_context(nc.Block())
        @block.sync
        def _(sp):
            sp.dma_start(x[:], d["x"].rearrange("(t p) n -> p t n", p=P)).then_inc(x_loaded, 16)
            sp.dma_start(tab[:], d["tables"]).then_inc(tables_loaded, 16)
            load_dilated(sp)
            load_units(sp, d["proj_w"][0], 4, 2 * D)
            load_units(sp, d["moe_w"][0], MOE_CHUNKS, UNIT)
            load_units(sp, d["sb_w"], PAIRS, UNIT)
            load_units(sp, d["proj_w"][1], 4, 2 * D)
            load_units(sp, d["moe_w"][1], MOE_CHUNKS, UNIT)
            sync_second_block(sp)

        @block.gpsimd
        def _(pool):
            pool.dma_start(hot[0:BUCKETS + 1, :], d["early_tables"][0:BUCKETS + 1, 0:GROUPS * 3 * P])\
                .then_inc(early_loaded, 16)
            pool.dma_start(rel_tab[0:BUCKETS, :], d["rel_table"]).then_inc(early_loaded, 16)
            pool.dma_start(pick[0:EXPERTS], d["early_tables"][0:EXPERTS, GROUPS * 3 * P:]
                           .rearrange("p (e n) -> p e n", e=EXPERTS)).then_inc(early_loaded, 16)
            pool.dma_start(router_w[:], d["router_w"]).then_inc(router_loaded, 16)
            pool.dma_start(router_b, d["router_b"].partition_broadcast(P)).then_inc(router_loaded, 16)
            pool.dma_start(vec[:], d["vectors"].rearrange("l p n -> p l n")).then_inc(vec_loaded, 16)
            pool.wait_ge(rel_copied, 1)
            pool.dma_start(rel_dram, rel_rows[0:HEADS, :]).then_inc(rel_stored, 16)
            pool_rows(0)
            pool_bias()
            pool_rows(1)
            pool.wait_ge(sb_v_ready, PAIRS)
            pool_rows(2)
            pool_rows(3)
            pool_second_block()

        @block.tensor
        def _(pe):
            pe.wait_ge(x_loaded, 16)
            pe.wait_ge(tables_loaded, 16)
            pe_turn(x, counted=False)
            pe.wait_ge(early_loaded, 48)
            pe.wait_ge(zero_ready, 1)
            for g in range(GROUPS):
                last = pe.matmul(psum[0:HEADS, 4 + g, 0:3 * P], rel_tab[0:BUCKETS + 1, :],
                                 hot[0:BUCKETS + 1, g * 3 * P:(g + 1) * 3 * P], start=True, stop=True)
            last.then_inc(rel_ready, 1)
            pe.wait_ge(rel_copied, 1)
            pe_dilated()
            pe_project(o_copied, PAIRS)
            pe_turn(x)
            pe_router(0)
            pe_glu(MOE_CHUNKS)
            pe_turn(x, flip=True)
            pe_sticks()
            pe_project(sb_o_copied, PAIRS)
            pe_turn(x)
            pe_router(1)
            pe_glu(MOE_CHUNKS)
            pe_turn(hn)
            nc.tensor.wait_ge(turned_used, pe_u.turned)
            pe_second_block()

        @block.vector
        def _(v):
            v.memset(zero[:], 0.0)
            v.memset(rel_tab[BUCKETS:BUCKETS + 1, :], NEG).then_inc(zero_ready, 1)
            dve_norm(None)
            v.wait_ge(rel_ready, 1)
            v.tensor_copy(rel_rows[0:HEADS, :].rearrange("p (g n) -> p g n", g=GROUPS),
                          psum[0:HEADS, 4:7, 0:3 * P]).then_inc(rel_copied, 1)
            dve_dilated()
            dve_ahead()
            dve_norm("norm", ln=True)
            dve_router(0)
            dve_glu(MOE_CHUNKS, True)
            dve_norm("norm", ln=True, flip=True)
            dve_sticks()
            dve_ahead()
            dve_norm("norm", ln=True)
            dve_router(1)
            dve_glu(MOE_CHUNKS, True)
            dve_norm("norm", ln=True, rms=True, gain=vec[:, 0, V_F1:V_F1 + KC])
            dve_second_block()

        @block.scalar
        def _(act):
            act.wait_ge(tables_loaded, 16)
            act_norm()
            act_dilated()
            act_ahead()
            act_norm(ln=True)
            act_router(0)
            act_glu(MOE_CHUNKS)
            act_norm(ln=True, flip=True)
            act_sticks()
            act_ahead()
            act_norm(ln=True)
            act_router(1)
            act_glu(MOE_CHUNKS)
            act_norm(ln=True, rms=True, gain=vec[:, 0, V_F1:V_F1 + KC])
            act_second_block()


_OUT = (1, SEQ, D)


def kernel(**inputs):
    import concourse.bacc as bacc
    from concourse.bass_utils import run_bass_kernel_spmd as run

    arrays = layout(inputs)
    nc = bacc.Bacc("TRN2", target_bir_lowering=False, num_devices=1)
    d = {k: nc.dram_tensor(k, v.shape, mybir.dt.from_np(v.dtype), kind="ExternalInput").ap()
         for k, v in arrays.items()}
    out = nc.dram_tensor("out", _OUT, F32, kind="ExternalOutput").ap()
    build_kernel(nc, d, out)
    r = run(nc, [arrays], core_ids=[0])
    return r.results[0]["out"]
```
